# Optimizing a Trainium2 kernel written in Bass

```python
import jax
import jax.numpy as jnp
from jax import lax
import numpy as np

D_MODEL = 1024
BATCH = 1
SEQ = 512
DEPTH = 1

PLE_DIM = 256
SGU_WIDTH = D_MODEL
SGU_CHUNK = 128
SGU_GROUPS = 8
SGU_GROUP_WIDTH = SGU_WIDTH // SGU_GROUPS
V_DIM = 128
MLA_HEADS = D_MODEL // V_DIM
QK_NOPE = 128
QK_ROPE = 64
QK_DIM = QK_NOPE + QK_ROPE
Q_LORA = 384
KV_LORA = 256
ROPE_THETA = 10000.0
Q_BLOCK = 128
N_EXPERTS = 64
N_GROUPS = 8
EXPERTS_PER_GROUP = N_EXPERTS // N_GROUPS
TOPK_GROUPS = 4
TOP_K = 8
EXPERT_FF = 256
SHARED_FF = 256
ROUTED_SCALE = 2.5

NORM_EPS = 1e-6
LN_EPS = 1e-5
NEG_INF = -1e30

kernel_name = 'hybrid_sgu_mla_moe_block'

def _in_sizes():
    return [SGU_WIDTH, SGU_WIDTH, Q_LORA, KV_LORA, QK_ROPE, SGU_WIDTH, MLA_HEADS * V_DIM]

def _in_offsets():
    offs, acc = [], 0
    for s in _in_sizes()[:-1]:
        acc += s
        offs.append(acc)
    return offs

def rms_norm(x, g):
    xf = x.astype(jnp.float32)
    y = xf * lax.rsqrt(jnp.mean(xf * xf, axis=-1, keepdims=True) + NORM_EPS)
    return (y * g.astype(jnp.float32)).astype(x.dtype)

def layer_norm(x, g, b):
    xf = x.astype(jnp.float32)
    mu = jnp.mean(xf, axis=-1, keepdims=True)
    xc = xf - mu
    var = jnp.mean(xc * xc, axis=-1, keepdims=True)
    y = xc * lax.rsqrt(var + LN_EPS) * g.astype(jnp.float32) + b.astype(jnp.float32)
    return y.astype(x.dtype)

def rope_tables(positions, dtype):
    half = QK_ROPE // 2
    inv_freq = 1.0 / (ROPE_THETA ** (jnp.arange(half, dtype=jnp.float32) * (2.0 / QK_ROPE)))
    ang = positions.astype(jnp.float32)[..., None] * inv_freq
    return jnp.cos(ang)[:, :, None, :].astype(dtype), jnp.sin(ang)[:, :, None, :].astype(dtype)

def apply_rope(x, cos, sin):
    half = x.shape[-1] // 2
    x1, x2 = x[..., :half], x[..., half:]
    return jnp.concatenate([x1 * cos - x2 * sin, x2 * cos + x1 * sin], axis=-1)

def spatial_gating(u, v, ln_g, ln_b, w_sp, b_sp):
    B, S, _ = u.shape
    v = layer_norm(v, ln_g, ln_b)
    causal = jnp.tril(jnp.ones((SGU_CHUNK, SGU_CHUNK), dtype=bool))
    w = jnp.where(causal[None], w_sp, 0.0).astype(v.dtype)
    vc = v.reshape(B, S // SGU_CHUNK, SGU_CHUNK, SGU_GROUPS, SGU_GROUP_WIDTH)
    mixed = jnp.einsum('gij,bnjgc->bnigc', w, vc) + b_sp.T[:, :, None].astype(v.dtype)
    return u * mixed.reshape(B, S, SGU_WIDTH)

def mla_attention(q_lat, kv_lat, k_rope, cos, sin, g_qa, w_qb, g_kva, w_kvb,
                  g_q_nope, g_k_nope, g_q_rope, g_k_rope):
    B, S, _ = q_lat.shape
    H = MLA_HEADS
    q = (rms_norm(q_lat, g_qa) @ w_qb).reshape(B, S, H, QK_DIM)
    kv = (rms_norm(kv_lat, g_kva) @ w_kvb).reshape(B, S, H, QK_NOPE + V_DIM)
    q_nope = rms_norm(q[..., :QK_NOPE], g_q_nope)
    q_pe = apply_rope(rms_norm(q[..., QK_NOPE:], g_q_rope), cos, sin)
    k_nope = rms_norm(kv[..., :QK_NOPE], g_k_nope)
    v = kv[..., QK_NOPE:]
    k_pe = apply_rope(rms_norm(k_rope, g_k_rope)[:, :, None, :], cos, sin)
    k = jnp.concatenate([k_nope, jnp.broadcast_to(k_pe, (B, S, H, QK_ROPE))], axis=-1)
    qh = jnp.concatenate([q_nope, q_pe], axis=-1) * (QK_DIM ** -0.5)
    n_blk = S // Q_BLOCK
    q_blocks = qh.reshape(B, n_blk, Q_BLOCK, H, QK_DIM).transpose(1, 0, 3, 2, 4)
    kh = k.transpose(0, 2, 1, 3)
    vh = v.transpose(0, 2, 1, 3)
    kpos = jnp.arange(S)

    def block(args):
        q_i, i = args
        s = jnp.einsum('bhqd,bhkd->bhqk', q_i, kh).astype(jnp.float32)
        qpos = i * Q_BLOCK + jnp.arange(Q_BLOCK)
        s = jnp.where(kpos[None, :] <= qpos[:, None], s, NEG_INF)
        prob = jax.nn.softmax(s, axis=-1).astype(vh.dtype)
        return jnp.einsum('bhqk,bhkd->bhqd', prob, vh)

    o = lax.map(block, (q_blocks, jnp.arange(n_blk)))
    return o.transpose(1, 0, 3, 2, 4).reshape(B, S, H * V_DIM)

def moe(h, w_router, b_router, w_gate, w_up, w_down, w_sh_gate, w_sh_up, w_sh_down):
    B, S, D = h.shape
    t = h.reshape(B * S, D)
    scores = jax.nn.sigmoid((t @ w_router).astype(jnp.float32))
    sel = scores + b_router.astype(jnp.float32)
    grp = sel.reshape(-1, N_GROUPS, EXPERTS_PER_GROUP)
    group_score = lax.top_k(grp, 2)[0].sum(-1)
    _, gidx = lax.top_k(group_score, TOPK_GROUPS)
    gmask = jax.nn.one_hot(gidx, N_GROUPS, dtype=jnp.float32).sum(1) > 0
    emask = jnp.repeat(gmask, EXPERTS_PER_GROUP, axis=1)
    _, eidx = lax.top_k(jnp.where(emask, sel, -jnp.inf), TOP_K)
    w = jnp.take_along_axis(scores, eidx, axis=1)
    w = w / jnp.sum(w, axis=-1, keepdims=True) * ROUTED_SCALE
    combine = (jax.nn.one_hot(eidx, N_EXPERTS, dtype=jnp.float32) * w[..., None]).sum(1).astype(t.dtype)
    y = (jax.nn.silu(t @ w_sh_gate) * (t @ w_sh_up)) @ w_sh_down
    for g in range(N_GROUPS):
        sl = slice(g * EXPERTS_PER_GROUP, (g + 1) * EXPERTS_PER_GROUP)
        a = jax.nn.silu(jnp.einsum('td,edf->tef', t, w_gate[sl])) * jnp.einsum('td,edf->tef', t, w_up[sl])
        y = y + jnp.einsum('tef,efd->td', a * combine[:, sl, None], w_down[sl])
    return y.reshape(B, S, D)

def setup_inputs(seed: int = 0) -> dict:
    key = jax.random.key(seed)
    ks = iter(jax.random.split(key, 48))
    f32 = jnp.float32
    L = DEPTH

    def nrm(shape, fan_in):
        return jax.random.normal(next(ks), shape, f32) * (fan_in ** -0.5)

    def gain(shape):
        return 1.0 + 0.05 * jax.random.normal(next(ks), shape, f32)

    def small(shape, s):
        return s * jax.random.normal(next(ks), shape, f32)

    in_width = sum(_in_sizes())
    x = jax.random.normal(next(ks), (BATCH, SEQ, D_MODEL), f32)
    p = jax.random.normal(next(ks), (L, BATCH, SEQ, PLE_DIM), f32)
    offsets = jax.random.randint(next(ks), (BATCH, 1), 0, 4096, dtype=jnp.int32)
    positions = offsets + jnp.arange(SEQ, dtype=jnp.int32)[None, :]
    return {
        'x': x,
        'p': p,
        'positions': positions,
        'g_mix': gain((L, D_MODEL)),
        'w_in': nrm((L, D_MODEL, in_width), D_MODEL),
        'sgu_ln_g': gain((L, SGU_WIDTH)),
        'sgu_ln_b': small((L, SGU_WIDTH), 0.02),
        'sgu_w': nrm((L, SGU_GROUPS, SGU_CHUNK, SGU_CHUNK), SGU_CHUNK),
        'sgu_b': small((L, SGU_GROUPS, SGU_CHUNK), 0.02),
        'mla_g_qa': gain((L, Q_LORA)),
        'mla_w_qb': nrm((L, Q_LORA, MLA_HEADS * QK_DIM), Q_LORA),
        'mla_g_kva': gain((L, KV_LORA)),
        'mla_w_kvb': nrm((L, KV_LORA, MLA_HEADS * (QK_NOPE + V_DIM)), KV_LORA),
        'qk_g_q_nope': gain((L, QK_NOPE)),
        'qk_g_k_nope': gain((L, QK_NOPE)),
        'qk_g_q_rope': gain((L, QK_ROPE)),
        'qk_g_k_rope': gain((L, QK_ROPE)),
        'w_o': nrm((L, D_MODEL, D_MODEL), D_MODEL),
        'g_ffn': gain((L, D_MODEL)),
        'w_router': nrm((L, D_MODEL, N_EXPERTS), D_MODEL),
        'b_router': small((L, N_EXPERTS), 0.01),
        'w_exp_gate': nrm((L, N_EXPERTS, D_MODEL, EXPERT_FF), D_MODEL),
        'w_exp_up': nrm((L, N_EXPERTS, D_MODEL, EXPERT_FF), D_MODEL),
        'w_exp_down': nrm((L, N_EXPERTS, EXPERT_FF, D_MODEL), EXPERT_FF),
        'w_sh_gate': nrm((L, D_MODEL, SHARED_FF), D_MODEL),
        'w_sh_up': nrm((L, D_MODEL, SHARED_FF), D_MODEL),
        'w_sh_down': nrm((L, SHARED_FF, D_MODEL), SHARED_FF),
        'g_ple_in': gain((L, D_MODEL)),
        'w_ple_gate': nrm((L, D_MODEL, D_MODEL), D_MODEL),
        'w_ple_proj': nrm((L, PLE_DIM, D_MODEL), PLE_DIM),
        'g_ple_out': gain((L, D_MODEL)),
    }

def reference(x, p, positions, g_mix, w_in, sgu_ln_g, sgu_ln_b, sgu_w, sgu_b,
              mla_g_qa, mla_w_qb, mla_g_kva, mla_w_kvb,
              qk_g_q_nope, qk_g_k_nope, qk_g_q_rope, qk_g_k_rope,
              w_o, g_ffn, w_router, b_router, w_exp_gate, w_exp_up, w_exp_down,
              w_sh_gate, w_sh_up, w_sh_down, g_ple_in, w_ple_gate, w_ple_proj, g_ple_out):
    cos, sin = rope_tables(positions, x.dtype)
    offs = _in_offsets()
    for l in range(DEPTH):
        h = rms_norm(x, g_mix[l])
        z = h @ w_in[l]
        u, v, q_lat, kv_lat, k_rope, gate_a, gate_b = jnp.split(z, offs, axis=-1)
        y_a = spatial_gating(jax.nn.gelu(u), jax.nn.gelu(v), sgu_ln_g[l], sgu_ln_b[l], sgu_w[l], sgu_b[l])
        y_b = mla_attention(q_lat, kv_lat, k_rope, cos, sin, mla_g_qa[l], mla_w_qb[l],
                            mla_g_kva[l], mla_w_kvb[l], qk_g_q_nope[l], qk_g_k_nope[l],
                            qk_g_q_rope[l], qk_g_k_rope[l])
        merged = jax.nn.sigmoid(gate_a) * y_a + jax.nn.sigmoid(gate_b) * y_b
        x = x + merged @ w_o[l]
        x = x + moe(rms_norm(x, g_ffn[l]), w_router[l], b_router[l], w_exp_gate[l], w_exp_up[l],
                    w_exp_down[l], w_sh_gate[l], w_sh_up[l], w_sh_down[l])
        ple_gate = jax.nn.sigmoid(rms_norm(x, g_ple_in[l]) @ w_ple_gate[l])
        x = x + ple_gate * rms_norm(p[l] @ w_ple_proj[l], g_ple_out[l])
    return x


_drawn_inputs = setup_inputs


def setup_inputs(seed=0):
    import zlib

    import numpy as np

    out = dict(_drawn_inputs(seed))
    spreads = {}
    factors = {'qk_g_q_rope': 2.764, 'g_ple_in': 8.0, 'g_ple_out': 2.88}
    for name, (base, spread) in spreads.items():
        noise = np.random.default_rng([zlib.crc32(name.encode()), seed]).standard_normal(out[name].shape)
        drawn = base * np.exp(spread * noise) if base else spread * noise
        out[name] = jnp.asarray(drawn.astype(out[name].dtype))
    for name, factor in factors.items():
        out[name] = (out[name] * factor).astype(out[name].dtype)
    return out
```

```python
import concourse.bass as bass
from concourse import mybir
from contextlib import ExitStack
import numpy as np


def hybrid_block_kernel(nc, a, out):
    F32, BF16 = mybir.dt.float32, mybir.dt.bfloat16
    I32, U32 = mybir.dt.int32, mybir.dt.uint32
    ALU, ACT, AX = mybir.AluOpType, mybir.ActivationFunctionType, mybir.AxisListType

    P = 128
    SEQ, D = a["x"].shape[1], a["x"].shape[2]
    NT, KD = SEQ // P, D // P
    PLE = a["p"].shape[3]
    G = a["sgu_w"].shape[1]
    QL, KVL = a["mla_w_qb"].shape[1], a["mla_w_kvb"].shape[1]
    NOPE, ROPE = a["qk_g_q_nope"].shape[1], a["qk_g_q_rope"].shape[1]
    H = a["mla_w_qb"].shape[2] // (NOPE + ROPE)
    QK, VD, HR = NOPE + ROPE, P, ROPE // 2
    E = a["w_router"].shape[2]
    FF = a["w_exp_gate"].shape[3]
    NG, TOPG, TOPK = 8, 4, 8
    EG = E // NG
    SCALE, ROUTED = float(QK) ** -0.5, 2.5
    EPS, LN_EPS, THETA = 1e-6, 1e-5, 10000.0
    BIG = 1e30
    LAT = QL + KVL + ROPE
    KQ, KKV, KF = QL // P, KVL // P, FF // P
    OFF_U, OFF_V, OFF_LAT, OFF_GA, OFF_GB = 0, D, 2 * D, 2 * D + LAT, 3 * D + LAT
    NA = H * NT
    RING = 4
    WGU, WDN = KD * 2 * FF, KF * D
    WEXP = WGU + WDN
    NPASS_MAX = SEQ // P
    Q_LOOP = (E - 8) // RING

    h2_dram = nc.dram_tensor("h2_rows", (SEQ, D), F32, kind="Internal").ap()
    pn_dram = nc.dram_tensor("ple_rows", (SEQ, D), F32, kind="Internal").ap()
    y_dram = nc.dram_tensor("expert_rows", (SEQ * TOPK, D), F32, kind="Internal").ap()

    ctx = ExitStack()
    with ctx:
        def sb(name, width, dt=F32):
            return ctx.enter_context(nc.sbuf_tensor(name, [P, width], dt))

        def sem(name):
            return ctx.enter_context(nc.semaphore(name))

        def v2(t, at, x, y):
            return t[:, at:at + x * y].rearrange("p (x y) -> p x y", x=x)

        def v3(t, at, x, y, z):
            return t[:, at:at + x * y * z].rearrange("p (x y z) -> p x y z", x=x, y=y)

        xr_ = sb("resid", NT * D)
        x = v2(xr_, 0, NT, D)
        hT_ = sb("hT", KD * SEQ)
        hT = v2(hT_, 0, KD, SEQ)
        V = v3(hT_, 0, NT, H, VD)
        win = sb("win", 2 * 4096)
        ya_ = sb("ya", NT * D)
        ya = v2(ya_, 0, NT, D)
        xg = [ya_[:, i * D:(i + 1) * D] for i in range(2)]
        yo = [ya_[:, (2 + i) * D:(3 + i) * D] for i in range(2)]
        arena = sb("arena", RING * WEXP)

        base = 0
        def take(n):
            nonlocal base
            base += n
            return base - n
        o_qT = take(H * SEQ)
        o_kT = take(H * SEQ)
        o_sigb = take(NT * D)
        o_qrT = take(H // 2 * SEQ)
        o_latT = take((KQ + KKV) * SEQ)
        o_qc = take(2 * NT * 2 * QK)
        o_sq = take(NT * 2 * QK)
        o_spare = take(512)
        o_kpeT = take(SEQ)
        o_tab = take(2 * 4 * NT * HR)
        assert base <= RING * WEXP
        qT, kT = v2(arena, o_qT, H, SEQ), v2(arena, o_kT, H, SEQ)
        vbuf, siga = v2(arena, o_qT, NT, D), v2(arena, o_kT, NT, D)
        sigb = v2(arena, o_sigb, NT, D)
        hst = [arena[:, o_sigb + i * D:o_sigb + (i + 1) * D] for i in range(4)]
        qrT = v2(arena, o_qrT, H // 2, SEQ)
        wsp = v2(arena, o_qrT, G, P)
        wspT = v2(arena, o_qrT + G * P, G, P)
        latT = v2(arena, o_latT, KQ + KKV, SEQ)
        lat = v2(arena, o_qc, NT, LAT)
        qc = [v3(arena, o_qc + i * NT * 2 * QK, NT, 2, QK) for i in range(2)]
        sqc = v3(arena, o_sq, NT, 2, QK)
        probs = [arena[:, o_qc + i * SEQ:o_qc + (i + 1) * SEQ] for i in range(2)]
        probsT = [arena[:, o_qc + (2 + i) * SEQ:o_qc + (3 + i) * SEQ] for i in range(2)]
        otmp = [arena[:, o_sq + i * P:o_sq + (i + 1) * P] for i in range(2)]
        lng, lnb = arena[:, o_sq:o_sq + D], arena[:, o_sq + D:o_sq + 2 * D]
        kpeT = arena[:, o_kpeT:o_kpeT + SEQ]
        tabq = [v2(arena, o_tab + i * NT * HR, NT, HR) for i in range(4)]
        tabk = [v2(arena, o_tab + (4 + i) * NT * HR, NT, HR) for i in range(4)]
        z3 = 3 * WEXP
        gffn, gpo = arena[:, z3:z3 + D], arena[:, z3 + D:z3 + 2 * D]
        h2s = [arena[:, z3 + (2 + i) * D:z3 + (3 + i) * D] for i in range(4)]
        wgu = [arena[:, r * WEXP:r * WEXP + WGU].rearrange("p (g k f) -> p k g f", g=2, k=KD)
               for r in range(RING)]
        wdn = [v2(arena, r * WEXP + WGU, KF, D) for r in range(RING)]
        YT = TOPK * D
        yt = [arena[:, (t % 3) * YT:(t % 3 + 1) * YT] for t in range(NT)]

        work = sb("work", 3328)
        S_ = [v2(work, i * SEQ, NT, P) for i in range(2)]
        xgT = v2(work, D, KD, P)
        sg = work[:, 2 * D:2 * D + FF]
        a_ = [v2(work, 2 * D + FF * (1 + i), KF, P) for i in range(2)]
        aT = [v2(work, 2 * D + FF * (3 + i), KF, P) for i in range(2)]
        pbuf = v2(work, 0, NT, PLE)
        pT = v2(work, D, PLE // P, SEQ)
        rt = [v3(work, 2 * D + i * 256, NT, 2, HR) for i in range(2)]
        qrot = v3(work, 0, NT, 2, ROPE)
        kprot = v3(work, 512, NT, 2, ROPE)
        ang = [v2(work, D + i * P, NT, HR) for i in range(6)]
        h3 = [work[:, i * D:(i + 1) * D] for i in range(2)]
        gt = work[:, 2 * D:3 * D]

        ident, tri, ones = sb("ident", P), sb("tri", P), sb("ones", P)
        identb, negmask = sb("identb", P, BF16), sb("negmask", P, BF16)
        iota = sb("iota", SEQ)
        R = sb("R", E * NT * 3)
        Rv = R[:, :].rearrange("p (e t c) -> p e t c", e=E, t=NT)
        rank_ = sb("rank", E * NT)
        rank = v2(rank_, 0, E, NT)
        wr = sb("wr", KD * E)
        brt = sb("brt", E)
        sm = sb("small", 200)
        smi = sb("smalli", 8, I32)
        NSMALL = 4
        idx = [sb(f"idx{i}", 2, U32) for i in range(4)]
        wt = [sm[:, 180 + i:181 + i] for i in range(4)]
        rows = sb("rows", P)
        ROWS = [("positions", NT), ("g_mix", KD), ("g_ple_in", KD), ("sgu_b", G), ("mla_g_qa", KQ),
                ("mla_g_kva", KKV), ("qk_g_q_nope", 1), ("qk_g_k_nope", 1)]
        NROW = sum(n for _, n in ROWS)
        col = {}
        for name, n in ROWS:
            first = sum(len_ for _, len_ in ROWS[:len(col)])
            col[name] = sm[:, first:first + n]
        posf, gmix, gple, bsp = col["positions"], col["g_mix"], col["g_ple_in"], col["sgu_b"]
        gqa, gkva, gqn, gkn = col["mla_g_qa"], col["mla_g_kva"], col["qk_g_q_nope"], col["qk_g_k_nope"]
        gqk = sm[:, 35:36]
        assert NROW <= 35
        addc = sm[:, 36:38]
        st = [sm[:, 44 + 4 * i:48 + 4 * i] for i in range(8)]
        ssl, msl = sm[:, 76:88], sm[:, 88:100]
        bst = [sm[:, 100 + 12 * i:112 + 12 * i] for i in range(2)]
        mv = v2(sm, 124, NT, 2)
        ssq, msq = sm[:, 132:148], sm[:, 148:164]
        nm, rs, rinv = sm[:, 164:168], sm[:, 168:172], sm[:, 172:176]
        pos_i = sb("pos_i", P, I32)[0:NT, :]
        nb_i = smi[0:1, 6:7]
        gqr, gkr = sb("gqr", ROPE), sb("gkr", ROPE)
        invf = iota[:, 0:HR]
        rt_sc = v2(work, D, NT, E)
        rt_sel = v2(work, D + 256, NT, E)
        rt_rep = v2(work, D + 512, NT, E)
        rt_M = v2(work, D + 768, NT, E)
        rt_gt = work[:, 0:256].rearrange("p (t g h) -> p t g h", t=NT, g=NG)
        rt_eq = work[:, 256:512].rearrange("p (t g h) -> p t g h", t=NT, g=NG)
        g8 = v3(work, 512, NT, NG, 8)
        gs, gr, gm, t8 = (v2(work, 768 + 32 * i, NT, 8) for i in range(4))
        rden = work[:, 896:896 + NT]
        low = v2(work, 900, 8, 8)
        MT = work[0:E, 0:SEQ]
        cmp_ = work[:, 964:968]
        addt = sm[:, 176:180]

        bank = [ctx.enter_context(nc.psum_tensor(f"bank{i}", [P, 512], F32)) for i in range(8)]

        ld_x = [sem(f"x_loaded{t}") for t in range(NT)]
        ld_small, ld_pos, ld_wsp, ld_ln = sem("small_loaded"), sem("pos_loaded"), sem("wsp_loaded"), sem("ln_loaded")
        ld_late = sem("late_loaded")
        win_ready = [sem(f"win_ready{i}") for i in range(2)]
        const_pool = sem("const_pool")
        dve_step, pool_step = sem("dve_step"), sem("pool_step")
        rms_sq, rms_ms, rms_rt, rms_x = sem("rms_sq"), sem("rms_ms"), sem("rms_rt"), sem("rms_x")
        tr_done, tr_free = sem("tr_done"), [sem(f"tr_free{i}") for i in range(2)]
        pj_done, pj_free = sem("pj_done"), [sem(f"pj_free{i}") for i in range(4)]
        lat_sq, lat_ms, lat_rt, lat_n = sem("lat_sq"), sem("lat_ms"), sem("lat_rt"), sem("lat_n")
        ang_r, sincos, tables, kp_rot = sem("ang_r"), sem("sincos"), sem("tables"), sem("kp_rot")
        rows_ready, cols_done = sem("rows_ready"), sem("cols_done")
        wsp_m = sem("wsp_masked")
        ln_ms, ln_rt, ln_x, ln_v = sem("ln_ms"), sem("ln_rt"), sem("ln_x"), sem("ln_v")
        ya_g = sem("ya_gated")
        qk_ms, qk_rt, qk_n, q_rot = sem("qk_ms"), sem("qk_rt"), sem("qk_n"), sem("q_rot")
        s_done, nm_ready, exp_done = sem("s_done"), sem("nm_ready"), sem("exp_done")
        pt_done, pt_ready, pv_done = sem("pt_done"), sem("pt_ready"), sem("pv_done")
        o_ready, ya_add = sem("o_ready"), sem("ya_add")
        ple_ms, ple_rt, ple_n = sem("ple_ms"), sem("ple_rt"), sem("ple_n")
        h2_n, h2_st, pn_st = sem("h2_n"), sem("h2_stored"), sem("pn_stored")
        rt_logit, rt_score, m_ready = sem("rt_logit"), sem("rt_score"), sem("m_ready")
        rk_done, ks_done, rank_ready, R_ready, nb_ready = sem("rk_done"), sem("ks_done"), sem("rank_ready"), sem("R_ready"), sem("nb_ready")
        sh_gu, sh_silu, sh_a, sh_at, sh_aT, sh_dn, sh_y = (sem(f"sh_{n}") for n in ("gu", "silu", "a", "at", "aT", "dn", "y"))
        held = sem("held")
        xg_zero = sem("xg_zero")
        w_gu = [sem(f"w_gu{r}") for r in range(RING)]
        w_dn = [sem(f"w_dn{r}") for r in range(RING)]
        sel_ready, tab_done, idx_ready = sem("sel_ready"), sem("tab_done"), sem("idx_ready")
        gath = [sem(f"gathered{i}") for i in range(2)]
        scat = [sem(f"scattered{i}") for i in range(2)]
        xt_done, xta, xtb = sem("xt_done"), sem("xt_evac_a"), sem("xt_evac_b")
        gu_done, silu_done, a_ready, at_done, at_ready = sem("gu_done"), sem("silu_done"), sem("a_ready"), sem("at_done"), sem("at_ready")
        dn_done, yA, yB = sem("dn_done"), sem("y_evac_a"), sem("y_evac_b")
        yt_ld = [sem(f"yt_loaded{t}") for t in range(NT)]
        pn_ld, yt_add, yt_red = sem("pn_loaded"), sem("yt_add"), sem("yt_red")
        f_sq, f_ms, f_rt, f_h3 = sem("f_sq"), sem("f_ms"), sem("f_rt"), sem("f_h3")
        g_done, g_sig, g_x, out_st = sem("g_done"), sem("g_sig"), sem("g_x"), sem("out_stored")

        T_H, T_WSP, T_LAT, T_KPE, T_Q = 0, 2 * NT, 2 * NT + 2, 2 * NT + 2 + KQ + KKV, 2 * NT + 3 + KQ + KKV
        T_K = T_Q + 3 * (H // 2)
        T_M = T_K + H
        T_P = T_M + 2 * NT
        T_H2 = T_P + PLE // P
        T_MT = T_H2 + 2 * NT
        T_H3 = T_MT + 2
        assert T_H3 % 2 == 0 and T_H2 % 2 == 0
        P_SGU, P_Q, P_KV, P_WO, P_PLE = 40, 48, 64, 80, 88
        W_Q, W_KV, W_WO, W_PROJ, W_SHGU, W_SHDN, W_GATE = 10, 14, 18, 20, 21, 22, 23

        def win_at(w):
            return (w % 2) * 4096

        def last_P(w):
            if w < W_Q:
                return 4 * (w + 1)
            if w < W_KV:
                return P_Q + 4 * (w - W_Q + 1)
            if w < W_WO:
                return P_KV + 4 * (w - W_KV + 1)
            return P_WO + 4 * (w - W_WO + 1) if w < W_PROJ else P_PLE + 2 * NT

        def win_count(w):
            return 16 * (w // 2 + 1) + (16 if w % 2 and w >= W_SHGU else 0)

        def step_T(s):
            return T_Q + 3 * (s + 1) if s < 4 else T_K + 2 * (s - 3)

        def at(b, q, per_expert, c):
            val = b * int(E * per_expert) + c if b is not None else c
            return val if q is None else q * int(RING * per_expert) + val

        w_in = a["w_in"][0]

        def bc(row, n):
            return row.rearrange("(o n) -> o n", o=1).broadcast_to([P, n])

        block = ctx.enter_context(nc.Block())

        @block.sync
        def _(sp):
            for t in range(NT):
                sp.dma_start(x[:, t, :], a["x"][0, t * P:(t + 1) * P, :]).then_inc(ld_x[t], 16)

            def free(w):
                if w < W_SHGU:
                    sp.wait_ge(pj_done, last_P(w))
                else:
                    sp.wait_ge(sh_gu if w == W_SHGU else sh_dn, NT)

            def chunk(w, dst, src):
                if w >= 2:
                    free(w - 2)
                sp.dma_start(dst, src).then_inc(win_ready[w % 2], 16)

            cols = [(OFF_LAT, QL), (OFF_LAT + QL, KVL + ROPE)]
            for off in (OFF_U, OFF_V, OFF_GA, OFF_GB):
                cols += [(off, 512), (off + 512, 512)]
            for w, (off, n) in enumerate(cols):
                chunk(w, v2(win, win_at(w), KD, n),
                      w_in[:, off:off + n].rearrange("(k p) n -> p k n", p=P))
            for c in range(4):
                w = W_Q + c
                chunk(w, v2(win, win_at(w), KQ, 2 * QK),
                      a["mla_w_qb"][0][:, c * 2 * QK:(c + 1) * 2 * QK].rearrange("(k p) n -> p k n", p=P))
            for c in range(4):
                w = W_KV + c
                chunk(w, v2(win, win_at(w), KKV, 512),
                      a["mla_w_kvb"][0][:, c * 512:(c + 1) * 512].rearrange("(k p) n -> p k n", p=P))
            for c in range(2):
                w = W_WO + c
                chunk(w, v2(win, win_at(w), KD, 512),
                      a["w_o"][0][:, c * 512:(c + 1) * 512].rearrange("(k p) n -> p k n", p=P))

            def expert(e, r, one=True):
                for g, name in enumerate(("w_exp_gate", "w_exp_up")):
                    src = a[name][0][e] if one else a[name][0][bass.ds(e, 1)].rearrange("o d f -> (o d) f")
                    sp.dma_start(arena[:, r * WEXP + g * KD * FF:r * WEXP + (g + 1) * KD * FF],
                                 src.rearrange("(p k) f -> p (k f)", p=P)).then_inc(w_gu[r], 16)
                src = a["w_exp_down"][0][e] if one else a["w_exp_down"][0][bass.ds(e, 1)].rearrange("o d f -> (o d) f")
                sp.dma_start(arena[:, r * WEXP + WGU:(r + 1) * WEXP],
                             src.rearrange("(p k) f -> p (k f)", p=P)).then_inc(w_dn[r], 16)

            sp.wait_ge(ya_add, NA)
            sp.wait_ge(kp_rot, 1)
            sp.dma_start(pbuf, a["p"][0, 0].rearrange("(t q) n -> q t n", q=P)).then_inc(ld_late, 16)
            sp.dma_start(gffn, bc(a["g_ffn"][0], D)).then_inc(ld_late, 16)
            sp.dma_start(gpo, bc(a["g_ple_out"][0], D)).then_inc(ld_late, 16)
            expert(0, 0)
            chunk(W_PROJ, v2(win, win_at(W_PROJ), PLE // P, D),
                  a["w_ple_proj"][0].rearrange("(k p) n -> p k n", p=P))
            expert(1, 1)
            free(W_SHGU - 2)
            for g, name in enumerate(("w_sh_gate", "w_sh_up")):
                at0 = win_at(W_SHGU) + g * KD * FF
                sp.dma_start(win[:, at0:at0 + KD * FF],
                             a[name][0].rearrange("(p k) f -> p (k f)", p=P)).then_inc(win_ready[1], 16)
            chunk(W_SHDN, win[:, win_at(W_SHDN):win_at(W_SHDN) + WDN],
                  a["w_sh_down"][0].rearrange("(p k) f -> p (k f)", p=P))
            expert(2, 2)
            sp.wait_ge(h2_st, 16 * NT)
            sp.wait_ge(tr_done, T_MT)
            sp.wait_ge(ple_n, NT)
            expert(3, 3)
            for c in range(2):
                chunk(W_GATE + c, v2(win, win_at(W_GATE + c), KD, 512),
                      a["w_ple_gate"][0][:, c * 512:(c + 1) * 512].rearrange("(k p) n -> p k n", p=P))
            with sp.Fori(1, E // RING) as q:
                for r in range(RING):
                    sp.wait_ge(dn_done, q * RING + (r - RING + 1))
                    expert(q * RING + r, r, one=False)
            sp.wait_ge(nb_ready, 1)
            n_pass = sp.value_load(nb_i, min_val=1, max_val=NPASS_MAX)
            with sp.If(n_pass > 1):
                with sp.Fori(1, n_pass) as b:
                    with sp.Fori(0, E // RING) as q:
                        for r in range(RING):
                            sp.wait_ge(dn_done, b * E + q * RING + (r - RING + 1))
                            expert(q * RING + r, r, one=False)
            for i in range(2):
                sp.wait_ge(scat[i], n_pass * (16 * E // 2))
            for t in range(NT):
                if t == 3:
                    sp.wait_ge(yt_red, 1)
                sp.dma_start(yt[t], y_dram[t * P * TOPK:(t + 1) * P * TOPK, :]
                             .rearrange("(q s) n -> q (s n)", q=P)).then_inc(yt_ld[t], 16)
                if t == 0:
                    sp.dma_start(ya, pn_dram.rearrange("(t q) n -> q t n", q=P)).then_inc(pn_ld, 16)
            for t in range(NT):
                sp.wait_ge(g_x, 2 * (t + 1))
                sp.dma_start(out[0, t * P:(t + 1) * P, :], x[:, t, :]).then_inc(out_st, 16)
            sp.wait_ge(out_st, 16 * NT)

        @block.gpsimd
        def _(pool):
            steps = [0]

            def link(ins):
                steps[0] += 1
                ins.then_inc(pool_step, 1)
                pool.wait_ge(pool_step, steps[0])

            pool.memset(ident[:, :], 0.0)
            pool.memset(identb[:, :], 0.0)
            pool.memset(negmask[:, :], 0.0)
            pool.memset(tri[:, :], 1.0)
            link(pool.memset(ones[:, :], 1.0))
            for m in (ident, identb):
                pool.affine_select(out=m[:, :], in_=m[:, :], compare_op=ALU.not_equal, fill=1.0, base=0,
                                   pattern=[[-1, P]], channel_multiplier=1)
            pool.affine_select(out=negmask[:, :], in_=negmask[:, :], compare_op=ALU.is_ge, fill=-BIG, base=0,
                               pattern=[[-1, P]], channel_multiplier=1)
            pool.affine_select(out=tri[:, :], in_=tri[:, :], compare_op=ALU.is_ge, fill=0.0, base=-1,
                               pattern=[[1, P]], channel_multiplier=-1).then_inc(const_pool, 1)
            inv_freq = 1.0 / np.power(THETA, np.arange(HR) / HR).astype(np.float32)
            for j in range(HR):
                last = pool.memset(invf[:, j:j + 1], float(inv_freq[j]))
            last.then_inc(const_pool, 1)
            pool.wait_ge(ld_wsp, 16)
            pool.affine_select(out=wsp, in_=wsp, compare_op=ALU.is_ge, fill=0.0, base=0,
                               pattern=[[0, G], [-1, P]], channel_multiplier=1).then_inc(wsp_m, 1)
            pool.wait_ge(ld_small, 16 * NSMALL)
            link(pool.tensor_scalar(gqr[:, :], gqr[:, :], SCALE, None, ALU.mult))
            pool.wait_ge(sincos, 2)
            for tab, g in ((tabq, gqr), (tabk, gkr)):
                for i, (trig, half) in enumerate(((ang[4], 0), (ang[5], 1), (ang[4], 1), (ang[5], 0))):
                    gain = g[:, half * HR:(half + 1) * HR].unsqueeze(1).broadcast_to([P, NT, HR])
                    last = pool.tensor_tensor(tab[i], trig, gain, ALU.mult)
            link(last)

            pool.memset(addc[:, 0:1], 4096.0)
            pool.memset(addc[:, 1:2], 8192.0)
            pool.iota(addt, pattern=[[P, NT]], base=-4096, channel_multiplier=1,
                      allow_small_or_imprecise_dtypes=True)
            pool.iota(iota[:, :], pattern=[[1, SEQ]], base=0, channel_multiplier=0,
                      allow_small_or_imprecise_dtypes=True).then_inc(const_pool, 1)

            def rotate(src1, src2, tab, dst1, dst2, dup):
                def full(z):
                    return z.unsqueeze(2).broadcast_to([P, NT, 2, HR]) if len(z.shape) == 3 else z
                t1, t2 = rt
                for d, s1, s2, i1, i2, op in ((dst1, src1, src2, 0, 1, ALU.subtract),
                                              (dst2, src2, src1, 2, 3, ALU.add)):
                    pool.tensor_tensor(t1, full(s1), full(tab[i1]), ALU.mult)
                    link(pool.tensor_tensor(t2, full(s2), full(tab[i2]), ALU.mult))
                    last = pool.tensor_tensor(d, t1, t2, op)
                    if d is dst1:
                        link(last)
                return last

            pool.wait_ge(lat_n, 3)
            kr = lat[:, :, QL + KVL:LAT]
            rotate(kr[:, :, 0:HR], kr[:, :, HR:ROPE], tabk,
                   kprot[:, :, :, 0:HR], kprot[:, :, :, HR:ROPE], True).then_inc(kp_rot, 1)
            pool.wait_ge(ld_ln, 32)
            for t in range(NT):
                pool.wait_ge(ln_x, t + 1)
                link(pool.tensor_tensor(vbuf[:, t, :], vbuf[:, t, :], lng, ALU.mult))
                pool.tensor_tensor(vbuf[:, t, :], vbuf[:, t, :], lnb, ALU.add).then_inc(ln_v, 1)
            pool.wait_ge(pj_free[NT - 1], 8)
            for g in range(G):
                pool.wait_ge(pj_free[g % 4], 10 + g // 4 + 1)
                sl = slice(g * P, (g + 1) * P)
                pool.tensor_tensor(ya[:, :, sl], ya[:, :, sl], siga[:, :, sl], ALU.mult).then_inc(ya_g, 1)
            for c in range(4):
                pool.wait_ge(qk_n, c + 1)
                if c == 0:
                    pool.wait_ge(kp_rot, 1)
                else:
                    pool.wait_ge(tr_done, step_T(c - 1))
                z = qc[c % 2]
                rotate(z[:, :, :, NOPE:NOPE + HR], z[:, :, :, NOPE + HR:QK], tabq,
                       qrot[:, :, :, 0:HR], qrot[:, :, :, HR:ROPE], False).then_inc(q_rot, 1)
            pool.wait_ge(ya_g, G)
            for n in range(NA):
                h, i = divmod(n, NT)
                pool.wait_ge(o_ready, n + 1)
                dst = ya[:, i, h * VD:(h + 1) * VD]
                pool.tensor_tensor(dst, dst, otmp[n % 2], ALU.add).then_inc(ya_add, 1)
            pool.wait_ge(pn_st, 16 * NT)
            pool.memset(ya_[:, 0:2 * D], 0.0).then_inc(xg_zero, 1)
            pool.wait_ge(h2_st, 16 * NT)
            pool.wait_ge(nb_ready, 1)
            n_pass = pool.value_load(nb_i, min_val=1, max_val=NPASS_MAX)
            pool.wait_ge(xg_zero, 1)

            last_token, last_row = pool.to_reg(SEQ - 1), pool.to_reg(SEQ * TOPK - 1)

            def gather(b, q, j):
                pool.wait_ge(idx_ready, at(b, q, 1, j + 1))
                if q is not None or j >= 2:
                    pool.wait_ge(xt_done, at(b, q, 1, j - 1))
                pool.sem_inc(held, 1)
                pool.indirect_dma_start(xg[j % 2], None, h2_dram,
                                        bass.IndirectOffsetOnAxis(idx[j % 4][:, 0:1], 0),
                                        bounds_check=last_token, oob_is_err=False).then_inc(gath[j % 2], 16)

            def scatter(b, q, j):
                pool.wait_ge(yA, at(b, q, 1, j + 1))
                pool.wait_ge(yB, at(b, q, 1, j + 1))
                pool.sem_inc(held, 1)
                pool.indirect_dma_start(y_dram, bass.IndirectOffsetOnAxis(idx[j % 4][:, 1:2], 0),
                                        yo[j % 2], None,
                                        bounds_check=last_row, oob_is_err=False).then_inc(scat[j % 2], 16)

            def step(b, q, j):
                if q is not None or j + 2 < E:
                    gather(b, q, j + 2)
                if q is not None or 1 <= j <= E:
                    scatter(b, q, j - 1)

            with pool.Fori(0, n_pass) as b:
                for j in range(-2, 6):
                    step(b, None, j)
                with pool.Fori(0, Q_LOOP) as q:
                    for j in range(6, 6 + RING):
                        step(b, q, j)
                for j in range(E - 2, E + 1):
                    step(b, None, j)
                for i in range(2):
                    pool.wait_ge(scat[i], at(b, None, 8, 16 * E // 2))
            for t in range(NT):
                pool.wait_ge(yt_ld[t], 16)
                z = yt[t]
                pool.tensor_tensor(z[:, 6 * D:7 * D], z[:, 6 * D:7 * D], z[:, 7 * D:8 * D], ALU.add).then_inc(yt_add, 1)

        @block.scalar
        def _(act):
            def small(dst, src):
                act.dma_start(dst, src).then_inc(ld_small, 16)

            act.dma_start(pos_i, a["positions"][0].rearrange("(t p) -> t p", p=P)).then_inc(ld_pos, 16)
            first = NT
            for name, n in ROWS[1:]:
                src = a[name][0] if name == "sgu_b" else a[name][0].rearrange("(k p) -> k p", p=P)
                act.dma_start(rows[first:first + n, :], src).then_inc(ld_pos, 16)
                first += n
            act.dma_start(wsp, a["sgu_w"][0].rearrange("g i j -> i g j")).then_inc(ld_wsp, 16)
            small(gqr[:, :], bc(a["qk_g_q_rope"][0], ROPE))
            small(gkr[:, :], bc(a["qk_g_k_rope"][0], ROPE))
            small(brt[:, :], bc(a["b_router"][0], E))
            small(wr[:, :], a["w_router"][0].rearrange("(p k) e -> p (k e)", p=P))
            act.dma_start(lng, bc(a["sgu_ln_g"][0], D)).then_inc(ld_ln, 16)
            act.dma_start(lnb, bc(a["sgu_ln_b"][0], D)).then_inc(ld_ln, 16)

            for t in range(NT):
                act.wait_ge(ld_x[t], 16)
                act.activation(hst[t], x[:, t, :], ACT.Square, accum_out=st[0][:, t:t + 1]).then_inc(rms_sq, 1)
                act.wait_ge(rms_ms, t + 1)
                act.activation(st[2][:, t:t + 1], st[1][:, t:t + 1], ACT.Sqrt).then_inc(rms_rt, 1)
            act.wait_ge(ang_r, 2)
            act.activation(ang[5], ang[1], ACT.Sin).then_inc(sincos, 1)
            act.activation(ang[4], ang[3], ACT.Sin).then_inc(sincos, 1)
            for i in range(2):
                T = T_WSP + i
                act.wait_ge(tr_done, T + 1)
                act.activation(wspT[:, 4 * i:4 * i + 4, :], bank[4 + T % 2][:, :].rearrange("p (g i) -> p g i", g=4),
                               ACT.Copy).then_inc(tr_free[T % 2], 1)
            for t in range(NT):
                act.wait_ge(pj_done, t + 1)
                act.activation(lat[:, t, 0:QL], bank[t][:, 0:QL], ACT.Copy)
                act.activation(arena[:, o_latT + t * QL:o_latT + (t + 1) * QL], bank[t][:, 0:QL], ACT.Square,
                               accum_out=ssl[:, t:t + 1]).then_inc(pj_free[t], 1)
            for t in range(NT):
                act.wait_ge(pj_done, NT + t + 1)
                act.activation(lat[:, t, QL:LAT], bank[t][:, 0:KVL + ROPE], ACT.Copy)
                act.activation(arena[:, o_latT + 4 * QL + t * KVL:o_latT + 4 * QL + (t + 1) * KVL], bank[t][:, 0:KVL], ACT.Square, accum_out=ssl[:, NT + t:NT + t + 1])
                act.activation(kpeT[:, t * ROPE:(t + 1) * ROPE], bank[t][:, KVL:KVL + ROPE], ACT.Square,
                               accum_out=ssl[:, 2 * NT + t:2 * NT + t + 1]).then_inc(pj_free[t], 1)
            act.wait_ge(lat_ms, 3)
            act.activation(ssl, msl, ACT.Sqrt).then_inc(lat_rt, 1)
            for w in range(2, 6):
                for t in range(NT):
                    act.wait_ge(pj_done, 4 * w + t + 1)
                    c = w % 2
                    dst = (ya if w < 4 else vbuf)[:, t, c * 512:(c + 1) * 512]
                    act.activation(dst, bank[t][:, :], ACT.Gelu_apprx_tanh).then_inc(pj_free[t], 1)
            act.wait_ge(ln_ms, NT)
            act.activation(st[4], st[3], ACT.Sqrt).then_inc(ln_rt, 1)
            for w in range(6, 10):
                for t in range(NT):
                    act.wait_ge(pj_done, 4 * w + t + 1)
                    if w == 8 and t == 0:
                        act.wait_ge(tr_done, T_WSP)
                    c = w % 2
                    dst = (siga if w < 8 else sigb)[:, t, c * 512:(c + 1) * 512]
                    act.activation(dst, bank[t][:, :], ACT.Sigmoid).then_inc(pj_free[t], 1)
            for k in range(KQ + KKV + 1):
                T = T_LAT + k
                act.wait_ge(tr_done, T + 1)
                if k < KQ + KKV:
                    gain = gqa[:, k:k + 1] if k < KQ else gkva[:, k - KQ:k - KQ + 1]
                    act.activation(latT[:, k, :], bank[4 + T % 2][:, :], ACT.Copy, scale=gain).then_inc(tr_free[T % 2], 1)
                else:
                    act.activation(kpeT, bank[4 + T % 2][:, :], ACT.Copy).then_inc(tr_free[T % 2], 1)
            for s in range(9):
                if s < 8:
                    for t in range(NT):
                        n = P_Q + 4 * s + t
                        act.wait_ge(pj_done, n + 1)
                        if t == 0:
                            if s >= 1:
                                act.wait_ge(qk_ms, s)
                            if s >= 2:
                                act.wait_ge(tr_done, step_T(s - 2))
                            if s == 0:
                                act.wait_ge(ln_v, NT)
                        b_ = bank[n % 4]
                        if s < 4:
                            src = b_[:, 0:2 * QK].rearrange("p (h d) -> p h d", h=2)
                            act.activation(qc[s % 2][:, t], src, ACT.Copy)
                            act.activation(sqc[:, t], src, ACT.Square).then_inc(pj_free[n % 4], 1)
                        else:
                            src = b_[:, :].rearrange("p (h d) -> p h d", h=2)
                            c = s - 4
                            act.activation(qc[s % 2][:, t, :, 0:NOPE], src[:, :, 0:NOPE], ACT.Copy)
                            act.activation(sqc[:, t, :, 0:NOPE], src[:, :, 0:NOPE], ACT.Square)
                            act.activation(V[:, t, 2 * c:2 * c + 2, :], src[:, :, NOPE:], ACT.Copy).then_inc(pj_free[n % 4], 1)
                if 1 <= s <= 4:
                    c = s - 1
                    for h in range(2):
                        T = T_Q + 3 * c + h
                        act.wait_ge(tr_done, T + 1)
                        act.activation(qT[:, 2 * c + h, :], bank[4 + T % 2][:, :], ACT.Copy, scale=gqk).then_inc(tr_free[T % 2], 1)
                if s < 8:
                    act.wait_ge(qk_ms, s + 1)
                    n = 16 if s < 4 else 8
                    act.activation(ssq[:, 0:n], msq[:, 0:n], ACT.Sqrt).then_inc(qk_rt, 1)
            for s in range(NA + 1):
                if s < NA:
                    i = s % NT
                    W = (i + 1) * P
                    act.wait_ge(nm_ready, s + 1)
                    if s >= 2:
                        act.wait_ge(pt_done, s - 1)
                    act.activation(probs[s % 2][:, 0:W], bank[s % 2][:, 0:W], ACT.Exp, bias=nm[:, s % 4:s % 4 + 1],
                                   accum_out=rs[:, s % 4:s % 4 + 1]).then_inc(exp_done, 1)
                if s >= 1:
                    n = s - 1
                    W = (n % NT + 1) * P
                    act.wait_ge(pt_done, n + 1)
                    if n >= 2:
                        act.wait_ge(pv_done, n - 1)
                    act.activation(probsT[n % 2][:, 0:W], bank[4 + n % 2][:, 0:W], ACT.Copy).then_inc(pt_ready, 1)
            for T in range(T_M, T_M + 2 * NT, 2):
                t = (T - T_M) // 2
                act.wait_ge(tr_done, T + 1)
                act.activation(hT[:, 0:4, t * P:(t + 1) * P], bank[4][:, :].rearrange("p (k q) -> p k q", k=4),
                               ACT.Copy).then_inc(tr_free[0], 1)
            for k in range(PLE // P):
                T = T_P + k
                act.wait_ge(tr_done, T + 1)
                act.activation(pT[:, k, :], bank[4 + T % 2][:, :], ACT.Copy).then_inc(tr_free[T % 2], 1)
            for t in range(NT):
                act.wait_ge(pj_free[t], P_PLE // 4)
                act.activation(h2s[t], x[:, t, :], ACT.Square, accum_out=st[0][:, t:t + 1]).then_inc(rms_sq, 1)
            act.wait_ge(rms_ms, NT + 1)
            act.activation(st[2], st[1], ACT.Sqrt).then_inc(rms_rt, 1)
            for n in range(2 * NT):
                t, half = divmod(n, 2)
                act.wait_ge(pj_done, P_PLE + n + 1)
                if n == 0:
                    act.wait_ge(tr_done, T_P)
                b_ = bank[(P_PLE + n) % 4]
                act.activation(ya[:, t, half * 512:(half + 1) * 512], b_[:, :], ACT.Copy)
                act.activation(work[:, (0, 512, 2 * D, 2 * D + 512)[n % 4]:][:, 0:512], b_[:, :], ACT.Square, accum_out=ssl[:, n:n + 1]).then_inc(pj_free[(P_PLE + n) % 4], 1)
            act.wait_ge(ple_ms, 1)
            act.activation(st[6], st[5], ACT.Sqrt).then_inc(ple_rt, 1)
            for t in range(NT):
                act.wait_ge(h2_n, t + 1)
                act.dma_start(h2_dram[t * P:(t + 1) * P, :], h2s[t]).then_inc(h2_st, 16)
            for T in range(T_H2, T_H2 + 2 * NT, 2):
                t = (T - T_H2) // 2
                act.wait_ge(tr_done, T + 1)
                act.activation(hT[:, 0:4, t * P:(t + 1) * P], bank[4][:, :].rearrange("p (k q) -> p k q", k=4),
                               ACT.Copy).then_inc(tr_free[0], 1)
            act.wait_ge(rt_logit, 1)
            act.activation(rt_sc, bank[7][:, 0:NT * E].rearrange("p (t e) -> p t e", t=NT), ACT.Sigmoid).then_inc(rt_score, 1)
            for t in range(NT):
                act.wait_ge(ple_n, t + 1)
                act.dma_start(pn_dram[t * P:(t + 1) * P, :], ya[:, t, :]).then_inc(pn_st, 16)
            for m in range(NT + 1):
                if m < NT:
                    act.wait_ge(sh_gu, m + 1)
                    if m >= 1:
                        act.wait_ge(sh_a, m)
                    act.activation(sg, bank[2 + m % 2][:, 0:FF], ACT.Silu).then_inc(sh_silu, 1)
                if m >= 1:
                    act.wait_ge(sh_at, m)
                    if m >= 3:
                        act.wait_ge(sh_dn, m - 2)
                    act.activation(aT[(m - 1) % 2], bank[4][:, 0:FF].rearrange("p (k q) -> p k q", k=KF),
                                   ACT.Copy).then_inc(sh_aT, 1)
            act.wait_ge(pn_st, 16 * NT)
            act.wait_ge(nb_ready, 1)
            n_pass = act.value_load(nb_i, min_val=1, max_val=NPASS_MAX)

            def step(b, q, j):
                free = q is None
                if not free or 0 <= j < E:
                    act.wait_ge(gu_done, at(b, q, 1, j + 1))
                    if not free or j >= 1:
                        act.wait_ge(a_ready, at(b, q, 1, j))
                    act.activation(sg, bank[2 + j % 2][:, 0:FF], ACT.Silu).then_inc(silu_done, 1)
                if not free or 1 <= j <= E:
                    n = j - 1
                    act.wait_ge(at_done, at(b, q, 1, n + 1))
                    if not free or n >= 2:
                        act.wait_ge(dn_done, at(b, q, 1, n - 1))
                    act.activation(aT[n % 2], bank[4][:, 0:FF].rearrange("p (k q) -> p k q", k=KF),
                                   ACT.Copy).then_inc(at_ready, 1)
                if not free or 0 <= j + 1 < E:
                    act.wait_ge(xt_done, at(b, q, 1, j + 2))
                    act.activation(xgT[:, 0:4, :], bank[0][:, :].rearrange("p (k q) -> p k q", k=4),
                                   ACT.Copy).then_inc(xta, 1)
                if not free or 1 <= j <= E:
                    n = j - 1
                    act.wait_ge(dn_done, at(b, q, 1, n + 1))
                    if not free or n >= 2:
                        act.wait_ge(scat[n % 2], at(b, q, 8, 16 * (n // 2)))
                    act.activation(yo[n % 2][:, 0:512], bank[6][:, :], ACT.Copy).then_inc(yA, 1)

            with act.Fori(0, n_pass) as b:
                for j in range(-1, 6):
                    step(b, None, j)
                with act.Fori(0, Q_LOOP) as q:
                    for j in range(6, 6 + RING):
                        step(b, q, j)
                for j in range(E - 2, E + 1):
                    step(b, None, j)
                for i in range(2):
                    act.wait_ge(scat[i], at(b, None, 8, 16 * E // 2))

            def gate(t):
                for half in range(2):
                    act.wait_ge(g_done, 2 * t + half + 1)
                    if t >= 1:
                        act.wait_ge(g_x, 2 * (t - 1) + half + 1)
                    act.activation(gt[:, half * 512:(half + 1) * 512], bank[2 * (t % 2) + half][:, :],
                                   ACT.Sigmoid).then_inc(g_sig, 1)

            for t in range(NT):
                act.wait_ge(yt_red, t + 1)
                if t >= 2:
                    act.wait_ge(tr_done, T_H3 + 2 * (t - 1))
                act.activation(h3[t % 2], x[:, t, :], ACT.Square, accum_out=st[0][:, t:t + 1]).then_inc(f_sq, 1)
                act.wait_ge(f_ms, t + 1)
                act.activation(st[2][:, t:t + 1], st[1][:, t:t + 1], ACT.Sqrt).then_inc(f_rt, 1)
                if t >= 1:
                    gate(t - 1)
            gate(NT - 1)

        @block.vector
        def _(dve):
            steps = [0]

            def link(ins):
                steps[0] += 1
                ins.then_inc(dve_step, 1)
                dve.wait_ge(dve_step, steps[0])

            def mean(dst, src, n, eps):
                return dve.tensor_scalar(dst, src, 1.0 / n, eps, ALU.mult, ALU.add)

            def rep(z, shape, axis):
                return z.unsqueeze(axis).broadcast_to(shape)

            def half_T(T):
                return bank[4 + T % 2][:, :].rearrange("p (k q) -> p k q", k=4)

            dve.wait_ge(const_pool, 2)
            dve.wait_ge(ld_pos, 16 * len(ROWS))
            dve.tensor_copy(rows[0:NT, :], pos_i).then_inc(rows_ready, 1)
            dve.wait_ge(cols_done, 1)
            link(dve.tensor_copy(sm[:, 0:NROW], bank[7][:, 0:NROW]))

            def h_evac(t):
                for half in range(2):
                    T = T_H + 2 * t + half
                    dve.wait_ge(tr_done, T + 1)
                    dve.tensor_tensor(hT[:, 4 * half:4 * half + 4, t * P:(t + 1) * P], half_T(T),
                                      rep(gmix[:, 4 * half:4 * half + 4], [P, 4, P], 2), ALU.mult).then_inc(tr_free[T % 2], 1)

            for t in range(NT):
                dve.wait_ge(rms_sq, t + 1)
                mean(st[1][:, t:t + 1], st[0][:, t:t + 1], D, EPS).then_inc(rms_ms, 1)
                dve.wait_ge(rms_rt, t + 1)
                link(dve.reciprocal(st[3][:, t:t + 1], st[2][:, t:t + 1]))
                dve.tensor_scalar(hst[t], x[:, t, :], st[3][:, t:t + 1], None, ALU.mult).then_inc(rms_x, 1)
                if t >= 1:
                    h_evac(t - 1)
            h_evac(NT - 1)
            TWO_PI = 2 * np.pi
            C1 = 6.28125
            C2 = float(np.round((TWO_PI - C1) * 2.0 ** 21) / 2.0 ** 21)
            C3 = float(np.float32(TWO_PI - C1 - C2))
            MAGIC, PI = 12582912.0, 3.1415925
            link(dve.tensor_tensor(ang[0], rep(posf, [P, NT, HR], 2), rep(invf, [P, NT, HR], 1), ALU.mult))
            for dst, shift in ((ang[1], 0.0), (ang[3], 0.25)):
                link(dve.tensor_scalar(ang[2], ang[0], 1.0 / TWO_PI, shift, ALU.mult, ALU.add))
                link(dve.tensor_scalar(ang[2], ang[2], MAGIC, MAGIC, ALU.add, ALU.subtract))
                link(dve.scalar_tensor_tensor(dst, ang[2], -C1, ang[0], ALU.mult, ALU.add))
                link(dve.scalar_tensor_tensor(dst, ang[2], -C2, dst, ALU.mult, ALU.add))
                link(dve.scalar_tensor_tensor(dst, ang[2], -C3, dst, ALU.mult, ALU.add))
                link(dve.tensor_scalar(dst, dst, shift * TWO_PI, PI, ALU.add, ALU.min))
                dve.tensor_scalar(dst, dst, -PI, None, ALU.max).then_inc(ang_r, 1)
            link(dve.tensor_tensor(gqk, gqn, gkn, ALU.mult))
            link(dve.tensor_scalar(gqk, gqk, SCALE, None, ALU.mult))
            dve.wait_ge(pj_free[NT - 1], 2)
            for i, n in enumerate((QL, KVL, ROPE)):
                mean(msl[:, i * NT:(i + 1) * NT], ssl[:, i * NT:(i + 1) * NT], n, EPS).then_inc(lat_ms, 1)
            dve.wait_ge(lat_rt, 1)
            link(dve.reciprocal(msl, ssl))
            for i, (o, n) in enumerate(((0, QL), (QL, KVL), (QL + KVL, ROPE))):
                dst = lat[:, :, o:o + n]
                dve.tensor_tensor(dst, dst, rep(msl[:, i * NT:(i + 1) * NT], [P, NT, n], 2), ALU.mult).then_inc(lat_n, 1)
            for t in range(NT):
                dve.wait_ge(pj_free[t], 6)
                dve.bn_stats(bst[t % 2][:, 0:6], vbuf[:, t, 0:512])
                link(dve.bn_stats(bst[t % 2][:, 6:12], vbuf[:, t, 512:1024]))
                link(dve.bn_aggr(mv[:, t, :], bst[t % 2]))
                dve.tensor_scalar(st[3][:, t:t + 1], mv[:, t, 1:2], LN_EPS, None, ALU.add).then_inc(ln_ms, 1)
            dve.wait_ge(ln_rt, 1)
            link(dve.reciprocal(st[5], st[4]))
            for t in range(NT):
                dve.tensor_scalar(vbuf[:, t, :], vbuf[:, t, :], mv[:, t, 0:1], st[5][:, t:t + 1],
                                  ALU.subtract, ALU.mult).then_inc(ln_x, 1)
            for g in range(G):
                n = P_SGU + g
                dve.wait_ge(pj_done, n + 1)
                dst = ya[:, :, g * P:(g + 1) * P]
                dve.scalar_tensor_tensor(dst, bank[n % 4][:, :].rearrange("p (t c) -> p t c", t=NT),
                                         bsp[:, g:g + 1], dst, ALU.add, ALU.mult).then_inc(pj_free[n % 4], 1)
            for s in range(9):
                if s < 8:
                    dve.wait_ge(pj_free[3], (P_Q + 4 * s) // 4 + 1)
                    sq = sqc.rearrange("p t h d -> p (t h) d")
                    if s < 4:
                        link(dve.tensor_reduce(ssq[:, 8:16], sq[:, :, NOPE:QK], AX.X, ALU.add))
                    link(dve.tensor_reduce(ssq[:, 0:8], sq[:, :, 0:NOPE], AX.X, ALU.add))
                    if s < 4:
                        mean(msq[:, 8:16], ssq[:, 8:16], ROPE, EPS)
                    mean(msq[:, 0:8], ssq[:, 0:8], NOPE, EPS).then_inc(qk_ms, 1)
                if 1 <= s <= 4:
                    T = T_Q + 3 * (s - 1) + 2
                    dve.wait_ge(tr_done, T + 1)
                    dve.tensor_copy(qrT[:, s - 1, :], bank[4 + T % 2][:, :]).then_inc(tr_free[T % 2], 1)
                elif s >= 5:
                    if s == 5:
                        dve.wait_ge(ya_g, G)
                    for h in range(2):
                        T = T_K + 2 * (s - 5) + h
                        dve.wait_ge(tr_done, T + 1)
                        dve.tensor_copy(kT[:, 2 * (s - 5) + h, :], bank[4 + T % 2][:, :]).then_inc(tr_free[T % 2], 1)
                if s < 8:
                    dve.wait_ge(qk_rt, s + 1)
                    n = 16 if s < 4 else 8
                    link(dve.reciprocal(msq[:, 0:n], ssq[:, 0:n]))
                    z = qc[s % 2].rearrange("p t h d -> p (t h) d")
                    if s < 4:
                        dve.tensor_tensor(z[:, :, NOPE:QK], z[:, :, NOPE:QK], rep(msq[:, 8:16], [P, 8, ROPE], 2), ALU.mult)
                    dve.tensor_tensor(z[:, :, 0:NOPE], z[:, :, 0:NOPE], rep(msq[:, 0:8], [P, 8, NOPE], 2),
                                      ALU.mult).then_inc(qk_n, 1)
            for s in range(NA + 2):
                if s < NA:
                    W = (s % NT + 1) * P
                    dve.wait_ge(s_done, s + 1)
                    dve.tensor_reduce(nm[:, s % 4:s % 4 + 1], bank[s % 2][:, 0:W], AX.X, ALU.max,
                                      negate=True).then_inc(nm_ready, 1)
                if s >= 2:
                    n = s - 2
                    h, i = divmod(n, NT)
                    dve.wait_ge(pv_done, n + 1)
                    link(dve.reciprocal(rinv[:, n % 4:n % 4 + 1], rs[:, n % 4:n % 4 + 1]))
                    if n >= 2:
                        dve.wait_ge(ya_add, n - 1)
                    dve.scalar_tensor_tensor(otmp[n % 2], bank[2 + n % 2][:, 0:VD], rinv[:, n % 4:n % 4 + 1],
                                             sigb[:, i, h * VD:(h + 1) * VD], ALU.mult, ALU.mult).then_inc(o_ready, 1)
            for T in range(T_M + 1, T_M + 2 * NT, 2):
                t = (T - T_M) // 2
                dve.wait_ge(tr_done, T + 1)
                dve.tensor_copy(hT[:, 4:8, t * P:(t + 1) * P], half_T(T)).then_inc(tr_free[1], 1)
            for c in range(2):
                for t in range(NT):
                    n = P_WO + 4 * c + t
                    dve.wait_ge(pj_done, n + 1)
                    dst = x[:, t, c * 512:(c + 1) * 512]
                    dve.tensor_tensor(dst, dst, bank[n % 4][:, :], ALU.add).then_inc(pj_free[n % 4], 1)
            dve.wait_ge(rms_sq, 2 * NT)
            mean(st[1], st[0], D, EPS).then_inc(rms_ms, 1)
            dve.wait_ge(rms_rt, NT + 1)
            link(dve.reciprocal(st[3], st[2]))
            dve.wait_ge(ld_late, 48)

            def by_block(z):
                return z.rearrange("q (p k) -> q p k", k=KD)

            for t in range(NT):
                dve.scalar_tensor_tensor(h2s[t].rearrange("q (k p) -> q p k", k=KD), by_block(x[:, t, :]),
                                         st[3][:, t:t + 1], by_block(gffn), ALU.mult, ALU.mult).then_inc(h2_n, 1)
            dve.wait_ge(pj_free[3], P_PLE // 4 + 2)
            link(dve.tensor_reduce(st[4], v2(sm, 76, NT, 2), AX.X, ALU.add))
            mean(st[5], st[4], D, EPS).then_inc(ple_ms, 1)
            dve.wait_ge(ple_rt, 1)
            link(dve.reciprocal(st[7], st[6]))
            for T in range(T_H2 + 1, T_H2 + 2 * NT, 2):
                t = (T - T_H2) // 2
                dve.wait_ge(tr_done, T + 1)
                dve.tensor_copy(hT[:, 4:8, t * P:(t + 1) * P], half_T(T)).then_inc(tr_free[1], 1)
            for t in range(NT):
                dve.scalar_tensor_tensor(ya[:, t, :], ya[:, t, :], st[7][:, t:t + 1], gpo,
                                         ALU.mult, ALU.mult).then_inc(ple_n, 1)
            link(dve.memset(low, 0.0))
            for g in range(1, NG):
                last = dve.memset(low[:, g, 0:g], 1.0)
            link(last)
            dve.wait_ge(const_pool, 3)
            dve.wait_ge(rt_score, 1)
            link(dve.tensor_tensor(rt_sel, rt_sc, rep(brt[:, :], [P, NT, E], 1), ALU.add))
            for t in range(NT):
                for g in range(NG):
                    last = dve.max(g8[:, t, g, :], rt_sel[:, t, g * EG:(g + 1) * EG])
            link(last)
            link(dve.tensor_tensor(gs, g8[:, :, :, 0], g8[:, :, :, 1], ALU.add))
            other, own = rep(gs, [P, NT, NG, NG], 2), rep(gs, [P, NT, NG, NG], 3)
            dve.tensor_tensor(rt_gt, other, own, ALU.is_gt)
            link(dve.tensor_tensor(rt_eq, other, own, ALU.is_equal))
            link(dve.tensor_tensor(rt_eq, rt_eq, low.unsqueeze(1).broadcast_to([P, NT, NG, NG]), ALU.mult))
            link(dve.tensor_tensor(rt_gt, rt_gt, rt_eq, ALU.add))
            link(dve.tensor_reduce(gr, rt_gt, AX.X, ALU.add))
            link(dve.tensor_scalar(gm, gr, float(TOPG), None, ALU.is_lt))
            link(dve.tensor_scalar(gm, gm, BIG, -BIG, ALU.mult, ALU.add))
            sel4 = rt_sel.rearrange("p t (g e) -> p t g e", g=NG)
            link(dve.tensor_tensor(sel4, sel4, rep(gm, [P, NT, NG, EG], 3), ALU.add))
            for t in range(NT):
                last = dve.max(t8[:, t, :], rt_sel[:, t, :])
            link(last)
            for t in range(NT):
                last = dve.match_replace(out=rt_rep[:, t, :], in_to_replace=t8[:, t, :],
                                         in_values=rt_sel[:, t, :], imm_value=-3e38)
            link(last)
            dve.tensor_tensor(rt_M, rt_rep, rt_sel, ALU.not_equal).then_inc(m_ready, 1)
            dve.wait_ge(m_ready, 1)
            link(dve.tensor_tensor(rt_sc, rt_sc, rt_M, ALU.mult))
            link(dve.tensor_reduce(rden, rt_sc, AX.X, ALU.add))
            link(dve.reciprocal(rden, rden))
            link(dve.tensor_scalar(rden, rden, ROUTED, None, ALU.mult))
            dve.tensor_tensor(Rv[:, :, :, 2].rearrange("p e t -> p t e"), rt_sc, rep(rden, [P, NT, E], 2), ALU.mult)
            link(dve.tensor_copy(Rv[:, :, :, 0], addt.unsqueeze(1).broadcast_to([P, E, NT])))

            def sh_hidden(m):
                dve.wait_ge(sh_silu, m + 1)
                if m >= 2:
                    dve.wait_ge(sh_at, m - 1)
                hidden(m, None).then_inc(sh_a, 1)

            def hidden(j, w):
                dst = a_[j % 2].rearrange("q k p -> q p k")
                up = bank[2 + j % 2][:, FF:2 * FF].rearrange("q (p k) -> q p k", k=KF)
                s_ = sg.rearrange("q (p k) -> q p k", k=KF)
                if w is None:
                    return dve.tensor_tensor(dst, s_, up, ALU.mult)
                return dve.scalar_tensor_tensor(dst, s_, w, up, ALU.mult, ALU.mult)

            def sh_out(m):
                dve.wait_ge(sh_dn, m + 1)
                for half in range(2):
                    dst = x[:, m, half * 512:(half + 1) * 512]
                    last = dve.tensor_tensor(dst, dst, bank[6 + half][:, :], ALU.add)
                last.then_inc(sh_y, 1)

            sh_hidden(0)
            sh_hidden(1)
            for i in range(2):
                T = T_MT + i
                dve.wait_ge(tr_done, T + 1)
                dve.tensor_copy(MT[:, i * 256:(i + 1) * 256], bank[4 + T % 2][0:E, 0:256]).then_inc(tr_free[T % 2], 1)
            sh_hidden(2)
            dve.wait_ge(rk_done, 1)
            Mv = rt_M.rearrange("p t e -> p e t")
            pr = bank[0][:, 0:NT * E].rearrange("p (t e) -> p e t", t=NT)
            link(dve.scalar_tensor_tensor(rank, pr, 1.0, Mv, ALU.add, ALU.mult))
            dve.tensor_scalar(rank_[:, :], rank_[:, :], -1.0, None, ALU.add).then_inc(rank_ready, 1)
            link(dve.tensor_reduce(cmp_[:, 0:1], bank[0][:, NT * E:NT * E + E], AX.X, ALU.max))
            for i in range(1, NPASS_MAX):
                last = dve.tensor_scalar(cmp_[:, i:i + 1], cmp_[:, 0:1], float(P * i), None, ALU.is_gt)
            link(last)
            link(dve.tensor_reduce(cmp_[:, 0:1], cmp_[:, 1:NPASS_MAX], AX.X, ALU.add))
            dve.tensor_scalar(nb_i, cmp_[0:1, 0:1], 1.0, None, ALU.add).then_inc(nb_ready, 1)
            sh_out(0)
            sh_hidden(3)
            dve.wait_ge(ks_done, 1)
            link(dve.tensor_scalar(addt, addt, 8.0, 4096.0 * 8 - 8192.0, ALU.mult, ALU.add))
            dve.tensor_tensor(Rv[:, :, :, 1], bank[1][:, 0:NT * E].rearrange("p (t e) -> p e t", t=NT),
                              addt.unsqueeze(1).broadcast_to([P, E, NT]), ALU.add).then_inc(R_ready, 1)
            for m in range(1, NT):
                sh_out(m)
            dve.wait_ge(nb_ready, 1)
            dve.wait_ge(rank_ready, 1)
            dve.wait_ge(pn_st, 16 * NT)
            n_pass = dve.value_load(nb_i, min_val=1, max_val=NPASS_MAX)

            def select(b, q, j):
                if q is not None or j >= 2:
                    dve.wait_ge(tab_done, at(b, q, 1, j - 1))
                e = j if q is None else q * RING + j
                r_ = rank[:, e, :] if q is None else rank[:, bass.ds(e, 1), :].rearrange("p o t -> p (o t)")
                dve.tensor_tensor(S_[j % 2], rep(r_, [P, NT, P], 2),
                                  iota[:, bass.ds(b * P, P)].unsqueeze(1).broadcast_to([P, NT, P]),
                                  ALU.is_equal).then_inc(sel_ready, 1)

            def step(b, q, j):
                free = q is None
                if not free or j + 2 < E:
                    n = j + 2
                    select(b, q, n)
                    dve.wait_ge(tab_done, at(b, q, 1, n + 1))
                    if not free or n >= 4:
                        dve.wait_ge(scat[n % 2], at(b, q, 8, 16 * (n // 2 - 1)))
                    dve.tensor_copy(wt[n % 4], bank[5][:, 2:3])
                    dve.tensor_tensor(idx[n % 4][:, :], bank[5][:, 0:2], addc, ALU.add).then_inc(idx_ready, 1)
                if not free or 0 <= j < E:
                    dve.wait_ge(silu_done, at(b, q, 1, j + 1))
                    if not free or j >= 2:
                        dve.wait_ge(at_done, at(b, q, 1, j - 1))
                    dve.wait_ge(idx_ready, at(b, q, 1, j + 1))
                    hidden(j, wt[j % 4]).then_inc(a_ready, 1)
                if not free or 0 <= j + 1 < E:
                    dve.wait_ge(xt_done, at(b, q, 1, j + 2))
                    dve.tensor_copy(xgT[:, 4:8, :], bank[1][:, :].rearrange("p (k q) -> p k q", k=4)).then_inc(xtb, 1)
                if not free or 1 <= j <= E:
                    n = j - 1
                    dve.wait_ge(dn_done, at(b, q, 1, n + 1))
                    if not free or n >= 2:
                        dve.wait_ge(scat[n % 2], at(b, q, 8, 16 * (n // 2)))
                    dve.tensor_copy(yo[n % 2][:, 512:1024], bank[7][:, :]).then_inc(yB, 1)

            with dve.Fori(0, n_pass) as b:
                for j in range(-2, 6):
                    step(b, None, j)
                with dve.Fori(0, Q_LOOP) as q:
                    for j in range(6, 6 + RING):
                        step(b, q, j)
                for j in range(E - 2, E + 1):
                    step(b, None, j)
                for i in range(2):
                    dve.wait_ge(scat[i], at(b, None, 8, 16 * E // 2))

            def gated(t):
                for half in range(2):
                    dve.wait_ge(g_sig, 2 * t + half + 1)
                    sl = slice(half * 512, (half + 1) * 512)
                    link(dve.tensor_tensor(gt[:, sl], gt[:, sl], ya[:, t, sl], ALU.mult))
                    dve.tensor_tensor(x[:, t, sl], x[:, t, sl], gt[:, sl], ALU.add).then_inc(g_x, 1)

            dve.wait_ge(pn_ld, 16)
            for t in range(NT):
                dve.wait_ge(yt_ld[t], 16)
                dve.wait_ge(yt_add, t + 1)
                z = yt[t]
                for i in range(1, 7):
                    link(dve.tensor_tensor(x[:, t, :], x[:, t, :], z[:, i * D:(i + 1) * D], ALU.add))
                dve.tensor_tensor(x[:, t, :], x[:, t, :], z[:, 0:D], ALU.add).then_inc(yt_red, 1)
                dve.wait_ge(f_sq, t + 1)
                mean(st[1][:, t:t + 1], st[0][:, t:t + 1], D, EPS).then_inc(f_ms, 1)
                dve.wait_ge(f_rt, t + 1)
                link(dve.reciprocal(st[3][:, t:t + 1], st[2][:, t:t + 1]))
                dve.tensor_scalar(h3[t % 2], x[:, t, :], st[3][:, t:t + 1], None, ALU.mult).then_inc(f_h3, 1)
                for half in range(2):
                    T = T_H3 + 2 * t + half
                    dve.wait_ge(tr_done, T + 1)
                    dve.tensor_tensor(hT[:, 4 * half:4 * half + 4, t * P:(t + 1) * P], half_T(T),
                                      rep(gple[:, 4 * half:4 * half + 4], [P, 4, P], 2), ALU.mult).then_inc(tr_free[T % 2], 1)
                if t >= 1:
                    gated(t - 1)
            gated(NT - 1)

        @block.tensor
        def _(pe):
            def transposes(T, srcs, rows=P):
                if T >= 2:
                    pe.wait_ge(tr_free[T % 2], T // 2)
                for i, src in enumerate(srcs):
                    last = pe.transpose(bank[4 + T % 2][0:rows, i * P:(i + 1) * P], src, ident[:, :])
                last.then_inc(tr_done, 1)

            def project(n, pairs, width):
                if n >= 4:
                    pe.wait_ge(pj_free[n % 4], n // 4)
                for i, (l, r) in enumerate(pairs):
                    last = pe.matmul(bank[n % 4][:, 0:width], l, r, start=(i == 0), stop=(i == len(pairs) - 1))
                return last

            def blocks(z, half):
                return [z[:, k * P:(k + 1) * P] for k in range(4 * half, 4 * half + 4)]

            def tok(t):
                return slice(t * P, (t + 1) * P)

            pe.wait_ge(const_pool, 1)
            pe.wait_ge(rows_ready, 1)
            pe.transpose(bank[7][:, 0:NROW], rows[0:NROW, :], ident[0:NROW, 0:NROW]).then_inc(cols_done, 1)
            for t in range(NT):
                pe.wait_ge(rms_x, t + 1)
                for half in range(2):
                    transposes(T_H + 2 * t + half, blocks(hst[t], half))
            pe.wait_ge(wsp_m, 1)
            for i in range(2):
                transposes(T_WSP + i, [wsp[:, g, :] for g in range(4 * i, 4 * i + 4)])
            for i in range(2):
                pe.wait_ge(tr_free[i], NT)

            def z_chunk(slot, width, free, ready):
                pe.wait_ge(win_ready[slot], ready)
                rhs = v2(win, win_at(slot), KD, width)
                for t in range(NT):
                    if free is not None:
                        pe.wait_ge(pj_free[t], free)
                    for k in range(KD):
                        last = pe.matmul(bank[t][:, 0:width], hT[:, k, tok(t)], rhs[:, k, :],
                                         start=(k == 0), stop=(k == KD - 1))
                    last.then_inc(pj_done, 1)

            z_chunk(0, QL, None, 16)
            z_chunk(1, KVL + ROPE, 1, 16)
            with pe.Fori(1, W_Q // 2) as i:
                for slot in range(2):
                    z_chunk(slot, 512, i * 2 + slot, i * 16 + 16)
            pe.wait_ge(lat_n, 3)
            for k in range(KQ + KKV):
                transposes(T_LAT + k, [lat[:, t, k * P:(k + 1) * P] for t in range(NT)])
            pe.wait_ge(kp_rot, 1)
            transposes(T_KPE, [kprot[:, t].rearrange("p h d -> p (h d)") for t in range(NT)])
            pe.wait_ge(ln_v, NT)
            for i in range(2):
                pe.wait_ge(tr_free[i], T_LAT // 2)
            for g in range(G):
                n = P_SGU + g
                project(n, [(wspT[:, g, :], vbuf[:, :, g * P:(g + 1) * P])], 512).then_inc(pj_done, 1)
            for i in range(2):
                pe.wait_ge(tr_free[i], T_Q // 2)
            for s in range(9):
                if s < 8:
                    w = W_Q + s
                    pe.wait_ge(win_ready[w % 2], win_count(w))
                    nk, k0, width = (KQ, 0, 2 * QK) if s < 4 else (KKV, KQ, 512)
                    rhs = v2(win, win_at(w), nk, width)
                    for t in range(NT):
                        project(P_Q + 4 * s + t, [(latT[:, k0 + k, tok(t)], rhs[:, k, :]) for k in range(nk)],
                                width).then_inc(pj_done, 1)
                if s >= 1:
                    c = s - 1
                    z = qc[c % 2]
                    pe.wait_ge(qk_n, c + 1)
                    for h in range(2):
                        transposes((T_Q + 3 * c if c < 4 else T_K + 2 * (c - 4)) + h,
                                   [z[:, t, h, 0:NOPE] for t in range(NT)])
                    if c < 4:
                        pe.wait_ge(q_rot, c + 1)
                        transposes(T_Q + 3 * c + 2, [qrot[:, t].rearrange("p h d -> p (h d)") for t in range(NT)])
            for i in range(4):
                pe.wait_ge(pj_free[i], P_WO // 4)
            for i in range(2):
                pe.wait_ge(tr_free[i], T_M // 2)
            for s in range(NA + 2):
                if s < NA:
                    h, i = divmod(s, NT)
                    W, r0 = (i + 1) * P, ROPE * (h % 2)
                    if s >= 2:
                        pe.wait_ge(exp_done, s - 1)
                    b_ = bank[s % 2]
                    pe.matmul(b_[:, 0:W], qT[:, h, tok(i)], kT[:, h, 0:W], start=True, stop=False)
                    pe.matmul(b_[:, i * P:W], identb[:, :], negmask[:, :], start=False, stop=False)
                    pe.matmul(b_[:, 0:W], qrT[r0:r0 + ROPE, h // 2, tok(i)], kpeT[r0:r0 + ROPE, 0:W],
                              start=False, stop=True).then_inc(s_done, 1)
                if 1 <= s <= NA:
                    n = s - 1
                    pe.wait_ge(exp_done, n + 1)
                    if n >= 2:
                        pe.wait_ge(pt_ready, n - 1)
                    for k in range(n % NT + 1):
                        last = pe.transpose(bank[4 + n % 2][:, tok(k)], probs[n % 2][:, tok(k)], ident[:, :])
                    last.then_inc(pt_done, 1)
                if s >= 2:
                    n = s - 2
                    h, i = divmod(n, NT)
                    pe.wait_ge(pt_ready, n + 1)
                    if n >= 2:
                        pe.wait_ge(o_ready, n - 1)
                    for k in range(i + 1):
                        last = pe.matmul(bank[2 + n % 2][:, 0:VD], probsT[n % 2][:, tok(k)], V[:, k, h, :],
                                         start=(k == 0), stop=(k == i))
                    last.then_inc(pv_done, 1)
            pe.wait_ge(ya_add, NA)
            pe.wait_ge(pt_ready, NA)
            pe.wait_ge(o_ready, NA)
            for t in range(NT):
                for half in range(2):
                    transposes(T_M + 2 * t + half, blocks(ya[:, t, :], half))
            pe.wait_ge(ld_late, 48)
            for k in range(PLE // P):
                transposes(T_P + k, [pbuf[:, t, k * P:(k + 1) * P] for t in range(NT)])
            for i in range(2):
                pe.wait_ge(tr_free[i], T_P // 2)
            for c in range(2):
                w = W_WO + c
                pe.wait_ge(win_ready[w % 2], win_count(w))
                rhs = v2(win, win_at(w), KD, 512)
                for t in range(NT):
                    project(P_WO + 4 * c + t, [(hT[:, k, tok(t)], rhs[:, k, :]) for k in range(KD)],
                            512).then_inc(pj_done, 1)
            for i in range(2):
                pe.wait_ge(tr_free[i], T_H2 // 2)
            pe.wait_ge(win_ready[W_PROJ % 2], win_count(W_PROJ))
            rhs = v2(win, win_at(W_PROJ), PLE // P, D)
            for n in range(2 * NT):
                t, half = divmod(n, 2)
                project(P_PLE + n, [(pT[:, k, tok(t)], rhs[:, k, half * 512:(half + 1) * 512])
                                    for k in range(PLE // P)], 512).then_inc(pj_done, 1)
            for t in range(NT):
                pe.wait_ge(h2_n, t + 1)
                for half in range(2):
                    transposes(T_H2 + 2 * t + half, blocks(h2s[t], half))
            for i in range(2):
                pe.wait_ge(tr_free[i], T_MT // 2)
            for t in range(NT):
                for k in range(KD):
                    last = pe.matmul(bank[7][:, t * E:(t + 1) * E], hT[:, k, tok(t)], wr[:, k * E:(k + 1) * E],
                                     start=(k == 0), stop=(k == KD - 1))
            last.then_inc(rt_logit, 1)
            for i in range(4):
                pe.wait_ge(pj_free[i], P_PLE // 4 + 2)
            pe.wait_ge(win_ready[1], win_count(W_SHGU))
            shgu = win[:, win_at(1):win_at(1) + WGU].rearrange("p (g k f) -> p k g f", g=2, k=KD)
            shdn = v2(win, win_at(0), KF, D)

            def gate_up(bk, xT, w):
                for k in range(KD):
                    last = pe.matmul(bk[:, :], xT[:, k, :], w[:, k], start=(k == 0), stop=(k == KD - 1))
                return last

            def hidden_T(a_buf):
                for k in range(KF):
                    last = pe.transpose(bank[4][:, k * P:(k + 1) * P], a_buf[:, k, :], ident[:, :])
                return last

            def down(aT_buf, w):
                for half in range(2):
                    for k in range(KF):
                        last = pe.matmul(bank[6 + half][:, :], aT_buf[:, k, :], w[:, k, half * 512:(half + 1) * 512],
                                         start=(k == 0), stop=(k == KF - 1))
                return last

            for m in range(NT + 2):
                if m < NT:
                    if m >= 2:
                        pe.wait_ge(sh_a, m - 1)
                    gate_up(bank[2 + m % 2], hT[:, :, tok(m)], shgu).then_inc(sh_gu, 1)
                if m == 2:
                    pe.wait_ge(m_ready, 1)
                    pe.wait_ge(sh_aT, 1)
                    for i in range(2):
                        T = T_MT + i
                        for t in range(2):
                            last = pe.transpose(bank[4 + i][0:E, tok(t)], rt_M[:, 2 * i + t, :], ident[:, :])
                        last.then_inc(tr_done, 1)
                    for t in range(NT):
                        for u in range(t + 1):
                            pe.matmul(bank[0][:, t * E:(t + 1) * E], (ones if u < t else tri)[:, :], rt_M[:, u, :],
                                      start=(u == 0), stop=(u == t))
                    for t in range(NT):
                        last = pe.matmul(bank[0][:, NT * E:NT * E + E], ones[:, :], rt_M[:, t, :],
                                         start=(t == 0), stop=(t == NT - 1))
                    last.then_inc(rk_done, 1)
                if m == 3:
                    for t in range(NT):
                        last = pe.matmul(bank[1][:, t * E:(t + 1) * E], MT[:, tok(t)], tri[0:E, 0:E],
                                         start=True, stop=True)
                    last.then_inc(ks_done, 1)
                if 1 <= m <= NT:
                    n = m - 1
                    pe.wait_ge(sh_a, n + 1)
                    if n >= 1:
                        pe.wait_ge(sh_aT, n)
                        for i in range(2):
                            pe.wait_ge(tr_free[i], T_H3 // 2)
                    hidden_T(a_[n % 2]).then_inc(sh_at, 1)
                if m >= 2:
                    n = m - 2
                    pe.wait_ge(sh_aT, n + 1)
                    if n == 0:
                        pe.wait_ge(win_ready[0], win_count(W_SHDN))
                        pe.wait_ge(rt_score, 1)
                    else:
                        pe.wait_ge(sh_y, n)
                    down(aT[n % 2], shdn).then_inc(sh_dn, 1)
            pe.wait_ge(R_ready, 1)
            pe.wait_ge(sh_y, NT)
            n_pass = pe.value_load(nb_i, min_val=1, max_val=NPASS_MAX)

            def step(b, q, j):
                free = q is None
                if not free or j + 2 < E:
                    n = j + 2
                    pe.wait_ge(sel_ready, at(b, q, 1, n + 1))
                    if not free or n >= 1:
                        pe.wait_ge(idx_ready, at(b, q, 1, n))
                    for t in range(NT):
                        r_ = Rv[:, n, t, :] if free else Rv[:, bass.ds(q * RING + n, 1), t, :].rearrange("p o c -> p (o c)")
                        last = pe.matmul(bank[5][:, 0:3], S_[n % 2][:, t, :], r_, start=(t == 0), stop=(t == NT - 1))
                    last.then_inc(tab_done, 1)
                if not free or 0 <= j < E:
                    pe.wait_ge(w_gu[j % RING], at(b, q, 8, 32 * (j // RING + 1)))
                    pe.wait_ge(xta, at(b, q, 1, j + 1))
                    pe.wait_ge(xtb, at(b, q, 1, j + 1))
                    if not free or j >= 2:
                        pe.wait_ge(a_ready, at(b, q, 1, j - 1))
                    gate_up(bank[2 + j % 2], xgT, wgu[j % RING]).then_inc(gu_done, 1)
                if not free or 1 <= j <= E:
                    n = j - 1
                    pe.wait_ge(a_ready, at(b, q, 1, n + 1))
                    if not free or n >= 1:
                        pe.wait_ge(at_ready, at(b, q, 1, n))
                    hidden_T(a_[n % 2]).then_inc(at_done, 1)
                if not free or 0 <= j + 1 < E:
                    n = j + 1
                    pe.wait_ge(gath[n % 2], at(b, q, 8, 16 * (n // 2 + 1)))
                    if not free or n >= 1:
                        pe.wait_ge(xta, at(b, q, 1, n))
                        pe.wait_ge(xtb, at(b, q, 1, n))
                    for k in range(KD):
                        last = pe.transpose(bank[k // 4][:, (k % 4) * P:(k % 4 + 1) * P], xg[n % 2][:, k * P:(k + 1) * P],
                                            ident[:, :])
                    last.then_inc(xt_done, 1)
                if not free or 1 <= j <= E:
                    n = j - 1
                    pe.wait_ge(at_ready, at(b, q, 1, n + 1))
                    pe.wait_ge(w_dn[n % RING], at(b, q, 4, 16 * (n // RING + 1)))
                    if not free or n >= 1:
                        pe.wait_ge(yA, at(b, q, 1, n))
                        pe.wait_ge(yB, at(b, q, 1, n))
                    down(aT[n % 2], wdn[n % RING]).then_inc(dn_done, 1)

            with pe.Fori(0, n_pass) as b:
                for j in range(-2, 6):
                    step(b, None, j)
                with pe.Fori(0, Q_LOOP) as q:
                    for j in range(6, 6 + RING):
                        step(b, q, j)
                for j in range(E - 2, E + 1):
                    step(b, None, j)
                for i in range(2):
                    pe.wait_ge(scat[i], at(b, None, 8, 16 * E // 2))

            def h3_T(t):
                pe.wait_ge(f_h3, t + 1)
                for half in range(2):
                    transposes(T_H3 + 2 * t + half, blocks(h3[t % 2], half))

            h3_T(0)
            for t in range(NT):
                for i in range(2):
                    pe.wait_ge(tr_free[i], T_H3 // 2 + t + 1)
                for half in range(2):
                    w = W_GATE + half
                    pe.wait_ge(win_ready[w % 2], win_count(w))
                    if t >= 2:
                        pe.wait_ge(g_sig, 2 * (t - 2) + half + 1)
                    rhs = v2(win, win_at(w), KD, 512)
                    for k in range(KD):
                        last = pe.matmul(bank[2 * (t % 2) + half][:, :], hT[:, k, tok(t)], rhs[:, k, :],
                                         start=(k == 0), stop=(k == KD - 1))
                    last.then_inc(g_done, 1)
                    if half == 0 and t + 1 < NT:
                        h3_T(t + 1)


_INS = ["x", "p", "positions", "g_mix", "w_in", "sgu_ln_g", "sgu_ln_b", "sgu_w", "sgu_b", "mla_g_qa", "mla_w_qb",
        "mla_g_kva", "mla_w_kvb", "qk_g_q_nope", "qk_g_k_nope", "qk_g_q_rope", "qk_g_k_rope", "w_o", "g_ffn",
        "w_router", "b_router", "w_exp_gate", "w_exp_up", "w_exp_down", "w_sh_gate", "w_sh_up", "w_sh_down",
        "g_ple_in", "w_ple_gate", "w_ple_proj", "g_ple_out"]


def kernel(**inputs):
    import concourse.bacc as bacc
    from concourse.bass_utils import run_bass_kernel_spmd

    nc = bacc.Bacc("TRN2", target_bir_lowering=False, num_devices=1)
    arrays, aps = {}, {}
    for name in _INS:
        v = np.ascontiguousarray(inputs[name])
        arrays["in_" + name] = v
        aps[name] = nc.dram_tensor("in_" + name, v.shape, mybir.dt.from_np(v.dtype), kind="ExternalInput").ap()
    out = nc.dram_tensor("out_0", arrays["in_x"].shape, mybir.dt.float32, kind="ExternalOutput").ap()
    hybrid_block_kernel(nc, aps, out)
    r = run_bass_kernel_spmd(nc, [arrays], core_ids=[0])
    return r.results[0]["out_0"]
```

```python
import concourse.bass as bass
from concourse import mybir
from contextlib import ExitStack
import numpy as np


def hybrid_block_kernel(nc, a, out):
    F32, F32R, BF16 = mybir.dt.float32, mybir.dt.float32r, mybir.dt.bfloat16
    I32, U32 = mybir.dt.int32, mybir.dt.uint32
    ALU, ACT, AX = mybir.AluOpType, mybir.ActivationFunctionType, mybir.AxisListType

    P = 128
    SEQ, D = a["x"].shape[1], a["x"].shape[2]
    NT, KD = SEQ // P, D // P
    PLE = a["p"].shape[3]
    G = a["sgu_w"].shape[1]
    QL, KVL = a["mla_w_qb"].shape[1], a["mla_w_kvb"].shape[1]
    NOPE, ROPE = a["qk_g_q_nope"].shape[1], a["qk_g_q_rope"].shape[1]
    H = a["mla_w_qb"].shape[2] // (NOPE + ROPE)
    QK, VD, HR = NOPE + ROPE, P, ROPE // 2
    E = a["w_router"].shape[2]
    FF = a["w_exp_gate"].shape[3]
    NG, TOPG, TOPK = 8, 4, 8
    EG = E // NG
    SCALE, ROUTED = float(QK) ** -0.5, 2.5
    EPS, LN_EPS, THETA = 1e-6, 1e-5, 10000.0
    BIG = 1e30
    LAT = QL + KVL + ROPE
    KQ, KKV, KF = QL // P, KVL // P, FF // P
    OFF_U, OFF_V, OFF_LAT, OFF_GA, OFF_GB = 0, D, 2 * D, 2 * D + LAT, 3 * D + LAT
    NA = H * NT
    RING = 4
    WGU, WDN = KD * 2 * FF, KF * D
    WEXP = WGU + WDN
    NS = 104
    NPASS_MAX = -(-SEQ // NS)
    Q_LOOP = (E - 8) // RING

    h2_dram = nc.dram_tensor("h2_rows", (SEQ, D), F32, kind="Internal").ap()
    pn_dram = nc.dram_tensor("ple_rows", (SEQ, D), F32, kind="Internal").ap()
    y_dram = nc.dram_tensor("expert_rows", (SEQ * TOPK, D), F32, kind="Internal").ap()

    ctx = ExitStack()
    with ctx:
        def sb(name, width, dt=F32):
            return ctx.enter_context(nc.sbuf_tensor(name, [P, width], dt))

        def sb2(name, width):
            with nc.sbuf_tensor(name + "_r", [P, width], F32R) as alias:
                pass
            t = sb(name, width)
            return t, alias

        def sem(name):
            return ctx.enter_context(nc.semaphore(name))

        def v2(t, at, x, y):
            return t[:, at:at + x * y].rearrange("p (x y) -> p x y", x=x)

        def v3(t, at, x, y, z):
            return t[:, at:at + x * y * z].rearrange("p (x y z) -> p x y z", x=x, y=y)

        xr_ = sb("resid", NT * D)
        x = v2(xr_, 0, NT, D)
        hT_, hT_r_ = sb2("hT", KD * SEQ)
        hT = v2(hT_, 0, KD, SEQ)
        V = v3(hT_, 0, NT, H, VD)
        hT_hi = v2(hT_r_, 0, KD, SEQ)
        win, win_r = sb2("win", 2 * 4096)
        ya_ = sb("ya", NT * D)
        ya = v2(ya_, 0, NT, D)
        xg = [ya_[:, i * D:(i + 1) * D] for i in range(2)]
        yo = [ya_[:, (2 + i) * D:(3 + i) * D] for i in range(2)]
        arena, arena_r = sb2("arena", RING * WEXP)

        base = 0
        def take(n):
            nonlocal base
            base += n
            return base - n
        o_qT = take(H * SEQ)
        o_kT = take(H * SEQ)
        o_sigb = take(NT * D)
        o_qrT = take(H // 2 * SEQ)
        o_qc = take(2 * NT * 2 * QK)
        o_sq = take(NT * 2 * QK)
        o_spare = take(512)
        o_tab = take(2 * 4 * NT * HR)
        o_kpeT = take(SEQ)
        o_latT = take((KQ + KKV) * SEQ)
        assert base <= RING * WEXP
        qT, kT = v2(arena, o_qT, H, SEQ), v2(arena, o_kT, H, SEQ)
        vbuf = v2(arena, o_qT, NT, D)
        whi_r = v2(arena_r, o_kT, KD, 512)
        hT_lo = v2(arena_r, o_kpeT, KD, SEQ)
        assert o_kpeT + KD * SEQ <= RING * WEXP
        sigb = v2(arena, o_sigb, NT, D)
        hst = [arena[:, o_sigb + i * D:o_sigb + (i + 1) * D] for i in range(4)]
        qrT = v2(arena, o_qrT, H // 2, SEQ)
        wsp = v2(arena, o_qrT, G, P)
        wspT = v2(arena, o_qrT + G * P, G, P)
        latT = v2(arena, o_latT, KQ + KKV, SEQ)
        lat = v2(arena, o_qc, NT, LAT)
        qc = [v3(arena, o_qc + i * NT * 2 * QK, NT, 2, QK) for i in range(2)]
        sqc = v3(arena, o_sq, NT, 2, QK)
        probs = [arena[:, o_qc + i * SEQ:o_qc + (i + 1) * SEQ] for i in range(2)]
        probsT = [arena[:, o_qc + (2 + i) * SEQ:o_qc + (3 + i) * SEQ] for i in range(2)]
        otmp = [arena[:, o_sq + i * P:o_sq + (i + 1) * P] for i in range(2)]
        lng, lnb = arena[:, o_sq:o_sq + D], arena[:, o_sq + D:o_sq + 2 * D]
        kpeT = arena[:, o_kpeT:o_kpeT + SEQ]
        tabq = [v2(arena, o_tab + i * NT * HR, NT, HR) for i in range(4)]
        tabk = [v2(arena, o_tab + (4 + i) * NT * HR, NT, HR) for i in range(4)]
        z3 = 3 * WEXP
        gffn, gpo = arena[:, z3:z3 + D], arena[:, z3 + D:z3 + 2 * D]
        h2s = [arena[:, z3 + (2 + i) * D:z3 + (3 + i) * D] for i in range(4)]
        wgu = [arena[:, r * WEXP:r * WEXP + WGU].rearrange("p (g k f) -> p k g f", g=2, k=KD)
               for r in range(RING)]
        wdn = [v2(arena, r * WEXP + WGU, KF, D) for r in range(RING)]
        YT = TOPK * D
        yt = [arena[:, (t % 3) * YT:(t % 3 + 1) * YT] for t in range(NT)]

        work = sb("work", 3328)
        S_all = work[:, 0:SEQ].bitcast(BF16)
        S_ = [S_all[:, i * SEQ:(i + 1) * SEQ].rearrange("p (t q) -> p t q", t=NT)
              for i in range(2)]
        xgT = v2(work, D, KD, P)
        sg = work[:, 2 * D:2 * D + FF]
        a_ = [v2(work, 2 * D + FF * (1 + i), KF, P) for i in range(2)]
        aT = [v2(work, 2 * D + FF * (3 + i), KF, P) for i in range(2)]
        pbuf = v2(work, 0, NT, PLE)
        pT = v2(work, D, PLE // P, SEQ)
        rt = [v3(work, 2 * D + i * 256, NT, 2, HR) for i in range(2)]
        qrot = v3(work, 0, NT, 2, ROPE)
        kprot = v3(work, 512, NT, 2, ROPE)
        ang = [v2(work, D + i * P, NT, HR) for i in range(6)]
        h3 = [work[:, i * D:(i + 1) * D] for i in range(2)]
        gt = work[:, 2 * D:3 * D]

        ident, tri, ones = sb("ident", P), sb("tri", P), sb("ones", P)
        identb, negmask = sb("identb", P, BF16), sb("negmask", P, BF16)
        iota = sb("iota", (NPASS_MAX - 1) * NS + P)
        R = sb("R", E * NT * 9, BF16)
        Rv = R[:, :].rearrange("p (e t c) -> p e t c", e=E, t=NT)
        rank_ = sb("rank", E * NT)
        rank = v2(rank_, 0, E, NT)
        wr = sb("wr", KD * E)
        brt = sb("brt", E)
        sm = sb("small", 208)
        smi = sb("smalli", 8, I32)
        NSMALL = 4
        gidx = [sb(f"gidx{i}", 1, U32) for i in range(4)]
        sidx = [sb(f"sidx{i}", 1, U32) for i in range(2)]
        slots = [sm[:, 180 + 3 * i:183 + 3 * i] for i in range(4)]
        wt = [z[:, 2:3] for z in slots]
        rows = sb("rows", P)
        ROWS = [("positions", NT), ("g_mix", KD), ("g_ple_in", KD), ("sgu_b", G), ("mla_g_qa", KQ),
                ("mla_g_kva", KKV), ("qk_g_q_nope", 1), ("qk_g_k_nope", 1)]
        NROW = sum(n for _, n in ROWS)
        col = {}
        for name, n in ROWS:
            first = sum(len_ for _, len_ in ROWS[:len(col)])
            col[name] = sm[:, first:first + n]
        posf, gmix, gple, bsp = col["positions"], col["g_mix"], col["g_ple_in"], col["sgu_b"]
        gqa, gkva, gqn, gkn = col["mla_g_qa"], col["mla_g_kva"], col["qk_g_q_nope"], col["qk_g_k_nope"]
        gqk = sm[:, 35:36]
        assert NROW <= 35
        addc = sm[:, 36:38]
        st = [sm[:, 44 + 4 * i:48 + 4 * i] for i in range(8)]
        ssl, msl = sm[:, 76:88], sm[:, 88:100]
        bst = [sm[:, 100 + 12 * i:112 + 12 * i] for i in range(2)]
        mv = v2(sm, 124, NT, 2)
        ssq, msq = sm[:, 132:148], sm[:, 148:164]
        nm, rs, rinv = sm[:, 164:168], sm[:, 168:172], sm[:, 172:176]
        pos_i = sb("pos_i", P, I32)[0:NT, :]
        nb_i = smi[0:1, 6:7]
        gqr, gkr = sb("gqr", ROPE), sb("gkr", ROPE)
        invf = iota[:, 0:HR]
        rt_sc = v2(work, D, NT, E)
        rt_sel = v2(work, D + 256, NT, E)
        rt_rep = v2(work, D + 512, NT, E)
        rt_M = v2(work, D + 768, NT, E)
        rt_gt = work[:, 0:256].rearrange("p (t g h) -> p t g h", t=NT, g=NG)
        rt_eq = work[:, 256:512].rearrange("p (t g h) -> p t g h", t=NT, g=NG)
        g8 = v3(work, 512, NT, NG, 8)
        gs, gr, gm, t8 = (v2(work, 768 + 32 * i, NT, 8) for i in range(4))
        rden = work[:, 896:896 + NT]
        low = v2(work, 900, 8, 8)
        MT = work[0:E, 0:SEQ]
        cmp_ = work[:, 964:964 + NPASS_MAX]
        addt = sm[:, 176:180]
        pcol = sm[:, 192:193]

        bank = [ctx.enter_context(nc.psum_tensor(f"bank{i}", [P, 512], F32)) for i in range(8)]

        ld_x = [sem(f"x_loaded{t}") for t in range(NT)]
        ld_small, ld_pos, ld_wsp, ld_ln = sem("small_loaded"), sem("pos_loaded"), sem("wsp_loaded"), sem("ln_loaded")
        ld_late = sem("late_loaded")
        win_ready = [sem(f"win_ready{i}") for i in range(2)]
        const_pool = sem("const_pool")
        dve_step, pool_step = sem("dve_step"), sem("pool_step")
        rms_sq, rms_ms, rms_rt, rms_x = sem("rms_sq"), sem("rms_ms"), sem("rms_rt"), sem("rms_x")
        tr_done, tr_free = sem("tr_done"), [sem(f"tr_free{i}") for i in range(2)]
        pj_done, pj_free = sem("pj_done"), [sem(f"pj_free{i}") for i in range(4)]
        lat_sq, lat_ms, lat_rt, lat_n = sem("lat_sq"), sem("lat_ms"), sem("lat_rt"), sem("lat_n")
        ang_r, sincos, tables, kp_rot = sem("ang_r"), sem("sincos"), sem("tables"), sem("kp_rot")
        rows_ready, cols_done, cols_ready = sem("rows_ready"), sem("cols_done"), sem("cols_ready")
        hi_ready, lo_ready, whi_used, hT_hi_ready = sem("hi_ready"), sem("lo_ready"), sem("whi_used"), sem("hT_hi_ready")
        ga_sig = sem("gate_a_sigmoid")
        wsp_m = sem("wsp_masked")
        ln_ms, ln_rt, ln_x, ln_v = sem("ln_ms"), sem("ln_rt"), sem("ln_x"), sem("ln_v")
        qk_ms, qk_rt, qk_n, q_rot = sem("qk_ms"), sem("qk_rt"), sem("qk_n"), sem("q_rot")
        s_done, nm_ready, exp_done = sem("s_done"), sem("nm_ready"), sem("exp_done")
        pt_done, pt_ready, pv_done = sem("pt_done"), sem("pt_ready"), sem("pv_done")
        o_ready, ya_add = sem("o_ready"), sem("ya_add")
        ple_ms, ple_rt, ple_n = sem("ple_ms"), sem("ple_rt"), sem("ple_n")
        h2_n, h2_st, pn_st = sem("h2_n"), sem("h2_stored"), sem("pn_stored")
        rt_logit, rt_score, m_ready = sem("rt_logit"), sem("rt_score"), sem("m_ready")
        rk_done, ks_done, rank_ready, R_ready, nb_ready = sem("rk_done"), sem("ks_done"), sem("rank_ready"), sem("R_ready"), sem("nb_ready")
        sh_gu, sh_silu, sh_a, sh_at, sh_aT, sh_dn, sh_y = (sem(f"sh_{n}") for n in ("gu", "silu", "a", "at", "aT", "dn", "y"))
        held = sem("held")
        xg_zero = sem("xg_zero")
        w_gu = [sem(f"w_gu{r}") for r in range(RING)]
        w_dn = [sem(f"w_dn{r}") for r in range(RING)]
        sel_ready, tab_done, tab_sum, idx_ready = sem("sel_ready"), sem("tab_done"), sem("tab_sum"), sem("idx_ready")
        gath = [sem(f"gathered{i}") for i in range(2)]
        scat = [sem(f"scattered{i}") for i in range(2)]
        xt_done, xta, xtb = sem("xt_done"), sem("xt_evac_a"), sem("xt_evac_b")
        gu_done, silu_done, a_ready, at_done, at_ready = sem("gu_done"), sem("silu_done"), sem("a_ready"), sem("at_done"), sem("at_ready")
        dn_done, yA, yB = sem("dn_done"), sem("y_evac_a"), sem("y_evac_b")
        yt_ld = [sem(f"yt_loaded{t}") for t in range(NT)]
        pn_ld, yt_add, yt_red = sem("pn_loaded"), sem("yt_add"), sem("yt_red")
        f_sq, f_ms, f_rt, f_h3 = sem("f_sq"), sem("f_ms"), sem("f_rt"), sem("f_h3")
        g_done, g_sig, g_x, out_st = sem("g_done"), sem("g_sig"), sem("g_x"), sem("out_stored")

        T_H, T_WSP, T_LAT, T_KPE, T_Q = 0, 2 * NT, 2 * NT + 2, 2 * NT + 2 + KQ + KKV, 2 * NT + 3 + KQ + KKV
        T_K = T_Q + 3 * (H // 2)
        T_M = T_K + H
        T_P = T_M + 2 * NT
        T_H2 = T_P + PLE // P
        T_MT = T_H2 + 2 * NT
        T_H3 = T_MT + 2
        assert T_H3 % 2 == 0 and T_H2 % 2 == 0
        P_SGU, P_Q, P_KV, P_WO, P_PLE = 40, 48, 64, 80, 88
        W_Q, W_KV, W_WO, W_PROJ, W_SHGU, W_SHDN, W_GATE = 10, 14, 18, 20, 21, 22, 23

        def chunk_width(w):
            return (QL, KVL + ROPE)[w] if w < 2 else 512

        def win_at(w):
            return (w % 2) * 4096

        def last_P(w):
            if w < W_Q:
                return 4 * (w + 1)
            if w < W_KV:
                return P_Q + 4 * (w - W_Q + 1)
            if w < W_WO:
                return P_KV + 4 * (w - W_KV + 1)
            return P_WO + 4 * (w - W_WO + 1) if w < W_PROJ else P_PLE + 2 * NT

        def win_count(w):
            return 16 * (w // 2 + 1) + (16 if w % 2 and w >= W_SHGU else 0)

        def step_T(s):
            return T_Q + 3 * (s + 1) if s < 4 else T_K + 2 * (s - 3)

        def at(b, q, per_expert, c):
            val = b * int(E * per_expert) + c if b is not None else c
            return val if q is None else q * int(RING * per_expert) + val

        w_in = a["w_in"][0]

        def bc(row, n):
            return row.rearrange("(o n) -> o n", o=1).broadcast_to([P, n])

        block = ctx.enter_context(nc.Block())

        @block.sync
        def _(sp):
            for t in range(NT):
                sp.dma_start(x[:, t, :], a["x"][0, t * P:(t + 1) * P, :]).then_inc(ld_x[t], 16)

            def free(w):
                if w < W_SHGU:
                    sp.wait_ge(pj_done, last_P(w))
                else:
                    sp.wait_ge(sh_gu if w == W_SHGU else sh_dn, NT)

            def chunk(w, dst, src):
                if w >= 2:
                    free(w - 2)
                sp.dma_start(dst, src).then_inc(win_ready[w % 2], 16)

            cols = [(OFF_LAT, QL), (OFF_LAT + QL, KVL + ROPE)]
            for off in (OFF_V, OFF_U, OFF_GA, OFF_GB):
                cols += [(off, 512), (off + 512, 512)]
            for w, (off, n) in enumerate(cols):
                chunk(w, v2(win, win_at(w), KD, n),
                      w_in[:, off:off + n].rearrange("(k p) n -> p k n", p=P))
            for c in range(4):
                w = W_Q + c
                chunk(w, v2(win, win_at(w), KQ, 2 * QK),
                      a["mla_w_qb"][0][:, c * 2 * QK:(c + 1) * 2 * QK].rearrange("(k p) n -> p k n", p=P))
            for c in range(4):
                w = W_KV + c
                chunk(w, v2(win, win_at(w), KKV, 512),
                      a["mla_w_kvb"][0][:, c * 512:(c + 1) * 512].rearrange("(k p) n -> p k n", p=P))
            for c in range(2):
                w = W_WO + c
                chunk(w, v2(win, win_at(w), KD, 512),
                      a["w_o"][0][:, c * 512:(c + 1) * 512].rearrange("(k p) n -> p k n", p=P))

            def expert(e, r, one=True):
                for g, name in enumerate(("w_exp_gate", "w_exp_up")):
                    src = a[name][0][e] if one else a[name][0][bass.ds(e, 1)].rearrange("o d f -> (o d) f")
                    sp.dma_start(arena[:, r * WEXP + g * KD * FF:r * WEXP + (g + 1) * KD * FF],
                                 src.rearrange("(p k) f -> p (k f)", p=P)).then_inc(w_gu[r], 16)
                src = a["w_exp_down"][0][e] if one else a["w_exp_down"][0][bass.ds(e, 1)].rearrange("o d f -> (o d) f")
                sp.dma_start(arena[:, r * WEXP + WGU:(r + 1) * WEXP],
                             src.rearrange("(p k) f -> p (k f)", p=P)).then_inc(w_dn[r], 16)

            sp.wait_ge(ya_add, NA)
            sp.wait_ge(kp_rot, 1)
            sp.dma_start(pbuf, a["p"][0, 0].rearrange("(t q) n -> q t n", q=P)).then_inc(ld_late, 16)
            sp.dma_start(gffn, bc(a["g_ffn"][0], D)).then_inc(ld_late, 16)
            sp.dma_start(gpo, bc(a["g_ple_out"][0], D)).then_inc(ld_late, 16)
            expert(0, 0)
            chunk(W_PROJ, v2(win, win_at(W_PROJ), PLE // P, D),
                  a["w_ple_proj"][0].rearrange("(k p) n -> p k n", p=P))
            expert(1, 1)
            free(W_SHGU - 2)
            for g, name in enumerate(("w_sh_gate", "w_sh_up")):
                at0 = win_at(W_SHGU) + g * KD * FF
                sp.dma_start(win[:, at0:at0 + KD * FF],
                             a[name][0].rearrange("(p k) f -> p (k f)", p=P)).then_inc(win_ready[1], 16)
            chunk(W_SHDN, win[:, win_at(W_SHDN):win_at(W_SHDN) + WDN],
                  a["w_sh_down"][0].rearrange("(p k) f -> p (k f)", p=P))
            expert(2, 2)
            sp.wait_ge(h2_st, 16 * NT)
            sp.wait_ge(tr_done, T_MT)
            sp.wait_ge(ple_n, NT)
            expert(3, 3)
            for c in range(2):
                chunk(W_GATE + c, v2(win, win_at(W_GATE + c), KD, 512),
                      a["w_ple_gate"][0][:, c * 512:(c + 1) * 512].rearrange("(k p) n -> p k n", p=P))
            with sp.Fori(1, E // RING) as q:
                for r in range(RING):
                    sp.wait_ge(dn_done, q * RING + (r - RING + 1))
                    expert(q * RING + r, r, one=False)
            sp.wait_ge(nb_ready, 1)
            n_pass = sp.value_load(nb_i, min_val=1, max_val=NPASS_MAX)
            with sp.If(n_pass > 1):
                with sp.Fori(1, n_pass) as b:
                    with sp.Fori(0, E // RING) as q:
                        for r in range(RING):
                            sp.wait_ge(dn_done, b * E + q * RING + (r - RING + 1))
                            expert(q * RING + r, r, one=False)
            for i in range(2):
                sp.wait_ge(scat[i], n_pass * (16 * E // 2))
            for t in range(NT):
                if t == 3:
                    sp.wait_ge(yt_red, 1)
                sp.dma_start(yt[t], y_dram[t * P * TOPK:(t + 1) * P * TOPK, :]
                             .rearrange("(q s) n -> q (s n)", q=P)).then_inc(yt_ld[t], 16)
                if t == 0:
                    sp.dma_start(ya, pn_dram.rearrange("(t q) n -> q t n", q=P)).then_inc(pn_ld, 16)
            for t in range(NT):
                sp.wait_ge(g_x, 2 * (t + 1))
                sp.dma_start(out[0, t * P:(t + 1) * P, :], x[:, t, :]).then_inc(out_st, 16)
            sp.wait_ge(out_st, 16 * NT)

        @block.gpsimd
        def _(pool):
            steps = [0]

            def link(ins):
                steps[0] += 1
                ins.then_inc(pool_step, 1)
                pool.wait_ge(pool_step, steps[0])

            pool.memset(ident[:, :], 0.0)
            pool.memset(identb[:, :], 0.0)
            pool.memset(negmask[:, :], 0.0)
            pool.memset(tri[:, :], 1.0)
            link(pool.memset(ones[:, :], 1.0))
            for m in (ident, identb):
                pool.affine_select(out=m[:, :], in_=m[:, :], compare_op=ALU.not_equal, fill=1.0, base=0,
                                   pattern=[[-1, P]], channel_multiplier=1)
            pool.affine_select(out=negmask[:, :], in_=negmask[:, :], compare_op=ALU.is_ge, fill=-BIG, base=0,
                               pattern=[[-1, P]], channel_multiplier=1)
            pool.affine_select(out=tri[:, :], in_=tri[:, :], compare_op=ALU.is_ge, fill=0.0, base=-1,
                               pattern=[[1, P]], channel_multiplier=-1).then_inc(const_pool, 1)
            inv_freq = 1.0 / np.power(THETA, np.arange(HR) / HR).astype(np.float32)
            for j in range(HR):
                last = pool.memset(invf[:, j:j + 1], float(inv_freq[j]))
            last.then_inc(const_pool, 1)
            pool.wait_ge(ld_wsp, 16)
            pool.affine_select(out=wsp, in_=wsp, compare_op=ALU.is_ge, fill=0.0, base=0,
                               pattern=[[0, G], [-1, P]], channel_multiplier=1).then_inc(wsp_m, 1)
            pool.wait_ge(ld_small, 16 * NSMALL)
            link(pool.tensor_scalar(gqr[:, :], gqr[:, :], SCALE, None, ALU.mult))
            pool.wait_ge(sincos, 2)
            for tab, g in ((tabq, gqr), (tabk, gkr)):
                for i, (trig, half) in enumerate(((ang[4], 0), (ang[5], 1), (ang[4], 1), (ang[5], 0))):
                    gain = g[:, half * HR:(half + 1) * HR].unsqueeze(1).broadcast_to([P, NT, HR])
                    last = pool.tensor_tensor(tab[i], trig, gain, ALU.mult)
            link(last)

            pool.memset(addc[:, 0:1], 4096.0)
            pool.memset(addc[:, 1:2], float(4096 * TOPK))
            pool.iota(pcol, pattern=[[0, 1]], base=0, channel_multiplier=1,
                      allow_small_or_imprecise_dtypes=True)
            pool.iota(addt, pattern=[[P, NT]], base=-4096, channel_multiplier=0,
                      allow_small_or_imprecise_dtypes=True)
            pool.iota(iota[:, :], pattern=[[1, (NPASS_MAX - 1) * NS + P]], base=0, channel_multiplier=0,
                      allow_small_or_imprecise_dtypes=True).then_inc(const_pool, 1)

            def rotate(src1, src2, tab, dst1, dst2, dup):
                def full(z):
                    return z.unsqueeze(2).broadcast_to([P, NT, 2, HR]) if len(z.shape) == 3 else z
                t1, t2 = rt
                for d, s1, s2, i1, i2, op in ((dst1, src1, src2, 0, 1, ALU.subtract),
                                              (dst2, src2, src1, 2, 3, ALU.add)):
                    pool.tensor_tensor(t1, full(s1), full(tab[i1]), ALU.mult)
                    link(pool.tensor_tensor(t2, full(s2), full(tab[i2]), ALU.mult))
                    last = pool.tensor_tensor(d, t1, t2, op)
                    if d is dst1:
                        link(last)
                return last

            pool.wait_ge(lat_n, 3)
            kr = lat[:, :, QL + KVL:LAT]
            rotate(kr[:, :, 0:HR], kr[:, :, HR:ROPE], tabk,
                   kprot[:, :, :, 0:HR], kprot[:, :, :, HR:ROPE], True).then_inc(kp_rot, 1)
            pool.wait_ge(ld_ln, 32)
            for t in range(NT):
                pool.wait_ge(ln_x, t + 1)
                link(pool.tensor_tensor(vbuf[:, t, :], vbuf[:, t, :], lng, ALU.mult))
                pool.tensor_tensor(vbuf[:, t, :], vbuf[:, t, :], lnb, ALU.add).then_inc(ln_v, 1)
            for c in range(4):
                pool.wait_ge(qk_n, c + 1)
                if c == 0:
                    pool.wait_ge(kp_rot, 1)
                else:
                    pool.wait_ge(tr_done, step_T(c - 1))
                z = qc[c % 2]
                rotate(z[:, :, :, NOPE:NOPE + HR], z[:, :, :, NOPE + HR:QK], tabq,
                       qrot[:, :, :, 0:HR], qrot[:, :, :, HR:ROPE], False).then_inc(q_rot, 1)
            for i in range(4):
                pool.wait_ge(pj_free[i], P_Q // 4)
            for n in range(NA):
                h, i = divmod(n, NT)
                pool.wait_ge(o_ready, n + 1)
                dst = ya[:, i, h * VD:(h + 1) * VD]
                pool.tensor_tensor(dst, dst, otmp[n % 2], ALU.add).then_inc(ya_add, 1)
            pool.wait_ge(pn_st, 16 * NT)
            pool.memset(ya_[:, 0:2 * D], 0.0).then_inc(xg_zero, 1)
            pool.wait_ge(h2_st, 16 * NT)
            pool.wait_ge(nb_ready, 1)
            n_pass = pool.value_load(nb_i, min_val=1, max_val=NPASS_MAX)
            pool.wait_ge(xg_zero, 1)

            last_token, last_row = pool.to_reg(SEQ - 1), pool.to_reg(SEQ * TOPK - 1)

            def gather(b, q, j):
                pool.wait_ge(idx_ready, at(b, q, 1, j + 1))
                if q is not None or j >= 2:
                    pool.wait_ge(xt_done, at(b, q, 1, j - 1))
                pool.sem_inc(held, 1)
                pool.indirect_dma_start(xg[j % 2][0:NS], None, h2_dram,
                                        bass.IndirectOffsetOnAxis(gidx[j % 4][0:NS, 0:1], 0),
                                        bounds_check=last_token, oob_is_err=False).then_inc(gath[j % 2], 16)

            def scatter(b, q, j):
                pool.wait_ge(yA, at(b, q, 1, j + 1))
                pool.wait_ge(yB, at(b, q, 1, j + 1))
                pool.sem_inc(held, 1)
                pool.indirect_dma_start(y_dram, bass.IndirectOffsetOnAxis(sidx[j % 2][0:NS, 0:1], 0),
                                        yo[j % 2][0:NS], None,
                                        bounds_check=last_row, oob_is_err=False).then_inc(scat[j % 2], 16)

            def step(b, q, j):
                if q is not None or 1 <= j <= E:
                    scatter(b, q, j - 1)
                if q is not None or j + 3 < E:
                    gather(b, q, j + 3)

            with pool.Fori(0, n_pass) as b:
                for j in range(-3, 5):
                    step(b, None, j)
                with pool.Fori(0, Q_LOOP) as q:
                    for j in range(5, 5 + RING):
                        step(b, q, j)
                for j in range(E - 3, E + 1):
                    step(b, None, j)
                for i in range(2):
                    pool.wait_ge(scat[i], at(b, None, 8, 16 * E // 2))
            for t in range(NT):
                pool.wait_ge(yt_ld[t], 16)
                z = yt[t]
                pool.tensor_tensor(z[:, 6 * D:7 * D], z[:, 6 * D:7 * D], z[:, 7 * D:8 * D], ALU.add).then_inc(yt_add, 1)

        @block.scalar
        def _(act):
            def small(dst, src):
                act.dma_start(dst, src).then_inc(ld_small, 16)

            act.dma_start(pos_i, a["positions"][0].rearrange("(t p) -> t p", p=P)).then_inc(ld_pos, 16)
            first = NT
            for name, n in ROWS[1:]:
                src = a[name][0] if name == "sgu_b" else a[name][0].rearrange("(k p) -> k p", p=P)
                act.dma_start(rows[first:first + n, :], src).then_inc(ld_pos, 16)
                first += n
            act.dma_start(wsp, a["sgu_w"][0].rearrange("g i j -> i g j")).then_inc(ld_wsp, 16)
            small(gqr[:, :], bc(a["qk_g_q_rope"][0], ROPE))
            small(gkr[:, :], bc(a["qk_g_k_rope"][0], ROPE))
            small(brt[:, :], bc(a["b_router"][0], E))
            small(wr[:, :], a["w_router"][0].rearrange("(p k) e -> p (k e)", p=P))
            act.dma_start(lng, bc(a["sgu_ln_g"][0], D)).then_inc(ld_ln, 16)
            act.dma_start(lnb, bc(a["sgu_ln_b"][0], D)).then_inc(ld_ln, 16)

            def hT_evac(t):
                for T in (T_H + 2 * t, T_H + 2 * t + 1):
                    act.wait_ge(tr_done, T + 1)
                    act.activation(hT_hi[:, 4 * (T % 2):4 * (T % 2) + 4, t * P:(t + 1) * P],
                                   bank[4 + T % 2][:, :].rearrange("p (k q) -> p k q", k=4), ACT.Copy).then_inc(hT_hi_ready, 1)

            def split(w):
                n = chunk_width(w)
                act.wait_ge(win_ready[w % 2], win_count(w))
                for k in range(KD):
                    if w >= 1:
                        act.wait_ge(whi_used, KD * (w - 1) + k + 1)
                    act.activation(whi_r[:, k, 0:n], v2(win, win_at(w), KD, n)[:, k, :], ACT.Copy,
                                   scale=gmix[:, k:k + 1]).then_inc(hi_ready, 1)

            for t in range(NT):
                act.wait_ge(ld_x[t], 16)
                act.activation(hst[t], x[:, t, :], ACT.Square, accum_out=st[0][:, t:t + 1]).then_inc(rms_sq, 1)
                act.wait_ge(rms_ms, t + 1)
                act.activation(st[2][:, t:t + 1], st[1][:, t:t + 1], ACT.Sqrt).then_inc(rms_rt, 1)
                if t >= 1:
                    hT_evac(t - 1)
            act.wait_ge(cols_ready, 1)
            split(0)
            hT_evac(NT - 1)
            act.wait_ge(ang_r, 2)
            act.activation(ang[5], ang[1], ACT.Sin).then_inc(sincos, 1)
            act.activation(ang[4], ang[3], ACT.Sin).then_inc(sincos, 1)

            def evac(w, t):
                act.wait_ge(pj_done, 4 * w + t + 1)
                b_ = bank[t]
                half = slice((w % 2) * 512, (w % 2 + 1) * 512)
                if w == 0:
                    act.activation(lat[:, t, 0:QL], b_[:, 0:QL], ACT.Copy)
                    act.activation(trash(t * QL, QL), b_[:, 0:QL], ACT.Square,
                                   accum_out=ssl[:, t:t + 1]).then_inc(pj_free[t], 1)
                elif w == 1:
                    act.activation(lat[:, t, QL:LAT], b_[:, 0:KVL + ROPE], ACT.Copy)
                    act.activation(trash(NT * QL + t * KVL, KVL), b_[:, 0:KVL], ACT.Square,
                                   accum_out=ssl[:, NT + t:NT + t + 1])
                    act.activation(trash(NT * (QL + KVL) + t * ROPE, ROPE), b_[:, KVL:KVL + ROPE], ACT.Square,
                                   accum_out=ssl[:, 2 * NT + t:2 * NT + t + 1]).then_inc(pj_free[t], 1)
                elif w < 4:
                    act.activation(vbuf[:, t, half], b_[:, :], ACT.Gelu_apprx_tanh).then_inc(pj_free[t], 1)
                elif w < 6:
                    act.activation(ya[:, t, half], b_[:, :], ACT.Gelu_apprx_tanh).then_inc(pj_free[t], 1)
                elif w < 8:
                    act.activation(b_[:, :], b_[:, :], ACT.Sigmoid).then_inc(ga_sig, 1)
                else:
                    act.activation(sigb[:, t, half], b_[:, :], ACT.Sigmoid).then_inc(pj_free[t], 1)

            def trash(first, n):
                return arena[:, o_sigb + first:o_sigb + first + n]

            act.wait_ge(tr_done, T_WSP)
            for w in range(W_Q):
                for t in range(NT):
                    if t == NT - 1 and w + 1 < W_Q:
                        split(w + 1)
                    evac(w, t)
                    if w == 2 and t == 1:
                        act.wait_ge(lat_ms, 3)
                        act.activation(ssl, msl, ACT.Sqrt).then_inc(lat_rt, 1)
                    if w == 4 and t == 2:
                        act.wait_ge(ln_ms, NT)
                        act.activation(st[4], st[3], ACT.Sqrt).then_inc(ln_rt, 1)
            for i in range(2):
                T = T_WSP + i
                act.wait_ge(tr_done, T + 1)
                act.activation(wspT[:, 4 * i:4 * i + 4, :], bank[4 + T % 2][:, :].rearrange("p (g i) -> p g i", g=4),
                               ACT.Copy).then_inc(tr_free[T % 2], 1)
            for k in range(KQ + KKV + 1):
                T = T_LAT + k
                act.wait_ge(tr_done, T + 1)
                if k < KQ + KKV:
                    gain = gqa[:, k:k + 1] if k < KQ else gkva[:, k - KQ:k - KQ + 1]
                    act.activation(latT[:, k, :], bank[4 + T % 2][:, :], ACT.Copy, scale=gain).then_inc(tr_free[T % 2], 1)
                else:
                    act.activation(kpeT, bank[4 + T % 2][:, :], ACT.Copy).then_inc(tr_free[T % 2], 1)
            for s in range(9):
                if s < 8:
                    for t in range(NT):
                        n = P_Q + 4 * s + t
                        act.wait_ge(pj_done, n + 1)
                        if t == 0:
                            if s >= 1:
                                act.wait_ge(qk_ms, s)
                            if s >= 2:
                                act.wait_ge(tr_done, step_T(s - 2))
                            if s == 0:
                                act.wait_ge(ln_v, NT)
                        b_ = bank[n % 4]
                        if s < 4:
                            src = b_[:, 0:2 * QK].rearrange("p (h d) -> p h d", h=2)
                            act.activation(qc[s % 2][:, t], src, ACT.Copy)
                            act.activation(sqc[:, t], src, ACT.Square).then_inc(pj_free[n % 4], 1)
                        else:
                            src = b_[:, :].rearrange("p (h d) -> p h d", h=2)
                            c = s - 4
                            act.activation(qc[s % 2][:, t, :, 0:NOPE], src[:, :, 0:NOPE], ACT.Copy)
                            act.activation(sqc[:, t, :, 0:NOPE], src[:, :, 0:NOPE], ACT.Square)
                            act.activation(V[:, t, 2 * c:2 * c + 2, :], src[:, :, NOPE:], ACT.Copy).then_inc(pj_free[n % 4], 1)
                if 1 <= s <= 4:
                    c = s - 1
                    for h in range(2):
                        T = T_Q + 3 * c + h
                        act.wait_ge(tr_done, T + 1)
                        act.activation(qT[:, 2 * c + h, :], bank[4 + T % 2][:, :], ACT.Copy, scale=gqk).then_inc(tr_free[T % 2], 1)
                if s < 8:
                    act.wait_ge(qk_ms, s + 1)
                    n = 16 if s < 4 else 8
                    act.activation(ssq[:, 0:n], msq[:, 0:n], ACT.Sqrt).then_inc(qk_rt, 1)
            for s in range(NA + 1):
                if s < NA:
                    i = s % NT
                    W = (i + 1) * P
                    act.wait_ge(nm_ready, s + 1)
                    if s >= 2:
                        act.wait_ge(pt_done, s - 1)
                    act.activation(probs[s % 2][:, 0:W], bank[s % 2][:, 0:W], ACT.Exp, bias=nm[:, s % 4:s % 4 + 1],
                                   accum_out=rs[:, s % 4:s % 4 + 1]).then_inc(exp_done, 1)
                if s >= 1:
                    n = s - 1
                    W = (n % NT + 1) * P
                    act.wait_ge(pt_done, n + 1)
                    if n >= 2:
                        act.wait_ge(pv_done, n - 1)
                    act.activation(probsT[n % 2][:, 0:W], bank[4 + n % 2][:, 0:W], ACT.Copy).then_inc(pt_ready, 1)
            for T in range(T_M, T_M + 2 * NT, 2):
                t = (T - T_M) // 2
                act.wait_ge(tr_done, T + 1)
                act.activation(hT[:, 0:4, t * P:(t + 1) * P], bank[4][:, :].rearrange("p (k q) -> p k q", k=4),
                               ACT.Copy).then_inc(tr_free[0], 1)
            for k in range(PLE // P):
                T = T_P + k
                act.wait_ge(tr_done, T + 1)
                act.activation(pT[:, k, :], bank[4 + T % 2][:, :], ACT.Copy).then_inc(tr_free[T % 2], 1)
            for t in range(NT):
                act.wait_ge(pj_free[t], P_PLE // 4)
                act.activation(h2s[t], x[:, t, :], ACT.Square, accum_out=st[0][:, t:t + 1]).then_inc(rms_sq, 1)
            act.wait_ge(rms_ms, NT + 1)
            act.activation(st[2], st[1], ACT.Sqrt).then_inc(rms_rt, 1)
            for n in range(2 * NT):
                t, half = divmod(n, 2)
                act.wait_ge(pj_done, P_PLE + n + 1)
                if n == 0:
                    act.wait_ge(tr_done, T_P)
                b_ = bank[(P_PLE + n) % 4]
                act.activation(ya[:, t, half * 512:(half + 1) * 512], b_[:, :], ACT.Copy)
                act.activation(work[:, (0, 512, 2 * D, 2 * D + 512)[n % 4]:][:, 0:512], b_[:, :], ACT.Square, accum_out=ssl[:, n:n + 1]).then_inc(pj_free[(P_PLE + n) % 4], 1)
            act.wait_ge(ple_ms, 1)
            act.activation(st[6], st[5], ACT.Sqrt).then_inc(ple_rt, 1)
            for t in range(NT):
                act.wait_ge(h2_n, t + 1)
                act.dma_start(h2_dram[t * P:(t + 1) * P, :], h2s[t]).then_inc(h2_st, 16)
            for T in range(T_H2, T_H2 + 2 * NT, 2):
                t = (T - T_H2) // 2
                act.wait_ge(tr_done, T + 1)
                act.activation(hT[:, 0:4, t * P:(t + 1) * P], bank[4][:, :].rearrange("p (k q) -> p k q", k=4),
                               ACT.Copy).then_inc(tr_free[0], 1)
            act.wait_ge(rt_logit, 1)
            act.activation(rt_sc, bank[7][:, 0:NT * E].rearrange("p (t e) -> p t e", t=NT), ACT.Sigmoid).then_inc(rt_score, 1)
            for t in range(NT):
                act.wait_ge(ple_n, t + 1)
                act.dma_start(pn_dram[t * P:(t + 1) * P, :], ya[:, t, :]).then_inc(pn_st, 16)
            for m in range(NT + 1):
                if m < NT:
                    act.wait_ge(sh_gu, m + 1)
                    if m >= 1:
                        act.wait_ge(sh_a, m)
                    act.activation(sg, bank[2 + m % 2][:, 0:FF], ACT.Silu).then_inc(sh_silu, 1)
                if m >= 1:
                    act.wait_ge(sh_at, m)
                    if m >= 3:
                        act.wait_ge(sh_dn, m - 2)
                    act.activation(aT[(m - 1) % 2], bank[4][:, 0:FF].rearrange("p (k q) -> p k q", k=KF),
                                   ACT.Copy).then_inc(sh_aT, 1)
            act.wait_ge(pn_st, 16 * NT)
            act.wait_ge(nb_ready, 1)
            n_pass = act.value_load(nb_i, min_val=1, max_val=NPASS_MAX)

            def step(b, q, j):
                free = q is None
                if not free or 0 <= j < E:
                    act.wait_ge(gu_done, at(b, q, 1, j + 1))
                    if not free or j >= 1:
                        act.wait_ge(a_ready, at(b, q, 1, j))
                    act.activation(sg, bank[2 + j % 2][:, 0:FF], ACT.Silu).then_inc(silu_done, 1)
                if not free or 1 <= j <= E:
                    n = j - 1
                    act.wait_ge(at_done, at(b, q, 1, n + 1))
                    if not free or n >= 2:
                        act.wait_ge(dn_done, at(b, q, 1, n - 1))
                    act.activation(aT[n % 2], bank[4][:, 0:FF].rearrange("p (k q) -> p k q", k=KF),
                                   ACT.Copy).then_inc(at_ready, 1)
                if not free or 0 <= j + 1 < E:
                    act.wait_ge(xt_done, at(b, q, 1, j + 2))
                    act.activation(xgT[:, 0:4, :], bank[0][:, :].rearrange("p (k q) -> p k q", k=4),
                                   ACT.Copy).then_inc(xta, 1)
                if not free or 1 <= j <= E:
                    n = j - 1
                    act.wait_ge(dn_done, at(b, q, 1, n + 1))
                    if not free or n >= 2:
                        act.wait_ge(scat[n % 2], at(b, q, 8, 16 * (n // 2)))
                    act.activation(yo[n % 2][:, 0:512], bank[6][:, :], ACT.Copy).then_inc(yA, 1)

            with act.Fori(0, n_pass) as b:
                for j in range(-1, 5):
                    step(b, None, j)
                with act.Fori(0, Q_LOOP) as q:
                    for j in range(5, 5 + RING):
                        step(b, q, j)
                for j in range(E - 3, E + 1):
                    step(b, None, j)
                for i in range(2):
                    act.wait_ge(scat[i], at(b, None, 8, 16 * E // 2))

            def gate(t):
                for half in range(2):
                    act.wait_ge(g_done, 2 * t + half + 1)
                    if t >= 1:
                        act.wait_ge(g_x, 2 * (t - 1) + half + 1)
                    act.activation(gt[:, half * 512:(half + 1) * 512], bank[2 * (t % 2) + half][:, :],
                                   ACT.Sigmoid).then_inc(g_sig, 1)

            for t in range(NT):
                act.wait_ge(yt_red, t + 1)
                if t >= 2:
                    act.wait_ge(tr_done, T_H3 + 2 * (t - 1))
                act.activation(h3[t % 2], x[:, t, :], ACT.Square, accum_out=st[0][:, t:t + 1]).then_inc(f_sq, 1)
                act.wait_ge(f_ms, t + 1)
                act.activation(st[2][:, t:t + 1], st[1][:, t:t + 1], ACT.Sqrt).then_inc(f_rt, 1)
                if t >= 1:
                    gate(t - 1)
            gate(NT - 1)

        @block.vector
        def _(dve):
            steps = [0]

            def link(ins):
                steps[0] += 1
                ins.then_inc(dve_step, 1)
                dve.wait_ge(dve_step, steps[0])

            def mean(dst, src, n, eps):
                return dve.tensor_scalar(dst, src, 1.0 / n, eps, ALU.mult, ALU.add)

            def rep(z, shape, axis):
                return z.unsqueeze(axis).broadcast_to(shape)

            def half_T(T):
                return bank[4 + T % 2][:, :].rearrange("p (k q) -> p k q", k=4)

            dve.wait_ge(const_pool, 2)
            dve.wait_ge(ld_pos, 16 * len(ROWS))
            dve.tensor_copy(rows[0:NT, :], pos_i).then_inc(rows_ready, 1)
            dve.wait_ge(cols_done, 1)
            dve.tensor_copy(sm[:, 0:NROW], bank[7][:, 0:NROW]).then_inc(cols_ready, 1)
            dve.wait_ge(cols_ready, 1)

            def h_evac(t):
                for half in range(2):
                    T = T_H + 2 * t + half
                    dve.wait_ge(hT_hi_ready, T + 1)
                    ks, q = slice(4 * half, 4 * half + 4), slice(t * P, (t + 1) * P)
                    dve.tensor_tensor(hT_lo[:, ks, q], half_T(T), hT_hi[:, ks, q].bitcast(F32), ALU.subtract).then_inc(tr_free[T % 2], 1)

            def split(w):
                n = chunk_width(w)
                for k in range(KD):
                    dve.wait_ge(hi_ready, KD * w + k + 1)
                    dve.scalar_tensor_tensor(v2(win_r, win_at(w), KD, n)[:, k, :], v2(win, win_at(w), KD, n)[:, k, :],
                                             gmix[:, k:k + 1], whi_r[:, k, 0:n].bitcast(F32), ALU.mult, ALU.subtract).then_inc(lo_ready, 1)

            for t in range(NT):
                dve.wait_ge(rms_sq, t + 1)
                mean(st[1][:, t:t + 1], st[0][:, t:t + 1], D, EPS).then_inc(rms_ms, 1)
                dve.wait_ge(rms_rt, t + 1)
                link(dve.reciprocal(st[3][:, t:t + 1], st[2][:, t:t + 1]))
                dve.tensor_scalar(hst[t], x[:, t, :], st[3][:, t:t + 1], None, ALU.mult).then_inc(rms_x, 1)
                if t >= 1:
                    h_evac(t - 1)
            split(0)
            h_evac(NT - 1)
            TWO_PI = 2 * np.pi
            C1 = 6.28125
            C2 = float(np.round((TWO_PI - C1) * 2.0 ** 21) / 2.0 ** 21)
            C3 = float(np.float32(TWO_PI - C1 - C2))
            MAGIC, PI = 12582912.0, 3.1415925
            link(dve.tensor_tensor(ang[0], rep(posf, [P, NT, HR], 2), rep(invf, [P, NT, HR], 1), ALU.mult))
            for dst, shift in ((ang[1], 0.0), (ang[3], 0.25)):
                link(dve.tensor_scalar(ang[2], ang[0], 1.0 / TWO_PI, shift, ALU.mult, ALU.add))
                link(dve.tensor_scalar(ang[2], ang[2], MAGIC, MAGIC, ALU.add, ALU.subtract))
                link(dve.scalar_tensor_tensor(dst, ang[2], -C1, ang[0], ALU.mult, ALU.add))
                link(dve.scalar_tensor_tensor(dst, ang[2], -C2, dst, ALU.mult, ALU.add))
                link(dve.scalar_tensor_tensor(dst, ang[2], -C3, dst, ALU.mult, ALU.add))
                link(dve.tensor_scalar(dst, dst, shift * TWO_PI, PI, ALU.add, ALU.min))
                dve.tensor_scalar(dst, dst, -PI, None, ALU.max).then_inc(ang_r, 1)
            link(dve.tensor_tensor(gqk, gqn, gkn, ALU.mult))
            link(dve.tensor_scalar(gqk, gqk, SCALE, None, ALU.mult))
            split(1)
            split(2)
            dve.wait_ge(pj_free[NT - 1], 2)
            for i, n in enumerate((QL, KVL, ROPE)):
                mean(msl[:, i * NT:(i + 1) * NT], ssl[:, i * NT:(i + 1) * NT], n, EPS).then_inc(lat_ms, 1)
            dve.wait_ge(lat_rt, 1)
            link(dve.reciprocal(msl, ssl))
            for i, (o, n) in enumerate(((0, QL), (QL, KVL), (QL + KVL, ROPE))):
                dst = lat[:, :, o:o + n]
                dve.tensor_tensor(dst, dst, rep(msl[:, i * NT:(i + 1) * NT], [P, NT, n], 2), ALU.mult).then_inc(lat_n, 1)
            split(3)
            split(4)
            for t in range(NT):
                dve.wait_ge(pj_free[t], 4)
                dve.bn_stats(bst[t % 2][:, 0:6], vbuf[:, t, 0:512])
                link(dve.bn_stats(bst[t % 2][:, 6:12], vbuf[:, t, 512:1024]))
                link(dve.bn_aggr(mv[:, t, :], bst[t % 2]))
                dve.tensor_scalar(st[3][:, t:t + 1], mv[:, t, 1:2], LN_EPS, None, ALU.add).then_inc(ln_ms, 1)
            dve.wait_ge(ln_rt, 1)
            link(dve.reciprocal(st[5], st[4]))
            for t in range(NT):
                dve.tensor_scalar(vbuf[:, t, :], vbuf[:, t, :], mv[:, t, 0:1], st[5][:, t:t + 1],
                                  ALU.subtract, ALU.mult).then_inc(ln_x, 1)
            split(5)
            split(6)
            for w in (6, 7):
                for t in range(NT):
                    if t == NT - 1:
                        split(w + 1)
                    dve.wait_ge(ga_sig, 4 * (w - 6) + t + 1)
                    dst = ya[:, t, (w % 2) * 512:(w % 2 + 1) * 512]
                    dve.tensor_tensor(dst, dst, bank[t][:, :], ALU.mult).then_inc(pj_free[t], 1)
            split(9)
            for g in range(G):
                n = P_SGU + g
                dve.wait_ge(pj_done, n + 1)
                dst = ya[:, :, g * P:(g + 1) * P]
                dve.scalar_tensor_tensor(dst, bank[n % 4][:, :].rearrange("p (t c) -> p t c", t=NT),
                                         bsp[:, g:g + 1], dst, ALU.add, ALU.mult).then_inc(pj_free[n % 4], 1)
            for s in range(9):
                if s < 8:
                    dve.wait_ge(pj_free[3], (P_Q + 4 * s) // 4 + 1)
                    sq = sqc.rearrange("p t h d -> p (t h) d")
                    if s < 4:
                        link(dve.tensor_reduce(ssq[:, 8:16], sq[:, :, NOPE:QK], AX.X, ALU.add))
                    link(dve.tensor_reduce(ssq[:, 0:8], sq[:, :, 0:NOPE], AX.X, ALU.add))
                    if s < 4:
                        mean(msq[:, 8:16], ssq[:, 8:16], ROPE, EPS)
                    mean(msq[:, 0:8], ssq[:, 0:8], NOPE, EPS).then_inc(qk_ms, 1)
                if 1 <= s <= 4:
                    T = T_Q + 3 * (s - 1) + 2
                    dve.wait_ge(tr_done, T + 1)
                    dve.tensor_copy(qrT[:, s - 1, :], bank[4 + T % 2][:, :]).then_inc(tr_free[T % 2], 1)
                elif s >= 5:
                    for h in range(2):
                        T = T_K + 2 * (s - 5) + h
                        dve.wait_ge(tr_done, T + 1)
                        dve.tensor_copy(kT[:, 2 * (s - 5) + h, :], bank[4 + T % 2][:, :]).then_inc(tr_free[T % 2], 1)
                if s < 8:
                    dve.wait_ge(qk_rt, s + 1)
                    n = 16 if s < 4 else 8
                    link(dve.reciprocal(msq[:, 0:n], ssq[:, 0:n]))
                    z = qc[s % 2].rearrange("p t h d -> p (t h) d")
                    if s < 4:
                        dve.tensor_tensor(z[:, :, NOPE:QK], z[:, :, NOPE:QK], rep(msq[:, 8:16], [P, 8, ROPE], 2), ALU.mult)
                    dve.tensor_tensor(z[:, :, 0:NOPE], z[:, :, 0:NOPE], rep(msq[:, 0:8], [P, 8, NOPE], 2),
                                      ALU.mult).then_inc(qk_n, 1)
            for s in range(NA + 2):
                if s < NA:
                    W = (s % NT + 1) * P
                    dve.wait_ge(s_done, s + 1)
                    dve.tensor_reduce(nm[:, s % 4:s % 4 + 1], bank[s % 2][:, 0:W], AX.X, ALU.max,
                                      negate=True).then_inc(nm_ready, 1)
                if s >= 2:
                    n = s - 2
                    h, i = divmod(n, NT)
                    dve.wait_ge(pv_done, n + 1)
                    link(dve.reciprocal(rinv[:, n % 4:n % 4 + 1], rs[:, n % 4:n % 4 + 1]))
                    if n >= 2:
                        dve.wait_ge(ya_add, n - 1)
                    dve.scalar_tensor_tensor(otmp[n % 2], bank[2 + n % 2][:, 0:VD], rinv[:, n % 4:n % 4 + 1],
                                             sigb[:, i, h * VD:(h + 1) * VD], ALU.mult, ALU.mult).then_inc(o_ready, 1)
            for T in range(T_M + 1, T_M + 2 * NT, 2):
                t = (T - T_M) // 2
                dve.wait_ge(tr_done, T + 1)
                dve.tensor_copy(hT[:, 4:8, t * P:(t + 1) * P], half_T(T)).then_inc(tr_free[1], 1)
            for c in range(2):
                for t in range(NT):
                    n = P_WO + 4 * c + t
                    dve.wait_ge(pj_done, n + 1)
                    dst = x[:, t, c * 512:(c + 1) * 512]
                    dve.tensor_tensor(dst, dst, bank[n % 4][:, :], ALU.add).then_inc(pj_free[n % 4], 1)
            dve.wait_ge(rms_sq, 2 * NT)
            mean(st[1], st[0], D, EPS).then_inc(rms_ms, 1)
            dve.wait_ge(rms_rt, NT + 1)
            link(dve.reciprocal(st[3], st[2]))
            dve.wait_ge(ld_late, 48)

            def by_block(z):
                return z.rearrange("q (p k) -> q p k", k=KD)

            for t in range(NT):
                dve.scalar_tensor_tensor(h2s[t].rearrange("q (k p) -> q p k", k=KD), by_block(x[:, t, :]),
                                         st[3][:, t:t + 1], by_block(gffn), ALU.mult, ALU.mult).then_inc(h2_n, 1)
            dve.wait_ge(pj_free[3], P_PLE // 4 + 2)
            link(dve.tensor_reduce(st[4], v2(sm, 76, NT, 2), AX.X, ALU.add))
            mean(st[5], st[4], D, EPS).then_inc(ple_ms, 1)
            dve.wait_ge(ple_rt, 1)
            link(dve.reciprocal(st[7], st[6]))
            for T in range(T_H2 + 1, T_H2 + 2 * NT, 2):
                t = (T - T_H2) // 2
                dve.wait_ge(tr_done, T + 1)
                dve.tensor_copy(hT[:, 4:8, t * P:(t + 1) * P], half_T(T)).then_inc(tr_free[1], 1)
            for t in range(NT):
                dve.scalar_tensor_tensor(ya[:, t, :], ya[:, t, :], st[7][:, t:t + 1], gpo,
                                         ALU.mult, ALU.mult).then_inc(ple_n, 1)
            link(dve.memset(low, 0.0))
            for g in range(1, NG):
                last = dve.memset(low[:, g, 0:g], 1.0)
            link(last)
            dve.wait_ge(const_pool, 3)
            dve.wait_ge(rt_score, 1)
            link(dve.tensor_tensor(rt_sel, rt_sc, rep(brt[:, :], [P, NT, E], 1), ALU.add))
            for t in range(NT):
                for g in range(NG):
                    last = dve.max(g8[:, t, g, :], rt_sel[:, t, g * EG:(g + 1) * EG])
            link(last)
            link(dve.tensor_tensor(gs, g8[:, :, :, 0], g8[:, :, :, 1], ALU.add))
            other, own = rep(gs, [P, NT, NG, NG], 2), rep(gs, [P, NT, NG, NG], 3)
            dve.tensor_tensor(rt_gt, other, own, ALU.is_gt)
            link(dve.tensor_tensor(rt_eq, other, own, ALU.is_equal))
            link(dve.tensor_tensor(rt_eq, rt_eq, low.unsqueeze(1).broadcast_to([P, NT, NG, NG]), ALU.mult))
            link(dve.tensor_tensor(rt_gt, rt_gt, rt_eq, ALU.add))
            link(dve.tensor_reduce(gr, rt_gt, AX.X, ALU.add))
            link(dve.tensor_scalar(gm, gr, float(TOPG), None, ALU.is_lt))
            link(dve.tensor_scalar(gm, gm, BIG, -BIG, ALU.mult, ALU.add))
            sel4 = rt_sel.rearrange("p t (g e) -> p t g e", g=NG)
            link(dve.tensor_tensor(sel4, sel4, rep(gm, [P, NT, NG, EG], 3), ALU.add))
            for t in range(NT):
                last = dve.max(t8[:, t, :], rt_sel[:, t, :])
            link(last)
            for t in range(NT):
                last = dve.match_replace(out=rt_rep[:, t, :], in_to_replace=t8[:, t, :],
                                         in_values=rt_sel[:, t, :], imm_value=-3e38)
            link(last)
            dve.tensor_tensor(rt_M, rt_rep, rt_sel, ALU.not_equal).then_inc(m_ready, 1)
            dve.wait_ge(m_ready, 1)
            link(dve.tensor_tensor(rt_sc, rt_sc, rt_M, ALU.mult))
            link(dve.tensor_reduce(rden, rt_sc, AX.X, ALU.add))
            link(dve.reciprocal(rden, rden))
            link(dve.tensor_scalar(rden, rden, ROUTED, None, ALU.mult))
            link(dve.tensor_tensor(rt_sc, rt_sc, rep(rden, [P, NT, E], 2), ALU.mult))
            for i in range(3):
                part = Rv[:, :, :, 6 + i].rearrange("p e t -> p t e")
                link(dve.tensor_copy(part, rt_sc))
                if i < 2:
                    link(dve.tensor_tensor(rt_sc, rt_sc, part, ALU.subtract))
            tile_ = addt.unsqueeze(1).broadcast_to([P, E, NT])
            within = pcol.unsqueeze(2).broadcast_to([P, E, NT])
            dve.tensor_copy(Rv[:, :, :, 0], within)
            dve.tensor_copy(Rv[:, :, :, 1], tile_)
            dve.memset(Rv[:, :, :, 2], 0.0)
            dve.tensor_scalar(Rv[:, :, :, 3], within, float(TOPK), None, ALU.mult)
            dve.tensor_scalar(Rv[:, :, :, 4], tile_, float(TOPK), None, ALU.mult)

            def sh_hidden(m):
                dve.wait_ge(sh_silu, m + 1)
                if m >= 2:
                    dve.wait_ge(sh_at, m - 1)
                hidden(m, None).then_inc(sh_a, 1)

            def hidden(j, w):
                dst = a_[j % 2].rearrange("q k p -> q p k")
                up = bank[2 + j % 2][:, FF:2 * FF].rearrange("q (p k) -> q p k", k=KF)
                s_ = sg.rearrange("q (p k) -> q p k", k=KF)
                if w is None:
                    return dve.tensor_tensor(dst, s_, up, ALU.mult)
                return dve.scalar_tensor_tensor(dst, s_, w, up, ALU.mult, ALU.mult)

            def sh_out(m):
                dve.wait_ge(sh_dn, m + 1)
                for half in range(2):
                    dst = x[:, m, half * 512:(half + 1) * 512]
                    last = dve.tensor_tensor(dst, dst, bank[6 + half][:, :], ALU.add)
                last.then_inc(sh_y, 1)

            sh_hidden(0)
            sh_hidden(1)
            for i in range(2):
                T = T_MT + i
                dve.wait_ge(tr_done, T + 1)
                dve.tensor_copy(MT[:, i * 256:(i + 1) * 256], bank[4 + T % 2][0:E, 0:256]).then_inc(tr_free[T % 2], 1)
            sh_hidden(2)
            dve.wait_ge(rk_done, 1)
            Mv = rt_M.rearrange("p t e -> p e t")
            pr = bank[0][:, 0:NT * E].rearrange("p (t e) -> p e t", t=NT)
            link(dve.scalar_tensor_tensor(rank, pr, 1.0, Mv, ALU.add, ALU.mult))
            dve.tensor_scalar(rank_[:, :], rank_[:, :], -1.0, None, ALU.add).then_inc(rank_ready, 1)
            link(dve.tensor_reduce(cmp_[:, 0:1], bank[0][:, NT * E:NT * E + E], AX.X, ALU.max))
            for i in range(1, NPASS_MAX):
                last = dve.tensor_scalar(cmp_[:, i:i + 1], cmp_[:, 0:1], float(NS * i), None, ALU.is_gt)
            link(last)
            link(dve.tensor_reduce(cmp_[:, 0:1], cmp_[:, 1:NPASS_MAX], AX.X, ALU.add))
            dve.tensor_scalar(nb_i, cmp_[0:1, 0:1], 1.0, None, ALU.add).then_inc(nb_ready, 1)
            sh_out(0)
            sh_hidden(3)
            dve.wait_ge(ks_done, 1)
            dve.tensor_copy(Rv[:, :, :, 5], bank[1][:, 0:NT * E].rearrange("p (t e) -> p e t", t=NT)).then_inc(R_ready, 1)
            for m in range(1, NT):
                sh_out(m)
            dve.wait_ge(nb_ready, 1)
            dve.wait_ge(rank_ready, 1)
            dve.wait_ge(pn_st, 16 * NT)
            n_pass = dve.value_load(nb_i, min_val=1, max_val=NPASS_MAX)

            def select(b, q, j):
                if q is not None or j >= 2:
                    dve.wait_ge(tab_done, at(b, q, 1, j - 1))
                e = j if q is None else q * RING + j
                r_ = rank[:, e, :] if q is None else rank[:, bass.ds(e, 1), :].rearrange("p o t -> p (o t)")
                dve.tensor_tensor(S_[j % 2], rep(r_, [P, NT, P], 2),
                                  iota[:, bass.ds(b * NS, P)].unsqueeze(1).broadcast_to([P, NT, P]),
                                  ALU.is_equal).then_inc(sel_ready, 1)

            def step(b, q, j):
                free = q is None
                if not free or j + 3 < E:
                    select(b, q, j + 3)
                if not free or 0 <= j < E:
                    dve.wait_ge(silu_done, at(b, q, 1, j + 1))
                    if not free or j >= 2:
                        dve.wait_ge(at_done, at(b, q, 1, j - 1))
                    dve.wait_ge(idx_ready, at(b, q, 1, j + 1))
                    hidden(j, wt[j % 4]).then_inc(a_ready, 1)
                if not free or 0 <= j + 1 < E:
                    dve.wait_ge(xt_done, at(b, q, 1, j + 2))
                    dve.tensor_copy(xgT[:, 4:8, :], bank[1][:, :].rearrange("p (k q) -> p k q", k=4)).then_inc(xtb, 1)
                if not free or 1 <= j <= E:
                    n = j - 1
                    dve.wait_ge(dn_done, at(b, q, 1, n + 1))
                    if not free or n >= 2:
                        dve.wait_ge(scat[n % 2], at(b, q, 8, 16 * (n // 2)))
                    dve.tensor_tensor(sidx[n % 2][:, :], slots[n % 4][:, 1:2], addc[:, 1:2], ALU.add)
                    dve.tensor_copy(yo[n % 2][:, 512:1024], bank[7][:, :]).then_inc(yB, 1)
                if not free or j + 3 < E:
                    n = j + 3
                    dve.wait_ge(tab_done, at(b, q, 1, n + 1))
                    if not free or n >= 4:
                        dve.wait_ge(yB, at(b, q, 1, n - 3))
                    dve.tensor_reduce(slots[n % 4], bank[5][:, 0:9].rearrange("p (c i) -> p c i", c=3),
                                      AX.X, ALU.add).then_inc(tab_sum, 1)
                    dve.wait_ge(tab_sum, at(b, q, 1, n + 1))
                    dve.tensor_tensor(gidx[n % 4][:, :], slots[n % 4][:, 0:1], addc[:, 0:1], ALU.add).then_inc(idx_ready, 1)

            with dve.Fori(0, n_pass) as b:
                for j in range(-3, 5):
                    step(b, None, j)
                with dve.Fori(0, Q_LOOP) as q:
                    for j in range(5, 5 + RING):
                        step(b, q, j)
                for j in range(E - 3, E + 1):
                    step(b, None, j)
                for i in range(2):
                    dve.wait_ge(scat[i], at(b, None, 8, 16 * E // 2))

            def gated(t):
                for half in range(2):
                    dve.wait_ge(g_sig, 2 * t + half + 1)
                    sl = slice(half * 512, (half + 1) * 512)
                    link(dve.tensor_tensor(gt[:, sl], gt[:, sl], ya[:, t, sl], ALU.mult))
                    dve.tensor_tensor(x[:, t, sl], x[:, t, sl], gt[:, sl], ALU.add).then_inc(g_x, 1)

            dve.wait_ge(pn_ld, 16)
            for t in range(NT):
                dve.wait_ge(yt_ld[t], 16)
                dve.wait_ge(yt_add, t + 1)
                z = yt[t]
                for i in range(1, 7):
                    link(dve.tensor_tensor(x[:, t, :], x[:, t, :], z[:, i * D:(i + 1) * D], ALU.add))
                dve.tensor_tensor(x[:, t, :], x[:, t, :], z[:, 0:D], ALU.add).then_inc(yt_red, 1)
                dve.wait_ge(f_sq, t + 1)
                mean(st[1][:, t:t + 1], st[0][:, t:t + 1], D, EPS).then_inc(f_ms, 1)
                dve.wait_ge(f_rt, t + 1)
                link(dve.reciprocal(st[3][:, t:t + 1], st[2][:, t:t + 1]))
                dve.tensor_scalar(h3[t % 2], x[:, t, :], st[3][:, t:t + 1], None, ALU.mult).then_inc(f_h3, 1)
                for half in range(2):
                    T = T_H3 + 2 * t + half
                    dve.wait_ge(tr_done, T + 1)
                    dve.tensor_tensor(hT[:, 4 * half:4 * half + 4, t * P:(t + 1) * P], half_T(T),
                                      rep(gple[:, 4 * half:4 * half + 4], [P, 4, P], 2), ALU.mult).then_inc(tr_free[T % 2], 1)
                if t >= 1:
                    gated(t - 1)
            gated(NT - 1)

        @block.tensor
        def _(pe):
            def transposes(T, srcs, rows=P):
                if T >= 2:
                    pe.wait_ge(tr_free[T % 2], T // 2)
                for i, src in enumerate(srcs):
                    last = pe.transpose(bank[4 + T % 2][0:rows, i * P:(i + 1) * P], src, ident[:, :])
                last.then_inc(tr_done, 1)

            def project(n, pairs, width):
                if n >= 4:
                    pe.wait_ge(pj_free[n % 4], n // 4)
                for i, (l, r) in enumerate(pairs):
                    last = pe.matmul(bank[n % 4][:, 0:width], l, r, start=(i == 0), stop=(i == len(pairs) - 1))
                return last

            def blocks(z, half):
                return [z[:, k * P:(k + 1) * P] for k in range(4 * half, 4 * half + 4)]

            def tok(t):
                return slice(t * P, (t + 1) * P)

            pe.wait_ge(const_pool, 1)
            pe.wait_ge(rows_ready, 1)
            pe.transpose(bank[7][:, 0:NROW], rows[0:NROW, :], ident[0:NROW, 0:NROW]).then_inc(cols_done, 1)
            for t in range(NT):
                pe.wait_ge(rms_x, t + 1)
                for half in range(2):
                    transposes(T_H + 2 * t + half, blocks(hst[t], half))

            def z_chunk(slot, width, free, before):
                lo = v2(win_r, win_at(slot), KD, width)
                for t in range(NT):
                    if free is None:
                        for i in range(2):
                            pe.wait_ge(tr_free[i], t + 1)
                    else:
                        pe.wait_ge(pj_free[t], free)
                    for k in range(KD):
                        if t == 0:
                            pe.wait_ge(lo_ready, before + k + 1)
                        x_hi, x_lo = hT_hi[:, k, tok(t)], hT_lo[:, k, tok(t)]
                        w_hi, w_lo = whi_r[:, k, 0:width], lo[:, k, :]
                        b_ = bank[t][:, 0:width]
                        pe.matmul(b_, x_hi, w_hi, start=(k == 0), stop=False)
                        last = pe.matmul(b_, x_lo, w_hi, start=False, stop=False)
                        if t == NT - 1:
                            last.then_inc(whi_used, 1)
                        last = pe.matmul(b_, x_hi, w_lo, start=False, stop=(k == KD - 1))
                    last.then_inc(pj_done, 1)

            z_chunk(0, QL, None, 0)
            z_chunk(1, KVL + ROPE, 1, KD)
            with pe.Fori(1, W_Q // 2) as i:
                for slot in range(2):
                    z_chunk(slot, 512, i * 2 + slot, i * (2 * KD) + slot * KD)
            pe.wait_ge(wsp_m, 1)
            for i in range(2):
                transposes(T_WSP + i, [wsp[:, g, :] for g in range(4 * i, 4 * i + 4)])
            pe.wait_ge(lat_n, 3)
            for k in range(KQ + KKV):
                transposes(T_LAT + k, [lat[:, t, k * P:(k + 1) * P] for t in range(NT)])
            pe.wait_ge(kp_rot, 1)
            transposes(T_KPE, [kprot[:, t].rearrange("p h d -> p (h d)") for t in range(NT)])
            pe.wait_ge(ln_v, NT)
            for i in range(2):
                pe.wait_ge(tr_free[i], T_LAT // 2)
            for g in range(G):
                n = P_SGU + g
                project(n, [(wspT[:, g, :], vbuf[:, :, g * P:(g + 1) * P])], 512).then_inc(pj_done, 1)
            for i in range(2):
                pe.wait_ge(tr_free[i], T_Q // 2)
            for s in range(9):
                if s < 8:
                    w = W_Q + s
                    pe.wait_ge(win_ready[w % 2], win_count(w))
                    nk, k0, width = (KQ, 0, 2 * QK) if s < 4 else (KKV, KQ, 512)
                    rhs = v2(win, win_at(w), nk, width)
                    for t in range(NT):
                        project(P_Q + 4 * s + t, [(latT[:, k0 + k, tok(t)], rhs[:, k, :]) for k in range(nk)],
                                width).then_inc(pj_done, 1)
                if s >= 1:
                    c = s - 1
                    z = qc[c % 2]
                    pe.wait_ge(qk_n, c + 1)
                    for h in range(2):
                        transposes((T_Q + 3 * c if c < 4 else T_K + 2 * (c - 4)) + h,
                                   [z[:, t, h, 0:NOPE] for t in range(NT)])
                    if c < 4:
                        pe.wait_ge(q_rot, c + 1)
                        transposes(T_Q + 3 * c + 2, [qrot[:, t].rearrange("p h d -> p (h d)") for t in range(NT)])
            for i in range(4):
                pe.wait_ge(pj_free[i], P_WO // 4)
            for i in range(2):
                pe.wait_ge(tr_free[i], T_M // 2)
            for s in range(NA + 2):
                if s < NA:
                    h, i = divmod(s, NT)
                    W, r0 = (i + 1) * P, ROPE * (h % 2)
                    if s >= 2:
                        pe.wait_ge(exp_done, s - 1)
                    b_ = bank[s % 2]
                    pe.matmul(b_[:, 0:W], qT[:, h, tok(i)], kT[:, h, 0:W], start=True, stop=False)
                    pe.matmul(b_[:, i * P:W], identb[:, :], negmask[:, :], start=False, stop=False)
                    pe.matmul(b_[:, 0:W], qrT[r0:r0 + ROPE, h // 2, tok(i)], kpeT[r0:r0 + ROPE, 0:W],
                              start=False, stop=True).then_inc(s_done, 1)
                if 1 <= s <= NA:
                    n = s - 1
                    pe.wait_ge(exp_done, n + 1)
                    if n >= 2:
                        pe.wait_ge(pt_ready, n - 1)
                    for k in range(n % NT + 1):
                        last = pe.transpose(bank[4 + n % 2][:, tok(k)], probs[n % 2][:, tok(k)], ident[:, :])
                    last.then_inc(pt_done, 1)
                if s >= 2:
                    n = s - 2
                    h, i = divmod(n, NT)
                    pe.wait_ge(pt_ready, n + 1)
                    if n >= 2:
                        pe.wait_ge(o_ready, n - 1)
                    for k in range(i + 1):
                        last = pe.matmul(bank[2 + n % 2][:, 0:VD], probsT[n % 2][:, tok(k)], V[:, k, h, :],
                                         start=(k == 0), stop=(k == i))
                    last.then_inc(pv_done, 1)
            pe.wait_ge(ya_add, NA)
            pe.wait_ge(pt_ready, NA)
            pe.wait_ge(o_ready, NA)
            for t in range(NT):
                for half in range(2):
                    transposes(T_M + 2 * t + half, blocks(ya[:, t, :], half))
            pe.wait_ge(ld_late, 48)
            for k in range(PLE // P):
                transposes(T_P + k, [pbuf[:, t, k * P:(k + 1) * P] for t in range(NT)])
            for i in range(2):
                pe.wait_ge(tr_free[i], T_P // 2)
            for c in range(2):
                w = W_WO + c
                pe.wait_ge(win_ready[w % 2], win_count(w))
                rhs = v2(win, win_at(w), KD, 512)
                for t in range(NT):
                    project(P_WO + 4 * c + t, [(hT[:, k, tok(t)], rhs[:, k, :]) for k in range(KD)],
                            512).then_inc(pj_done, 1)
            for i in range(2):
                pe.wait_ge(tr_free[i], T_H2 // 2)
            pe.wait_ge(win_ready[W_PROJ % 2], win_count(W_PROJ))
            rhs = v2(win, win_at(W_PROJ), PLE // P, D)
            for n in range(2 * NT):
                t, half = divmod(n, 2)
                project(P_PLE + n, [(pT[:, k, tok(t)], rhs[:, k, half * 512:(half + 1) * 512])
                                    for k in range(PLE // P)], 512).then_inc(pj_done, 1)
            for t in range(NT):
                pe.wait_ge(h2_n, t + 1)
                for half in range(2):
                    transposes(T_H2 + 2 * t + half, blocks(h2s[t], half))
            for i in range(2):
                pe.wait_ge(tr_free[i], T_MT // 2)
            for t in range(NT):
                for k in range(KD):
                    last = pe.matmul(bank[7][:, t * E:(t + 1) * E], hT[:, k, tok(t)], wr[:, k * E:(k + 1) * E],
                                     start=(k == 0), stop=(k == KD - 1))
            last.then_inc(rt_logit, 1)
            for i in range(4):
                pe.wait_ge(pj_free[i], P_PLE // 4 + 2)
            pe.wait_ge(win_ready[1], win_count(W_SHGU))
            shgu = win[:, win_at(1):win_at(1) + WGU].rearrange("p (g k f) -> p k g f", g=2, k=KD)
            shdn = v2(win, win_at(0), KF, D)

            def gate_up(bk, xT, w):
                for k in range(KD):
                    last = pe.matmul(bk[:, :], xT[:, k, :], w[:, k], start=(k == 0), stop=(k == KD - 1))
                return last

            def hidden_T(a_buf):
                for k in range(KF):
                    last = pe.transpose(bank[4][:, k * P:(k + 1) * P], a_buf[:, k, :], ident[:, :])
                return last

            def down(aT_buf, w):
                for half in range(2):
                    for k in range(KF):
                        last = pe.matmul(bank[6 + half][:, :], aT_buf[:, k, :], w[:, k, half * 512:(half + 1) * 512],
                                         start=(k == 0), stop=(k == KF - 1))
                return last

            for m in range(NT + 2):
                if m < NT:
                    if m >= 2:
                        pe.wait_ge(sh_a, m - 1)
                    gate_up(bank[2 + m % 2], hT[:, :, tok(m)], shgu).then_inc(sh_gu, 1)
                if m == 2:
                    pe.wait_ge(m_ready, 1)
                    pe.wait_ge(sh_aT, 1)
                    for i in range(2):
                        T = T_MT + i
                        for t in range(2):
                            last = pe.transpose(bank[4 + i][0:E, tok(t)], rt_M[:, 2 * i + t, :], ident[:, :])
                        last.then_inc(tr_done, 1)
                    for t in range(NT):
                        for u in range(t + 1):
                            pe.matmul(bank[0][:, t * E:(t + 1) * E], (ones if u < t else tri)[:, :], rt_M[:, u, :],
                                      start=(u == 0), stop=(u == t))
                    for t in range(NT):
                        last = pe.matmul(bank[0][:, NT * E:NT * E + E], ones[:, :], rt_M[:, t, :],
                                         start=(t == 0), stop=(t == NT - 1))
                    last.then_inc(rk_done, 1)
                if m == 3:
                    for t in range(NT):
                        last = pe.matmul(bank[1][:, t * E:(t + 1) * E], MT[:, tok(t)], tri[0:E, 0:E],
                                         start=True, stop=True)
                    last.then_inc(ks_done, 1)
                if 1 <= m <= NT:
                    n = m - 1
                    pe.wait_ge(sh_a, n + 1)
                    if n >= 1:
                        pe.wait_ge(sh_aT, n)
                        for i in range(2):
                            pe.wait_ge(tr_free[i], T_H3 // 2)
                    hidden_T(a_[n % 2]).then_inc(sh_at, 1)
                if m >= 2:
                    n = m - 2
                    pe.wait_ge(sh_aT, n + 1)
                    if n == 0:
                        pe.wait_ge(win_ready[0], win_count(W_SHDN))
                        pe.wait_ge(rt_score, 1)
                    else:
                        pe.wait_ge(sh_y, n)
                    down(aT[n % 2], shdn).then_inc(sh_dn, 1)
            pe.wait_ge(R_ready, 1)
            pe.wait_ge(sh_y, NT)
            n_pass = pe.value_load(nb_i, min_val=1, max_val=NPASS_MAX)

            def step(b, q, j):
                free = q is None
                if not free or 0 <= j < E:
                    pe.wait_ge(w_gu[j % RING], at(b, q, 8, 32 * (j // RING + 1)))
                    pe.wait_ge(xta, at(b, q, 1, j + 1))
                    pe.wait_ge(xtb, at(b, q, 1, j + 1))
                    if not free or j >= 2:
                        pe.wait_ge(a_ready, at(b, q, 1, j - 1))
                    gate_up(bank[2 + j % 2], xgT, wgu[j % RING]).then_inc(gu_done, 1)
                if not free or 1 <= j <= E:
                    n = j - 1
                    pe.wait_ge(a_ready, at(b, q, 1, n + 1))
                    if not free or n >= 1:
                        pe.wait_ge(at_ready, at(b, q, 1, n))
                    hidden_T(a_[n % 2]).then_inc(at_done, 1)
                if not free or j + 3 < E:
                    n = j + 3
                    pe.wait_ge(sel_ready, at(b, q, 1, n + 1))
                    if not free or n >= 1:
                        pe.wait_ge(idx_ready, at(b, q, 1, n))
                    for t in range(NT):
                        r_ = Rv[:, n, t, :] if free else Rv[:, bass.ds(q * RING + n, 1), t, :].rearrange("p o c -> p (o c)")
                        last = pe.matmul(bank[5][:, 0:9], S_[n % 2][:, t, :], r_, start=(t == 0), stop=(t == NT - 1))
                    last.then_inc(tab_done, 1)
                if not free or 0 <= j + 1 < E:
                    n = j + 1
                    pe.wait_ge(gath[n % 2], at(b, q, 8, 16 * (n // 2 + 1)))
                    if not free or n >= 1:
                        pe.wait_ge(xta, at(b, q, 1, n))
                        pe.wait_ge(xtb, at(b, q, 1, n))
                    for k in range(KD):
                        last = pe.transpose(bank[k // 4][:, (k % 4) * P:(k % 4 + 1) * P], xg[n % 2][:, k * P:(k + 1) * P],
                                            ident[:, :])
                    last.then_inc(xt_done, 1)
                if not free or 1 <= j <= E:
                    n = j - 1
                    pe.wait_ge(at_ready, at(b, q, 1, n + 1))
                    pe.wait_ge(w_dn[n % RING], at(b, q, 4, 16 * (n // RING + 1)))
                    if not free or n >= 1:
                        pe.wait_ge(yA, at(b, q, 1, n))
                        pe.wait_ge(yB, at(b, q, 1, n))
                    down(aT[n % 2], wdn[n % RING]).then_inc(dn_done, 1)

            with pe.Fori(0, n_pass) as b:
                for j in range(-3, 5):
                    step(b, None, j)
                with pe.Fori(0, Q_LOOP) as q:
                    for j in range(5, 5 + RING):
                        step(b, q, j)
                for j in range(E - 3, E + 1):
                    step(b, None, j)
                for i in range(2):
                    pe.wait_ge(scat[i], at(b, None, 8, 16 * E // 2))

            def h3_T(t):
                pe.wait_ge(f_h3, t + 1)
                for half in range(2):
                    transposes(T_H3 + 2 * t + half, blocks(h3[t % 2], half))

            h3_T(0)
            for t in range(NT):
                for i in range(2):
                    pe.wait_ge(tr_free[i], T_H3 // 2 + t + 1)
                for half in range(2):
                    w = W_GATE + half
                    pe.wait_ge(win_ready[w % 2], win_count(w))
                    if t >= 2:
                        pe.wait_ge(g_sig, 2 * (t - 2) + half + 1)
                    rhs = v2(win, win_at(w), KD, 512)
                    for k in range(KD):
                        last = pe.matmul(bank[2 * (t % 2) + half][:, :], hT[:, k, tok(t)], rhs[:, k, :],
                                         start=(k == 0), stop=(k == KD - 1))
                    last.then_inc(g_done, 1)
                    if half == 0 and t + 1 < NT:
                        h3_T(t + 1)


_INS = ["x", "p", "positions", "g_mix", "w_in", "sgu_ln_g", "sgu_ln_b", "sgu_w", "sgu_b", "mla_g_qa", "mla_w_qb",
        "mla_g_kva", "mla_w_kvb", "qk_g_q_nope", "qk_g_k_nope", "qk_g_q_rope", "qk_g_k_rope", "w_o", "g_ffn",
        "w_router", "b_router", "w_exp_gate", "w_exp_up", "w_exp_down", "w_sh_gate", "w_sh_up", "w_sh_down",
        "g_ple_in", "w_ple_gate", "w_ple_proj", "g_ple_out"]


def kernel(**inputs):
    import concourse.bacc as bacc
    from concourse.bass_utils import run_bass_kernel_spmd

    nc = bacc.Bacc("TRN2", target_bir_lowering=False, num_devices=1)
    arrays, aps = {}, {}
    for name in _INS:
        v = np.ascontiguousarray(inputs[name])
        arrays["in_" + name] = v
        aps[name] = nc.dram_tensor("in_" + name, v.shape, mybir.dt.from_np(v.dtype), kind="ExternalInput").ap()
    out = nc.dram_tensor("out_0", arrays["in_x"].shape, mybir.dt.float32, kind="ExternalOutput").ap()
    hybrid_block_kernel(nc, aps, out)
    r = run_bass_kernel_spmd(nc, [arrays], core_ids=[0])
    return r.results[0]["out_0"]
```

```python
import concourse.bass as bass
from concourse import mybir
from contextlib import ExitStack
import numpy as np


def hybrid_block_kernel(nc, a, out):
    F32, F32R, BF16 = mybir.dt.float32, mybir.dt.float32r, mybir.dt.bfloat16
    I32, U32 = mybir.dt.int32, mybir.dt.uint32
    ALU, ACT, AX = mybir.AluOpType, mybir.ActivationFunctionType, mybir.AxisListType

    P = 128
    SEQ, D = a["x"].shape[1], a["x"].shape[2]
    NT, KD = SEQ // P, D // P
    PLE = a["p"].shape[3]
    G = a["sgu_w"].shape[1]
    QL, KVL = a["mla_w_qb"].shape[1], a["mla_w_kvb"].shape[1]
    NOPE, ROPE = a["qk_g_q_nope"].shape[1], a["qk_g_q_rope"].shape[1]
    H = a["mla_w_qb"].shape[2] // (NOPE + ROPE)
    QK, VD, HR = NOPE + ROPE, P, ROPE // 2
    E = a["w_router"].shape[2]
    FF = a["w_exp_gate"].shape[3]
    NG, TOPG, TOPK = 8, 4, 8
    EG = E // NG
    SCALE, ROUTED = float(QK) ** -0.5, 2.5
    EPS, LN_EPS, THETA = 1e-6, 1e-5, 10000.0
    BIG = 1e30
    LAT = QL + KVL + ROPE
    KQ, KKV, KF = QL // P, KVL // P, FF // P
    OFF_U, OFF_V, OFF_LAT, OFF_GA, OFF_GB = 0, D, 2 * D, 2 * D + LAT, 3 * D + LAT
    NA = H * NT
    RING = 4
    WGU, WDN = KD * 2 * FF, KF * D
    WEXP = WGU + WDN
    NS = 104
    NPASS_MAX = -(-SEQ // NS)
    Q_LOOP = (E - 8) // RING

    h2_dram = nc.dram_tensor("h2_rows", (SEQ, D), F32, kind="Internal").ap()
    pn_dram = nc.dram_tensor("ple_rows", (SEQ, D), F32, kind="Internal").ap()
    y_dram = nc.dram_tensor("expert_rows", (SEQ * TOPK, D), F32, kind="Internal").ap()

    ctx = ExitStack()
    with ctx:
        def sb(name, width, dt=F32):
            return ctx.enter_context(nc.sbuf_tensor(name, [P, width], dt))

        def sb2(name, width):
            with nc.sbuf_tensor(name + "_r", [P, width], F32R) as alias:
                pass
            t = sb(name, width)
            return t, alias

        def sem(name):
            return ctx.enter_context(nc.semaphore(name))

        def v2(t, at, x, y):
            return t[:, at:at + x * y].rearrange("p (x y) -> p x y", x=x)

        def v3(t, at, x, y, z):
            return t[:, at:at + x * y * z].rearrange("p (x y z) -> p x y z", x=x, y=y)

        xr_ = sb("resid", NT * D)
        x = v2(xr_, 0, NT, D)
        hT_, hT_r_ = sb2("hT", KD * SEQ)
        hT = v2(hT_, 0, KD, SEQ)
        V = v3(hT_, 0, NT, H, VD)
        hT_hi = v2(hT_r_, 0, KD, SEQ)
        win, win_r = sb2("win", 2 * 4096)
        ya_ = sb("ya", NT * D)
        ya = v2(ya_, 0, NT, D)
        xg = [ya_[:, i * D:(i + 1) * D] for i in range(2)]
        yo = [ya_[:, (2 + i) * D:(3 + i) * D] for i in range(2)]
        arena, arena_r = sb2("arena", RING * WEXP)

        base = 0
        def take(n):
            nonlocal base
            base += n
            return base - n
        o_qT = take(H * SEQ)
        o_kT = take(H * SEQ)
        o_sigb = take(NT * D)
        o_qrT = take(H // 2 * SEQ)
        o_qc = take(2 * NT * 2 * QK)
        o_kpeT = take(SEQ)
        o_otmp = take(512)
        o_tab = take(2 * 4 * NT * HR)
        o_sq = take(NT * 2 * QK)
        take(512)
        o_latT = take((KQ + KKV) * SEQ)
        assert base <= RING * WEXP
        qT, kT = v2(arena, o_qT, H, SEQ), v2(arena, o_kT, H, SEQ)
        vbuf = v2(arena, o_qT, NT, D)
        whi_r = v2(arena_r, o_kT, KD, 512)
        hT_lo = [(4, 6, v2(arena_r, o_kpeT, 2, SEQ)), (0, 4, v2(arena_r, o_latT, 4, SEQ)),
                 (6, 8, v2(arena_r, o_latT + 4 * SEQ, 2, SEQ))]
        assert o_latT + 6 * SEQ <= RING * WEXP
        sigb = v2(arena, o_sigb, NT, D)
        hst = [arena[:, o_sigb + i * D:o_sigb + (i + 1) * D] for i in range(4)]
        qrT = v2(arena, o_qrT, H // 2, SEQ)
        wsp = v2(arena, o_qrT, G, P)
        wspT = v2(arena, o_qrT + G * P, G, P)
        latT_hi = v2(arena_r, o_latT, KQ + KKV, SEQ)
        lat = v2(arena, o_qc, NT, LAT)
        qc = [v3(arena, o_qc + i * NT * 2 * QK, NT, 2, QK) for i in range(2)]
        sqc = v3(arena, o_sq, NT, 2, QK)
        probs = [arena[:, o_qc + i * SEQ:o_qc + (i + 1) * SEQ] for i in range(2)]
        probsT = [arena[:, o_qc + (2 + i) * SEQ:o_qc + (3 + i) * SEQ] for i in range(2)]
        otmp = [arena[:, o_otmp + i * P:o_otmp + (i + 1) * P] for i in range(2)]
        lng, lnb = arena[:, o_sq:o_sq + D], arena[:, o_sq + D:o_sq + 2 * D]
        kpeT = arena[:, o_kpeT:o_kpeT + SEQ]
        tabq = [v2(arena, o_tab + i * NT * HR, NT, HR) for i in range(4)]
        tabk = [v2(arena, o_tab + (4 + i) * NT * HR, NT, HR) for i in range(4)]
        wpj = v2(arena, 0, PLE // P, D)
        pT = v2(arena, PLE // P * D, PLE // P, SEQ)
        o_psq = PLE // P * (D + SEQ)
        mT = [[v2(arena_r, WEXP + (2 * part + i) * D, KD, P) for i in range(2)] for part in range(2)]
        z2 = 2 * WEXP
        gffn, gpo = arena[:, z2:z2 + D], arena[:, z2 + D:z2 + 2 * D]
        h2s = [arena[:, z2 + (2 + i) * D:z2 + (3 + i) * D] for i in range(4)]
        wgu = [arena[:, r * WEXP:r * WEXP + WGU].rearrange("p (g k f) -> p k g f", g=2, k=KD)
               for r in range(RING)]
        wdn = [v2(arena, r * WEXP + WGU, KF, D) for r in range(RING)]
        wdn_lo = [v2(arena_r, r * WEXP + WGU, KF, D) for r in range(RING)]
        wdn_hi = [v2(hT_r_, i * WDN, KF, D) for i in range(2)]
        YT = TOPK * D
        yt = [arena[:, (t % 2) * YT:(t % 2 + 1) * YT] for t in range(NT)]
        g_hi = [v2(arena_r, 2 * YT + c * 4096, KD, 512) for c in range(2)]
        h3T = [[v2(hT_r_, (2 * part + i) * D, KD, P) for i in range(2)] for part in range(2)]

        work, work_r = sb2("work", 3328)
        wo_at = [(arena_r, 3 * WEXP + i * 512) for i in range(WEXP // 512)] + [(work_r, D + i * 512) for i in range(4)]
        wo_hi = [[t_[:, o:o + 512] for t_, o in wo_at[c * KD:(c + 1) * KD]] for c in range(2)]
        S_all = work[:, 0:SEQ].bitcast(BF16)
        S_ = [S_all[:, i * SEQ:(i + 1) * SEQ].rearrange("p (t q) -> p t q", t=NT)
              for i in range(2)]
        xgT = v2(work, D, KD, P)
        sg = work[:, 2 * D:2 * D + FF]
        a_ = [v2(work, 2 * D + FF * (1 + i), KF, P) for i in range(2)]
        aT = [v2(work, 2 * D + FF * (3 + i), KF, P) for i in range(2)]
        aT_hi = [v2(work_r, 2 * D + FF * (3 + i), KF, P) for i in range(2)]
        aT_lo = [v2(work_r, SEQ + FF * i, KF, P) for i in range(2)]
        pbuf = v2(work, 0, NT, PLE)
        rt = [v3(work, 2 * D + i * 256, NT, 2, HR) for i in range(2)]
        qrot = [v3(work, i * 512, NT, 2, ROPE) for i in range(2)]
        kprot = v3(work, 512, NT, 2, ROPE)
        latT_lo = [hT_r_[:, k * SEQ:(k + 1) * SEQ] for k in range(KQ)] + [work_r[:, D + k * SEQ:D + (k + 1) * SEQ] for k in range(KKV)]
        ang = [v2(work, D + i * P, NT, HR) for i in range(6)]
        h3 = [work[:, i * D:(i + 1) * D] for i in range(2)]
        gt = work[:, 2 * D:3 * D]

        ident, tri, ones = sb("ident", P), sb("tri", P), sb("ones", P)
        identb, negmask = sb("identb", P, BF16), sb("negmask", P, BF16)
        iota = sb("iota", NPASS_MAX * NS + P)
        R = sb("R", E * NT * 9, BF16)
        Rv = R[:, :].rearrange("p (e t c) -> p e t c", e=E, t=NT)
        rank_ = sb("rank", E * NT)
        rank = v2(rank_, 0, E, NT)
        wr = sb("wr", KD * E)
        brt = sb("brt", E)
        sm = sb("small", 208)
        smi = sb("smalli", 8, I32)
        NSMALL = 4
        gidx = [sb(f"gidx{i}", 1, U32) for i in range(4)]
        sidx = [sb(f"sidx{i}", 1, U32) for i in range(2)]
        slots = [sm[:, 180 + 3 * i:183 + 3 * i] for i in range(4)]
        wt = [z[:, 2:3] for z in slots]
        rows = sb("rows", P)
        ROWS = [("positions", NT), ("g_mix", KD), ("g_ple_in", KD), ("sgu_b", G), ("mla_g_qa", KQ),
                ("mla_g_kva", KKV), ("qk_g_q_nope", 1), ("qk_g_k_nope", 1)]
        NROW = sum(n for _, n in ROWS)
        col = {}
        for name, n in ROWS:
            first = sum(len_ for _, len_ in ROWS[:len(col)])
            col[name] = sm[:, first:first + n]
        posf, gmix, gple, bsp = col["positions"], col["g_mix"], col["g_ple_in"], col["sgu_b"]
        gqa, gkva, gqn, gkn = col["mla_g_qa"], col["mla_g_kva"], col["qk_g_q_nope"], col["qk_g_k_nope"]
        gqk = sm[:, 35:36]
        assert NROW <= 35
        addc = sm[:, 36:38]
        st = [sm[:, 44 + 4 * i:48 + 4 * i] for i in range(8)]
        ssl, msl = sm[:, 76:88], sm[:, 88:100]
        bst = [sm[:, 100 + 12 * i:112 + 12 * i] for i in range(2)]
        mv = v2(sm, 124, NT, 2)
        ssq, msq = sm[:, 132:148], sm[:, 148:164]
        nm, rs, rinv = sm[:, 164:168], sm[:, 168:172], sm[:, 172:176]
        pos_i = sb("pos_i", P, I32)[0:NT, :]
        nb_i = smi[0:1, 6:7]
        gqr, gkr = sb("gqr", ROPE), sb("gkr", ROPE)
        invf = iota[:, 0:HR]
        rt_sc = v2(work, D, NT, E)
        rt_sel = v2(work, D + 256, NT, E)
        rt_rep = v2(work, D + 512, NT, E)
        rt_M = v2(work, D + 768, NT, E)
        rt_gt = work[:, 0:256].rearrange("p (t g h) -> p t g h", t=NT, g=NG)
        rt_eq = work[:, 256:512].rearrange("p (t g h) -> p t g h", t=NT, g=NG)
        g8 = v3(work, 512, NT, NG, 8)
        gs, gr, gm, t8 = (v2(work, 768 + 32 * i, NT, 8) for i in range(4))
        rden = work[:, 896:896 + NT]
        low = v2(work, 900, 8, 8)
        MT = work[0:E, 0:SEQ]
        cmp_ = work[:, 964:964 + NPASS_MAX]
        addt = sm[:, 176:180]
        pcol = sm[:, 192:193]

        bank = [ctx.enter_context(nc.psum_tensor(f"bank{i}", [P, 512], F32)) for i in range(8)]

        ld_x = [sem(f"x_loaded{t}") for t in range(NT)]
        ld_small, ld_pos, ld_wsp, ld_ln = sem("small_loaded"), sem("pos_loaded"), sem("wsp_loaded"), sem("ln_loaded")
        ld_late = sem("late_loaded")
        ld_p, ld_pj, wo_hi_r, wo_lo_r, mT_hi = sem("p_loaded"), sem("proj_loaded"), sem("wo_hi_ready"), sem("wo_lo_ready"), sem("mT_hi_ready")
        win_ready = [sem(f"win_ready{i}") for i in range(2)]
        const_pool = sem("const_pool")
        dve_step, pool_step = sem("dve_step"), sem("pool_step")
        rms_sq, rms_ms, rms_rt, rms_x = sem("rms_sq"), sem("rms_ms"), sem("rms_rt"), sem("rms_x")
        tr_done, tr_free = sem("tr_done"), [sem(f"tr_free{i}") for i in range(2)]
        pj_done, pj_free = sem("pj_done"), [sem(f"pj_free{i}") for i in range(4)]
        lat_sq, lat_ms, lat_rt, lat_n = sem("lat_sq"), sem("lat_ms"), sem("lat_rt"), sem("lat_n")
        ang_r, sincos, tables, kp_rot = sem("ang_r"), sem("sincos"), sem("tables"), sem("kp_rot")
        rows_ready, cols_done, cols_ready = sem("rows_ready"), sem("cols_done"), sem("cols_ready")
        hi_ready, lo_ready, whi_used, hT_hi_ready = sem("hi_ready"), sem("lo_ready"), sem("whi_used"), sem("hT_hi_ready")
        ga_sig = sem("gate_a_sigmoid")
        latT_hi_r, qkv_hi, qkv_lo = sem("latT_hi_ready"), sem("qkv_hi_ready"), sem("qkv_lo_ready")
        wsp_m = sem("wsp_masked")
        ln_ms, ln_rt, ln_x, ln_v = sem("ln_ms"), sem("ln_rt"), sem("ln_x"), sem("ln_v")
        qk_ms, qk_rt, qk_n, q_rot = sem("qk_ms"), sem("qk_rt"), sem("qk_n"), sem("q_rot")
        s_done, nm_ready, exp_done = sem("s_done"), sem("nm_ready"), sem("exp_done")
        pt_done, pt_ready, pv_done = sem("pt_done"), sem("pt_ready"), sem("pv_done")
        o_ready, ya_add = sem("o_ready"), sem("ya_add")
        ple_ms, ple_rt, ple_n = sem("ple_ms"), sem("ple_rt"), sem("ple_n")
        h2_n, h2_st, pn_st = sem("h2_n"), sem("h2_stored"), sem("pn_stored")
        rt_logit, rt_score, m_ready = sem("rt_logit"), sem("rt_score"), sem("m_ready")
        rk_done, ks_done, rank_ready, R_ready, nb_ready = sem("rk_done"), sem("ks_done"), sem("rank_ready"), sem("R_ready"), sem("nb_ready")
        sh_gu, sh_silu, sh_a, sh_at, sh_aT, sh_dn, sh_y = (sem(f"sh_{n}") for n in ("gu", "silu", "a", "at", "aT", "dn", "y"))
        held = sem("held")
        xg_zero = sem("xg_zero")
        w_gu = [sem(f"w_gu{r}") for r in range(RING)]
        w_dn = [sem(f"w_dn{r}") for r in range(RING)]
        sel_ready, tab_done, tab_sum, idx_ready = sem("sel_ready"), sem("tab_done"), sem("tab_sum"), sem("idx_ready")
        gath = [sem(f"gathered{i}") for i in range(2)]
        scat = [sem(f"scattered{i}") for i in range(2)]
        xt_done, xta, xtb = sem("xt_done"), sem("xt_evac_a"), sem("xt_evac_b")
        gu_done, silu_done, a_ready, at_done, at_hi, at_ready = sem("gu_done"), sem("silu_done"), sem("a_ready"), sem("at_done"), sem("at_hi"), sem("at_ready")
        dn_hi, dn_lo = sem("down_hi_ready"), sem("down_lo_ready")
        dn_done, yA, yB = sem("dn_done"), sem("y_evac_a"), sem("y_evac_b")
        yt_ld = [sem(f"yt_loaded{n}") for n in range(2 * NT)]
        pn_ld, yt_add, yt_red = [sem(f"pn_loaded{t}") for t in range(NT)], sem("yt_add"), sem("yt_red")
        f_sq, f_ms, f_rt, f_inv = sem("f_sq"), sem("f_ms"), sem("f_rt"), sem("f_inv")
        g_hi_r, g_lo_r, h3_hi = sem("gate_hi_ready"), sem("gate_lo_ready"), sem("h3_hi_ready")
        g_done, g_sig, g_x, out_st = sem("g_done"), sem("g_sig"), sem("g_x"), sem("out_stored")

        T_H, T_WSP, T_LAT, T_KPE, T_Q = 0, 2 * NT, 2 * NT + 2, 2 * NT + 2 + KQ + KKV, 2 * NT + 3 + KQ + KKV
        T_K = T_Q + 3 * (H // 2)
        T_M = T_K + H
        T_H2 = T_M + 2 * NT
        T_P = T_H2 + 2 * (NT - 1)
        T_MT = T_P + PLE // P + 2
        T_H3 = T_MT + 2
        assert T_H3 % 2 == 0 and T_H2 % 2 == 0
        P_SGU, P_Q, P_KV, P_WO, P_PLE = 40, 48, 64, 80, 88
        W_Q, W_KV, W_WO, W_SHDN, W_SHGU, W_GATE = 10, 14, 18, 20, 21, 22

        def chunk_width(w):
            return (QL, KVL + ROPE)[w] if w < 2 else 512

        def win_at(w):
            return (w % 2) * 4096

        def qkv_width(s):
            return KQ * 2 * QK if s < 4 else KKV * 512

        def qkv_chunk(t_, s, part):
            first = win_at(W_Q + s) + part * 2048
            return t_[:, first:first + qkv_width(s)]

        def last_P(w):
            if w < W_Q:
                return 4 * (w + 1)
            if w < W_KV:
                return P_Q + 4 * (w - W_Q + 1)
            if w < W_WO:
                return P_KV + 4 * (w - W_KV + 1)
            return P_PLE

        def win_count(w):
            return 16 * (w // 2 + 1) + (16 if w % 2 and w >= W_SHGU else 0)

        def T_h2(t):
            return T_H2 + 2 * t if t < NT - 1 else T_P + PLE // P

        def step_T(s):
            return T_Q + 3 * (s + 1) if s < 4 else T_K + 2 * (s - 3)

        def at(b, q, per_expert, c):
            val = b * int(E * per_expert) + c if b is not None else c
            return val if q is None else q * int(RING * per_expert) + val

        def ahead(b, c):
            return c if b is None else b * E + (E + c)

        w_in = a["w_in"][0]

        def bc(row, n):
            return row.rearrange("(o n) -> o n", o=1).broadcast_to([P, n])

        block = ctx.enter_context(nc.Block())

        @block.sync
        def _(sp):
            for t in range(NT):
                sp.dma_start(x[:, t, :], a["x"][0, t * P:(t + 1) * P, :]).then_inc(ld_x[t], 16)

            def free(w):
                if w < W_SHDN:
                    sp.wait_ge(pj_done, last_P(w))
                else:
                    sp.wait_ge(sh_gu if w == W_SHGU else sh_dn, NT)

            def chunk(w, dst, src):
                if w >= 2:
                    free(w - 2)
                sp.dma_start(dst, src).then_inc(win_ready[w % 2], 16)

            def small_loads():
                sp.dma_start(wsp, a["sgu_w"][0].rearrange("g i j -> i g j")).then_inc(ld_wsp, 16)
                small(gqr[:, :], bc(a["qk_g_q_rope"][0], ROPE))
                small(gkr[:, :], bc(a["qk_g_k_rope"][0], ROPE))
                small(brt[:, :], bc(a["b_router"][0], E))
                small(wr[:, :], a["w_router"][0].rearrange("(p k) e -> p (k e)", p=P))
                sp.dma_start(lng, bc(a["sgu_ln_g"][0], D)).then_inc(ld_ln, 16)
                sp.dma_start(lnb, bc(a["sgu_ln_b"][0], D)).then_inc(ld_ln, 16)

            cols = [(OFF_LAT, QL), (OFF_LAT + QL, KVL + ROPE)]
            for off in (OFF_V, OFF_U, OFF_GA, OFF_GB):
                cols += [(off, 512), (off + 512, 512)]
            def small(dst, src):
                sp.dma_start(dst, src).then_inc(ld_small, 16)

            sp.dma_start(pos_i, a["positions"][0].rearrange("(t p) -> t p", p=P)).then_inc(ld_pos, 16)
            first = NT
            for name, n in ROWS[1:]:
                src = a[name][0] if name == "sgu_b" else a[name][0].rearrange("(k p) -> k p", p=P)
                sp.dma_start(rows[first:first + n, :], src).then_inc(ld_pos, 16)
                first += n
            for w, (off, n) in enumerate(cols):
                if w == 2:
                    small_loads()
                chunk(w, v2(win, win_at(w), KD, n),
                      w_in[:, off:off + n].rearrange("(k p) n -> p k n", p=P))
            for c in range(4):
                w = W_Q + c
                chunk(w, v2(win, win_at(w), KQ, 2 * QK),
                      a["mla_w_qb"][0][:, c * 2 * QK:(c + 1) * 2 * QK].rearrange("(k p) n -> p k n", p=P))
            for c in range(4):
                w = W_KV + c
                chunk(w, v2(win, win_at(w), KKV, 512),
                      a["mla_w_kvb"][0][:, c * 512:(c + 1) * 512].rearrange("(k p) n -> p k n", p=P))
            for c in range(2):
                w = W_WO + c
                chunk(w, v2(win, win_at(w), KD, 512),
                      a["w_o"][0][:, c * 512:(c + 1) * 512].rearrange("(k p) n -> p k n", p=P))

            def expert(e, r, one=True):
                for g, name in enumerate(("w_exp_gate", "w_exp_up")):
                    src = a[name][0][e] if one else a[name][0][bass.ds(e, 1)].rearrange("o d f -> (o d) f")
                    sp.dma_start(arena[:, r * WEXP + g * KD * FF:r * WEXP + (g + 1) * KD * FF],
                                 src.rearrange("(p k) f -> p (k f)", p=P)).then_inc(w_gu[r], 16)
                src = a["w_exp_down"][0][e] if one else a["w_exp_down"][0][bass.ds(e, 1)].rearrange("o d f -> (o d) f")
                sp.dma_start(arena[:, r * WEXP + WGU:(r + 1) * WEXP],
                             src.rearrange("(p k) f -> p (k f)", p=P)).then_inc(w_dn[r], 16)

            sp.wait_ge(ya_add, NA)
            sp.wait_ge(kp_rot, 1)
            sp.dma_start(gffn, bc(a["g_ffn"][0], D)).then_inc(ld_late, 16)
            sp.dma_start(gpo, bc(a["g_ple_out"][0], D)).then_inc(ld_late, 16)
            sp.dma_start(pbuf, a["p"][0, 0].rearrange("(t q) n -> q t n", q=P)).then_inc(ld_p, 16)
            sp.dma_start(wpj, a["w_ple_proj"][0].rearrange("(k p) n -> p k n", p=P)).then_inc(ld_pj, 16)
            free(W_SHGU - 2)
            for g, name in enumerate(("w_sh_gate", "w_sh_up")):
                at0 = win_at(W_SHGU) + g * KD * FF
                sp.dma_start(win[:, at0:at0 + KD * FF],
                             a[name][0].rearrange("(p k) f -> p (k f)", p=P)).then_inc(win_ready[1], 16)
            chunk(W_SHDN, win[:, win_at(W_SHDN):win_at(W_SHDN) + WDN],
                  a["w_sh_down"][0].rearrange("(p k) f -> p (k f)", p=P))
            expert(1, 1)
            for i in range(4):
                sp.wait_ge(pj_free[i], P_PLE // 4 + 2)
            expert(0, 0)
            expert(3, 3)
            sp.wait_ge(h2_st, 16 * NT)
            sp.wait_ge(tr_done, T_MT)
            sp.wait_ge(ple_n, NT)
            expert(2, 2)
            for c in range(2):
                chunk(W_GATE + c, v2(win, win_at(W_GATE + c), KD, 512),
                      a["w_ple_gate"][0][:, c * 512:(c + 1) * 512].rearrange("(k p) n -> p k n", p=P))
            with sp.Fori(1, E // RING) as q:
                for r in range(RING):
                    sp.wait_ge(dn_done, q * RING + (r - RING + 1))
                    expert(q * RING + r, r, one=False)
            sp.wait_ge(nb_ready, 1)
            n_pass = sp.value_load(nb_i, min_val=1, max_val=NPASS_MAX)
            with sp.If(n_pass > 1):
                with sp.Fori(1, n_pass) as b:
                    with sp.Fori(0, E // RING) as q:
                        for r in range(RING):
                            sp.wait_ge(dn_done, b * E + q * RING + (r - RING + 1))
                            expert(q * RING + r, r, one=False)
            for i in range(2):
                sp.wait_ge(scat[i], n_pass * (16 * E // 2))
            for t in range(NT):
                if t >= 2:
                    sp.wait_ge(yt_red, t - 1)
                rows_of_tile = y_dram[t * P * TOPK:(t + 1) * P * TOPK, :].rearrange("(q s) n -> q (s n)", q=P)
                for i in range(2):
                    half = slice(i * YT // 2, (i + 1) * YT // 2)
                    sp.dma_start(yt[t][:, half], rows_of_tile[:, half]).then_inc(yt_ld[2 * t + i], 16)
                if t == 1:
                    for i in range(2):
                        sp.wait_ge(gath[i], n_pass * (16 * E // 2) + 16)
                for u in ((), (0,), (1,), (2, 3))[t]:
                    sp.dma_start(ya[:, u, :], pn_dram[u * P:(u + 1) * P, :]).then_inc(pn_ld[u], 16)
            for t in range(NT):
                for i in range(2):
                    sl = slice(i * 512, (i + 1) * 512)
                    sp.wait_ge(g_x, 2 * t + i + 1)
                    sp.dma_start(out[0, t * P:(t + 1) * P, sl], x[:, t, sl]).then_inc(out_st, 16)
            sp.wait_ge(out_st, 32 * NT)

        @block.gpsimd
        def _(pool):
            steps = [0]

            def link(ins):
                steps[0] += 1
                ins.then_inc(pool_step, 1)
                pool.wait_ge(pool_step, steps[0])

            pool.memset(ident[:, :], 0.0)
            pool.memset(identb[:, :], 0.0)
            pool.memset(negmask[:, :], 0.0)
            pool.memset(tri[:, :], 1.0)
            link(pool.memset(ones[:, :], 1.0))
            for m in (ident, identb):
                pool.affine_select(out=m[:, :], in_=m[:, :], compare_op=ALU.not_equal, fill=1.0, base=0,
                                   pattern=[[-1, P]], channel_multiplier=1)
            pool.affine_select(out=negmask[:, :], in_=negmask[:, :], compare_op=ALU.is_ge, fill=-BIG, base=0,
                               pattern=[[-1, P]], channel_multiplier=1)
            pool.affine_select(out=tri[:, :], in_=tri[:, :], compare_op=ALU.is_ge, fill=0.0, base=-1,
                               pattern=[[1, P]], channel_multiplier=-1).then_inc(const_pool, 1)
            inv_freq = 1.0 / np.power(THETA, np.arange(HR) / HR).astype(np.float32)
            for j in range(HR):
                last = pool.memset(invf[:, j:j + 1], float(inv_freq[j]))
            last.then_inc(const_pool, 1)
            pool.wait_ge(ld_wsp, 16)
            pool.affine_select(out=wsp, in_=wsp, compare_op=ALU.is_ge, fill=0.0, base=0,
                               pattern=[[0, G], [-1, P]], channel_multiplier=1).then_inc(wsp_m, 1)
            pool.wait_ge(ld_small, 16 * NSMALL)
            link(pool.tensor_scalar(gqr[:, :], gqr[:, :], SCALE, None, ALU.mult))
            pool.wait_ge(sincos, 2)
            for tab, g in ((tabq, gqr), (tabk, gkr)):
                for i, (trig, half) in enumerate(((ang[4], 0), (ang[5], 1), (ang[4], 1), (ang[5], 0))):
                    gain = g[:, half * HR:(half + 1) * HR].unsqueeze(1).broadcast_to([P, NT, HR])
                    last = pool.tensor_tensor(tab[i], trig, gain, ALU.mult)
            link(last)

            pool.memset(addc[:, 0:1], 4096.0)
            pool.memset(addc[:, 1:2], float(4096 * TOPK))
            pool.iota(pcol, pattern=[[0, 1]], base=0, channel_multiplier=1,
                      allow_small_or_imprecise_dtypes=True)
            pool.iota(addt, pattern=[[P, NT]], base=-4096, channel_multiplier=0,
                      allow_small_or_imprecise_dtypes=True)
            pool.iota(iota[:, :], pattern=[[1, NPASS_MAX * NS + P]], base=0, channel_multiplier=0,
                      allow_small_or_imprecise_dtypes=True).then_inc(const_pool, 1)

            def rotate(src1, src2, tab, dst1, dst2, dup):
                def full(z):
                    return z.unsqueeze(2).broadcast_to([P, NT, 2, HR]) if len(z.shape) == 3 else z
                t1, t2 = rt
                for d, s1, s2, i1, i2, op in ((dst1, src1, src2, 0, 1, ALU.subtract),
                                              (dst2, src2, src1, 2, 3, ALU.add)):
                    pool.tensor_tensor(t1, full(s1), full(tab[i1]), ALU.mult)
                    link(pool.tensor_tensor(t2, full(s2), full(tab[i2]), ALU.mult))
                    last = pool.tensor_tensor(d, t1, t2, op)
                    if d is dst1:
                        link(last)
                return last

            pool.wait_ge(lat_n, 3)
            kr = lat[:, :, QL + KVL:LAT]
            rotate(kr[:, :, 0:HR], kr[:, :, HR:ROPE], tabk,
                   kprot[:, :, :, 0:HR], kprot[:, :, :, HR:ROPE], True).then_inc(kp_rot, 1)
            pool.wait_ge(ld_ln, 32)
            for t in range(NT):
                pool.wait_ge(ln_x, t + 1)
                link(pool.tensor_tensor(vbuf[:, t, :], vbuf[:, t, :], lng, ALU.mult))
                pool.tensor_tensor(vbuf[:, t, :], vbuf[:, t, :], lnb, ALU.add).then_inc(ln_v, 1)
            for c in range(4):
                pool.wait_ge(qk_n, c + 1)
                if c == 0:
                    pool.wait_ge(kp_rot, 1)
                else:
                    pool.wait_ge(tr_done, T_Q if c == 1 else step_T(c - 2))
                    pool.wait_ge(q_rot, c)
                z = qc[c % 2]
                rotate(z[:, :, :, NOPE:NOPE + HR], z[:, :, :, NOPE + HR:QK], tabq,
                       qrot[c % 2][:, :, :, 0:HR], qrot[c % 2][:, :, :, HR:ROPE], False).then_inc(q_rot, 1)
            for i in range(4):
                pool.wait_ge(pj_free[i], P_Q // 4)
            for n in range(NA):
                h, i = divmod(n, NT)
                pool.wait_ge(o_ready, n + 1)
                dst = ya[:, i, h * VD:(h + 1) * VD]
                pool.tensor_tensor(dst, dst, otmp[n % 2], ALU.add).then_inc(ya_add, 1)
                (c, k), low_part = divmod(n // 2, KD), n % 2
                if n == 0:
                    pool.wait_ge(tr_done, T_K)
                if k == 0 and not low_part:
                    pool.wait_ge(win_ready[c], win_count(W_WO + c))
                w_ = v2(win, win_at(c), KD, 512)[:, k, :]
                if not low_part:
                    pool.tensor_copy(wo_hi[c][k], w_).then_inc(wo_hi_r, 1)
                else:
                    pool.wait_ge(wo_hi_r, n // 2 + 1)
                    pool.tensor_tensor(v2(win_r, win_at(c), KD, 512)[:, k, :], w_, wo_hi[c][k].bitcast(F32),
                                       ALU.subtract).then_inc(wo_lo_r, 1)
            for t in range(NT):
                pool.wait_ge(ple_n, t + 1)
                pool.dma_start(pn_dram[t * P:(t + 1) * P, :], ya[:, t, :]).then_inc(pn_st, 16)
            pool.wait_ge(pn_st, 16 * NT)
            pool.memset(ya_[:, 0:2 * D], 0.0).then_inc(xg_zero, 1)
            pool.wait_ge(h2_st, 16 * NT)
            pool.wait_ge(nb_ready, 1)
            pool.wait_ge(xg_zero, 1)

            last_token, last_row = pool.to_reg(SEQ - 1), pool.to_reg(SEQ * TOPK - 1)

            def gather_rows(j):
                pool.sem_inc(held, 1)
                pool.indirect_dma_start(xg[j % 2][0:NS], None, h2_dram,
                                        bass.IndirectOffsetOnAxis(gidx[j % 4][0:NS, 0:1], 0),
                                        bounds_check=last_token, oob_is_err=False).then_inc(gath[j % 2], 16)

            def first_gathers(b):
                for j in range(2):
                    pool.wait_ge(idx_ready, ahead(b, j + 1))
                    gather_rows(j)

            def gather(b, q, j):
                pool.wait_ge(idx_ready, at(b, q, 1, j + 1))
                if q is not None or j >= 2:
                    pool.wait_ge(xt_done, at(b, q, 1, j - 1))
                gather_rows(j)

            def scatter(b, q, j):
                pool.wait_ge(yA, at(b, q, 1, j + 1))
                pool.wait_ge(yB, at(b, q, 1, j + 1))
                pool.sem_inc(held, 1)
                pool.indirect_dma_start(y_dram, bass.IndirectOffsetOnAxis(sidx[j % 2][0:NS, 0:1], 0),
                                        yo[j % 2][0:NS], None,
                                        bounds_check=last_row, oob_is_err=False).then_inc(scat[j % 2], 16)

            def step(b, q, j):
                if q is not None or 1 <= j <= E:
                    scatter(b, q, j - 1)
                if q is not None or j + 3 < E:
                    gather(b, q, j + 3)

            first_gathers(None)
            n_pass = pool.value_load(nb_i, min_val=1, max_val=NPASS_MAX)
            with pool.Fori(0, n_pass) as b:
                for j in range(-1, 5):
                    step(b, None, j)
                with pool.Fori(0, Q_LOOP) as q:
                    for j in range(5, 5 + RING):
                        step(b, q, j)
                for j in range(E - 3, E + 1):
                    step(b, None, j)
                for i in range(2):
                    pool.wait_ge(scat[i], at(b, None, 8, 16 * E // 2))
                first_gathers(b)
            for t in range(NT):
                z = yt[t]
                for i, pairs in enumerate((((2, 3), (2, 1)), ((6, 7),))):
                    pool.wait_ge(yt_ld[2 * t + i], 16)
                    for m, (to, from_) in enumerate(pairs):
                        dst = z[:, to * D:(to + 1) * D]
                        last = pool.tensor_tensor(dst, dst, z[:, from_ * D:(from_ + 1) * D], ALU.add)
                        if m + 1 < len(pairs):
                            link(last)
                    last.then_inc(yt_add, 1)

        @block.scalar
        def _(act):
            def hT_evac(t):
                for T in (T_H + 2 * t, T_H + 2 * t + 1):
                    act.wait_ge(tr_done, T + 1)
                    act.activation(hT_hi[:, 4 * (T % 2):4 * (T % 2) + 4, t * P:(t + 1) * P],
                                   bank[4 + T % 2][:, :].rearrange("p (k q) -> p k q", k=4), ACT.Copy).then_inc(hT_hi_ready, 1)

            def split(w):
                n = chunk_width(w)
                act.wait_ge(win_ready[w % 2], win_count(w))
                for k in range(KD):
                    if w >= 1:
                        act.wait_ge(whi_used, KD * (w - 1) + k + 1)
                    act.activation(whi_r[:, k, 0:n], v2(win, win_at(w), KD, n)[:, k, :], ACT.Copy,
                                   scale=gmix[:, k:k + 1]).then_inc(hi_ready, 1)

            for t in range(NT):
                act.wait_ge(ld_x[t], 16)
                act.activation(hst[t], x[:, t, :], ACT.Square, accum_out=st[0][:, t:t + 1]).then_inc(rms_sq, 1)
                act.wait_ge(rms_ms, t + 1)
                act.activation(st[2][:, t:t + 1], st[1][:, t:t + 1], ACT.Sqrt).then_inc(rms_rt, 1)
                if t >= 1:
                    hT_evac(t - 1)
            act.wait_ge(cols_ready, 1)
            split(0)
            hT_evac(NT - 1)
            act.wait_ge(ang_r, 2)
            act.activation(ang[5], ang[1], ACT.Sin).then_inc(sincos, 1)
            act.activation(ang[4], ang[3], ACT.Sin).then_inc(sincos, 1)

            def evac(w, t):
                act.wait_ge(pj_done, 4 * w + t + 1)
                b_ = bank[t]
                half = slice((w % 2) * 512, (w % 2 + 1) * 512)
                if w == 0:
                    act.activation(lat[:, t, 0:QL], b_[:, 0:QL], ACT.Copy)
                    act.activation(trash(t * QL, QL), b_[:, 0:QL], ACT.Square,
                                   accum_out=ssl[:, t:t + 1]).then_inc(pj_free[t], 1)
                elif w == 1:
                    act.activation(lat[:, t, QL:LAT], b_[:, 0:KVL + ROPE], ACT.Copy)
                    act.activation(trash(NT * QL + t * KVL, KVL), b_[:, 0:KVL], ACT.Square,
                                   accum_out=ssl[:, NT + t:NT + t + 1])
                    act.activation(trash(NT * (QL + KVL) + t * ROPE, ROPE), b_[:, KVL:KVL + ROPE], ACT.Square,
                                   accum_out=ssl[:, 2 * NT + t:2 * NT + t + 1]).then_inc(pj_free[t], 1)
                elif w < 4:
                    act.activation(vbuf[:, t, half], b_[:, :], ACT.Gelu_apprx_tanh).then_inc(pj_free[t], 1)
                elif w < 6:
                    act.activation(ya[:, t, half], b_[:, :], ACT.Gelu_apprx_tanh).then_inc(pj_free[t], 1)
                elif w < 8:
                    act.activation(b_[:, :], b_[:, :], ACT.Sigmoid).then_inc(ga_sig, 1)
                else:
                    act.activation(sigb[:, t, half], b_[:, :], ACT.Sigmoid).then_inc(pj_free[t], 1)

            def trash(first, n):
                return arena[:, o_sigb + first:o_sigb + first + n]

            act.wait_ge(tr_done, T_WSP)
            for w in range(W_Q):
                for t in range(NT):
                    if t == NT - 1 and w + 1 < W_Q:
                        split(w + 1)
                    evac(w, t)
                    if w == 2 and t == 1:
                        act.wait_ge(lat_ms, 3)
                        act.activation(ssl, msl, ACT.Sqrt).then_inc(lat_rt, 1)
                    if w == 4 and t == 2:
                        act.wait_ge(ln_ms, NT)
                        act.activation(st[4], st[3], ACT.Sqrt).then_inc(ln_rt, 1)
            for i in range(2):
                T = T_WSP + i
                act.wait_ge(tr_done, T + 1)
                act.activation(wspT[:, 4 * i:4 * i + 4, :], bank[4 + T % 2][:, :].rearrange("p (g i) -> p g i", g=4),
                               ACT.Copy).then_inc(tr_free[T % 2], 1)
            for k in range(KQ + KKV + 1):
                T = T_LAT + k
                act.wait_ge(tr_done, T + 1)
                if k < KQ + KKV:
                    gain = gqa[:, k:k + 1] if k < KQ else gkva[:, k - KQ:k - KQ + 1]
                    act.activation(latT_hi[:, k, :], bank[4 + T % 2][:, :], ACT.Copy, scale=gain).then_inc(latT_hi_r, 1)
                else:
                    act.activation(kpeT, bank[4 + T % 2][:, :], ACT.Copy).then_inc(tr_free[T % 2], 1)
            def qkv_split(s):
                act.wait_ge(win_ready[(W_Q + s) % 2], win_count(W_Q + s))
                act.activation(qkv_chunk(win_r, s, 1), qkv_chunk(win, s, 0), ACT.Copy).then_inc(qkv_hi, 1)

            qkv_split(0)
            for s in range(9):
                if s < 8:
                    for t in range(NT):
                        n = P_Q + 4 * s + t
                        act.wait_ge(pj_done, n + 1)
                        if t == 0:
                            if s >= 1:
                                act.wait_ge(qk_ms, s)
                            if 2 <= s < 6:
                                act.wait_ge(tr_done, T_Q + 3 * (s - 2) + 2)
                                act.wait_ge(q_rot, s - 1)
                            elif s >= 6:
                                act.wait_ge(tr_done, step_T(s - 2))
                            if s == 0:
                                act.wait_ge(ln_v, NT)
                        b_ = bank[n % 4]
                        if s < 4:
                            src = b_[:, 0:2 * QK].rearrange("p (h d) -> p h d", h=2)
                            act.activation(qc[s % 2][:, t], src, ACT.Copy)
                            act.activation(sqc[:, t], src, ACT.Square).then_inc(pj_free[n % 4], 1)
                        else:
                            src = b_[:, :].rearrange("p (h d) -> p h d", h=2)
                            c = s - 4
                            act.activation(qc[s % 2][:, t, :, 0:NOPE], src[:, :, 0:NOPE], ACT.Copy)
                            act.activation(sqc[:, t, :, 0:NOPE], src[:, :, 0:NOPE], ACT.Square)
                            act.activation(V[:, t, 2 * c:2 * c + 2, :], src[:, :, NOPE:], ACT.Copy).then_inc(pj_free[n % 4], 1)
                        if t == 1 and s + 1 < 8:
                            qkv_split(s + 1)
                if 1 <= s <= 4:
                    c = s - 1
                    for h in range(2):
                        T = T_Q + 3 * c + h
                        act.wait_ge(tr_done, T + 1)
                        act.activation(qT[:, 2 * c + h, :], bank[4 + T % 2][:, :], ACT.Copy, scale=gqk).then_inc(tr_free[T % 2], 1)
                if s < 8:
                    act.wait_ge(qk_ms, s + 1)
                    n = 16 if s < 4 else 8
                    act.activation(ssq[:, 0:n], msq[:, 0:n], ACT.Sqrt).then_inc(qk_rt, 1)
            for s in range(NA + 1):
                if s < NA:
                    i = s % NT
                    W = (i + 1) * P
                    act.wait_ge(nm_ready, s + 1)
                    if s >= 2:
                        act.wait_ge(pt_done, s - 1)
                    act.activation(probs[s % 2][:, 0:W], bank[s % 2][:, 0:W], ACT.Exp, bias=nm[:, s % 4:s % 4 + 1],
                                   accum_out=rs[:, s % 4:s % 4 + 1]).then_inc(exp_done, 1)
                if s >= 1:
                    n = s - 1
                    W = (n % NT + 1) * P
                    act.wait_ge(pt_done, n + 1)
                    if n >= 2:
                        act.wait_ge(pv_done, n - 1)
                    act.activation(probsT[n % 2][:, 0:W], bank[4 + n % 2][:, 0:W], ACT.Copy).then_inc(pt_ready, 1)
            def mT_evac(t):
                for half in range(2):
                    T = T_M + 2 * t + half
                    act.wait_ge(tr_done, T + 1)
                    act.activation(mT[0][t % 2][:, 4 * half:4 * half + 4, :],
                                   bank[4 + T % 2][:, :].rearrange("p (k q) -> p k q", k=4), ACT.Copy).then_inc(mT_hi, 1)

            def x_rms(t):
                for half in range(2):
                    n = P_WO + 2 * t + half
                    act.wait_ge(pj_free[n % 4], n // 4 + 1)
                act.activation(h2s[t], x[:, t, :], ACT.Square, accum_out=st[0][:, t:t + 1]).then_inc(rms_sq, 1)
                act.wait_ge(rms_ms, NT + t + 1)
                act.activation(st[2][:, t:t + 1], st[1][:, t:t + 1], ACT.Sqrt).then_inc(rms_rt, 1)

            def h2T_evac(t):
                act.wait_ge(tr_done, T_h2(t) + 1)
                act.dma_start(h2_dram[t * P:(t + 1) * P, :], h2s[t]).then_inc(h2_st, 16)
                act.activation(hT[:, 0:4, t * P:(t + 1) * P], bank[4][:, :].rearrange("p (k q) -> p k q", k=4),
                               ACT.Copy).then_inc(tr_free[0], 1)

            def ple_evac(n):
                t, half = divmod(n, 2)
                act.wait_ge(pj_done, P_PLE + n + 1)
                b_ = bank[(P_PLE + n) % 4]
                act.activation(ya[:, t, half * 512:(half + 1) * 512], b_[:, :], ACT.Copy)
                act.activation(arena[:, o_psq + (n % 4) * 512:o_psq + (n % 4 + 1) * 512], b_[:, :], ACT.Square, accum_out=ssl[:, n:n + 1]).then_inc(pj_free[(P_PLE + n) % 4], 1)

            mT_evac(0)
            mT_evac(1)
            for t in range(NT):
                if t + 2 < NT:
                    mT_evac(t + 2)
                x_rms(t)
                if t >= 1:
                    h2T_evac(t - 1)
            for k in range(PLE // P):
                T = T_P + k
                act.wait_ge(tr_done, T + 1)
                act.activation(pT[:, k, :], bank[4 + T % 2][:, :], ACT.Copy).then_inc(tr_free[T % 2], 1)
            for n in range(4):
                ple_evac(n)
            h2T_evac(NT - 1)
            for n in range(4, 6):
                ple_evac(n)
            act.wait_ge(rt_logit, 1)
            act.activation(rt_sc, bank[7][:, 0:NT * E].rearrange("p (t e) -> p t e", t=NT), ACT.Sigmoid).then_inc(rt_score, 1)
            for n in range(6, 2 * NT):
                ple_evac(n)
            for m in range(NT + 1):
                if m < NT:
                    act.wait_ge(sh_gu, m + 1)
                    if m >= 1:
                        act.wait_ge(sh_a, m)
                    act.activation(sg, bank[2 + m % 2][:, 0:FF], ACT.Silu).then_inc(sh_silu, 1)
                if m == 1:
                    act.wait_ge(ple_ms, 1)
                    act.activation(st[6], st[5], ACT.Sqrt).then_inc(ple_rt, 1)
                if m >= 1:
                    act.wait_ge(sh_at, m)
                    if m >= 3:
                        act.wait_ge(sh_dn, m - 2)
                    act.activation(aT[(m - 1) % 2], bank[4][:, 0:FF].rearrange("p (k q) -> p k q", k=KF),
                                   ACT.Copy).then_inc(sh_aT, 1)
            act.wait_ge(pn_st, 16 * NT)
            act.wait_ge(nb_ready, 1)
            n_pass = act.value_load(nb_i, min_val=1, max_val=NPASS_MAX)

            def step(b, q, j):
                free = q is None
                if not free or 1 <= j <= E:
                    n = j - 1
                    act.wait_ge(at_done, at(b, q, 1, n + 1))
                    if not free or n >= 2:
                        act.wait_ge(dn_done, at(b, q, 1, n - 1))
                    act.activation(aT_hi[n % 2], bank[4][:, 0:FF].rearrange("p (k q) -> p k q", k=KF),
                                   ACT.Copy).then_inc(at_hi, 1)
                if not free or 0 <= j < E:
                    act.wait_ge(gu_done, at(b, q, 1, j + 1))
                    if not free or j >= 1:
                        act.wait_ge(a_ready, at(b, q, 1, j))
                    act.activation(sg, bank[2 + j % 2][:, 0:FF], ACT.Silu).then_inc(silu_done, 1)
                if not free or 0 <= j + 1 < E:
                    act.wait_ge(xt_done, at(b, q, 1, j + 2))
                    act.activation(xgT[:, 0:4, :], bank[0][:, :].rearrange("p (k q) -> p k q", k=4),
                                   ACT.Copy).then_inc(xta, 1)
                if not free or 0 <= j < E:
                    act.wait_ge(w_dn[j % RING], at(b, q, 4, 16 * (j // RING + 1)))
                    if not free or j >= 2:
                        act.wait_ge(dn_done, at(b, q, 1, j - 1))
                    for k in range(KF):
                        act.activation(wdn_hi[j % 2][:, k, :], wdn[j % RING][:, k, :], ACT.Copy).then_inc(dn_hi, 1)
                if not free or 1 <= j <= E:
                    n = j - 1
                    act.wait_ge(dn_done, at(b, q, 1, n + 1))
                    if not free or n >= 2:
                        act.wait_ge(scat[n % 2], at(b, q, 8, 16 * (n // 2)))
                    act.activation(yo[n % 2][:, 0:512], bank[6][:, :], ACT.Copy).then_inc(yA, 1)

            with act.Fori(0, n_pass) as b:
                for j in range(-1, 5):
                    step(b, None, j)
                with act.Fori(0, Q_LOOP) as q:
                    for j in range(5, 5 + RING):
                        step(b, q, j)
                for j in range(E - 3, E + 1):
                    step(b, None, j)
                for i in range(2):
                    act.wait_ge(scat[i], at(b, None, 8, 16 * E // 2))

            for c in range(2):
                act.wait_ge(win_ready[c], win_count(W_GATE + c))
                for k in range(KD):
                    act.activation(g_hi[c][:, k, :], v2(win, win_at(c), KD, 512)[:, k, :], ACT.Copy,
                                   scale=gple[:, k:k + 1]).then_inc(g_hi_r, 1)

            def gate(t):
                act.wait_ge(f_inv, t + 1)
                for half in range(2):
                    act.wait_ge(g_done, 2 * t + half + 1)
                    if t >= 1:
                        act.wait_ge(g_x, 2 * (t - 1) + half + 1)
                    act.activation(gt[:, half * 512:(half + 1) * 512], bank[2 * (t % 2) + half][:, :],
                                   ACT.Sigmoid, scale=st[3][:, t:t + 1]).then_inc(g_sig, 1)

            for t in range(NT):
                act.wait_ge(yt_red, t + 1)
                act.activation(h3[t % 2], x[:, t, :], ACT.Square, accum_out=st[0][:, t:t + 1]).then_inc(f_sq, 1)
                for half in range(2):
                    T = T_H3 + 2 * t + half
                    act.wait_ge(tr_done, T + 1)
                    if t >= 2:
                        act.wait_ge(g_done, 2 * (t - 1))
                    act.activation(h3T[0][t % 2][:, 4 * half:4 * half + 4, :],
                                   bank[4 + T % 2][:, :].rearrange("p (k q) -> p k q", k=4), ACT.Copy).then_inc(h3_hi, 1)
                act.wait_ge(f_ms, t + 1)
                act.activation(st[2][:, t:t + 1], st[1][:, t:t + 1], ACT.Sqrt).then_inc(f_rt, 1)
                if t >= 1:
                    gate(t - 1)
            gate(NT - 1)

        @block.vector
        def _(dve):
            steps = [0]

            def link(ins):
                steps[0] += 1
                ins.then_inc(dve_step, 1)
                dve.wait_ge(dve_step, steps[0])

            def mean(dst, src, n, eps):
                return dve.tensor_scalar(dst, src, 1.0 / n, eps, ALU.mult, ALU.add)

            def rep(z, shape, axis):
                return z.unsqueeze(axis).broadcast_to(shape)

            def half_T(T):
                return bank[4 + T % 2][:, :].rearrange("p (k q) -> p k q", k=4)


            def h_evac(t):
                for half in range(2):
                    T = T_H + 2 * t + half
                    dve.wait_ge(hT_hi_ready, T + 1)
                    q = slice(t * P, (t + 1) * P)
                    for k0, k1, lo in hT_lo:
                        if k0 // 4 == half:
                            last = dve.tensor_tensor(lo[:, :, q], half_T(T)[:, k0 % 4:k0 % 4 + k1 - k0, :],
                                                     hT_hi[:, k0:k1, q].bitcast(F32), ALU.subtract)
                    last.then_inc(tr_free[T % 2], 1)

            def split(w):
                n = chunk_width(w)
                for k in range(KD):
                    dve.wait_ge(hi_ready, KD * w + k + 1)
                    dve.scalar_tensor_tensor(v2(win_r, win_at(w), KD, n)[:, k, :], v2(win, win_at(w), KD, n)[:, k, :],
                                             gmix[:, k:k + 1], whi_r[:, k, 0:n].bitcast(F32), ALU.mult, ALU.subtract).then_inc(lo_ready, 1)

            for t in range(NT):
                dve.wait_ge(rms_sq, t + 1)
                mean(st[1][:, t:t + 1], st[0][:, t:t + 1], D, EPS).then_inc(rms_ms, 1)
                dve.wait_ge(rms_rt, t + 1)
                link(dve.reciprocal(st[3][:, t:t + 1], st[2][:, t:t + 1]))
                dve.tensor_scalar(hst[t], x[:, t, :], st[3][:, t:t + 1], None, ALU.mult).then_inc(rms_x, 1)
                if t == 0:
                    dve.wait_ge(ld_pos, 16 * len(ROWS))
                    dve.tensor_copy(rows[0:NT, :], pos_i).then_inc(rows_ready, 1)
                if t == 1:
                    dve.wait_ge(cols_done, 1)
                    dve.tensor_copy(sm[:, 0:NROW], bank[7][:, 0:NROW]).then_inc(cols_ready, 1)
                    dve.wait_ge(cols_ready, 1)
                if t >= 1:
                    h_evac(t - 1)
            split(0)
            h_evac(NT - 1)
            TWO_PI = 2 * np.pi
            C1 = 6.28125
            C2 = float(np.round((TWO_PI - C1) * 2.0 ** 21) / 2.0 ** 21)
            C3 = float(np.float32(TWO_PI - C1 - C2))
            MAGIC, PI = 12582912.0, 3.1415925
            dve.wait_ge(const_pool, 2)
            link(dve.tensor_tensor(ang[0], rep(posf, [P, NT, HR], 2), rep(invf, [P, NT, HR], 1), ALU.mult))
            for dst, shift in ((ang[1], 0.0), (ang[3], 0.25)):
                link(dve.tensor_scalar(ang[2], ang[0], 1.0 / TWO_PI, shift, ALU.mult, ALU.add))
                link(dve.tensor_scalar(ang[2], ang[2], MAGIC, MAGIC, ALU.add, ALU.subtract))
                link(dve.scalar_tensor_tensor(dst, ang[2], -C1, ang[0], ALU.mult, ALU.add))
                link(dve.scalar_tensor_tensor(dst, ang[2], -C2, dst, ALU.mult, ALU.add))
                link(dve.scalar_tensor_tensor(dst, ang[2], -C3, dst, ALU.mult, ALU.add))
                link(dve.tensor_scalar(dst, dst, shift * TWO_PI, PI, ALU.add, ALU.min))
                dve.tensor_scalar(dst, dst, -PI, None, ALU.max).then_inc(ang_r, 1)
            link(dve.tensor_tensor(gqk, gqn, gkn, ALU.mult))
            link(dve.tensor_scalar(gqk, gqk, SCALE, None, ALU.mult))
            split(1)
            split(2)
            dve.wait_ge(pj_free[NT - 1], 2)
            for i, n in enumerate((QL, KVL, ROPE)):
                mean(msl[:, i * NT:(i + 1) * NT], ssl[:, i * NT:(i + 1) * NT], n, EPS).then_inc(lat_ms, 1)
            dve.wait_ge(lat_rt, 1)
            link(dve.reciprocal(msl, ssl))
            for i, (o, n) in enumerate(((0, QL), (QL, KVL), (QL + KVL, ROPE))):
                dst = lat[:, :, o:o + n]
                dve.tensor_tensor(dst, dst, rep(msl[:, i * NT:(i + 1) * NT], [P, NT, n], 2), ALU.mult).then_inc(lat_n, 1)
            split(3)
            split(4)
            for t in range(NT):
                dve.wait_ge(pj_free[t], 4)
                dve.bn_stats(bst[t % 2][:, 0:6], vbuf[:, t, 0:512])
                link(dve.bn_stats(bst[t % 2][:, 6:12], vbuf[:, t, 512:1024]))
                link(dve.bn_aggr(mv[:, t, :], bst[t % 2]))
                dve.tensor_scalar(st[3][:, t:t + 1], mv[:, t, 1:2], LN_EPS, None, ALU.add).then_inc(ln_ms, 1)
            dve.wait_ge(ln_rt, 1)
            link(dve.reciprocal(st[5], st[4]))
            for t in range(NT):
                dve.tensor_scalar(vbuf[:, t, :], vbuf[:, t, :], mv[:, t, 0:1], st[5][:, t:t + 1],
                                  ALU.subtract, ALU.mult).then_inc(ln_x, 1)
            split(5)
            split(6)
            for w in (6, 7):
                for t in range(NT):
                    if t == NT - 1:
                        split(w + 1)
                    dve.wait_ge(ga_sig, 4 * (w - 6) + t + 1)
                    dst = ya[:, t, (w % 2) * 512:(w % 2 + 1) * 512]
                    dve.tensor_tensor(dst, dst, bank[t][:, :], ALU.mult).then_inc(pj_free[t], 1)
            split(9)
            dve.wait_ge(const_pool, 3)
            for k in range(KQ + KKV):
                T = T_LAT + k
                gain = gqa[:, k:k + 1] if k < KQ else gkva[:, k - KQ:k - KQ + 1]
                dve.wait_ge(latT_hi_r, k + 1)
                dve.scalar_tensor_tensor(latT_lo[k], bank[4 + T % 2][:, :], gain, latT_hi[:, k, :].bitcast(F32),
                                         ALU.mult, ALU.subtract).then_inc(tr_free[T % 2], 1)

            def qkv_split(s):
                dve.wait_ge(qkv_hi, s + 1)
                dve.tensor_tensor(qkv_chunk(win_r, s, 0), qkv_chunk(win, s, 0), qkv_chunk(win_r, s, 1).bitcast(F32),
                                  ALU.subtract).then_inc(qkv_lo, 1)

            qkv_split(0)
            for g in range(G):
                n = P_SGU + g
                dve.wait_ge(pj_done, n + 1)
                dst = ya[:, :, g * P:(g + 1) * P]
                dve.scalar_tensor_tensor(dst, bank[n % 4][:, :].rearrange("p (t c) -> p t c", t=NT),
                                         bsp[:, g:g + 1], dst, ALU.add, ALU.mult).then_inc(pj_free[n % 4], 1)
            for s in range(9):
                if 2 <= s <= 5:
                    T = T_Q + 3 * (s - 2) + 2
                    dve.wait_ge(tr_done, T + 1)
                    dve.tensor_copy(qrT[:, s - 2, :], bank[4 + T % 2][:, :]).then_inc(tr_free[T % 2], 1)
                if s + 1 < 8:
                    qkv_split(s + 1)
                if s < 8:
                    dve.wait_ge(pj_free[3], (P_Q + 4 * s) // 4 + 1)
                    sq = sqc.rearrange("p t h d -> p (t h) d")
                    if s < 4:
                        link(dve.tensor_reduce(ssq[:, 8:16], sq[:, :, NOPE:QK], AX.X, ALU.add))
                    link(dve.tensor_reduce(ssq[:, 0:8], sq[:, :, 0:NOPE], AX.X, ALU.add))
                    if s < 4:
                        mean(msq[:, 8:16], ssq[:, 8:16], ROPE, EPS)
                    mean(msq[:, 0:8], ssq[:, 0:8], NOPE, EPS).then_inc(qk_ms, 1)
                if s >= 5:
                    for h in range(2):
                        T = T_K + 2 * (s - 5) + h
                        dve.wait_ge(tr_done, T + 1)
                        dve.tensor_copy(kT[:, 2 * (s - 5) + h, :], bank[4 + T % 2][:, :]).then_inc(tr_free[T % 2], 1)
                if s < 8:
                    dve.wait_ge(qk_rt, s + 1)
                    n = 16 if s < 4 else 8
                    link(dve.reciprocal(msq[:, 0:n], ssq[:, 0:n]))
                    z = qc[s % 2].rearrange("p t h d -> p (t h) d")
                    if s < 4:
                        dve.tensor_tensor(z[:, :, NOPE:QK], z[:, :, NOPE:QK], rep(msq[:, 8:16], [P, 8, ROPE], 2), ALU.mult)
                    dve.tensor_tensor(z[:, :, 0:NOPE], z[:, :, 0:NOPE], rep(msq[:, 0:8], [P, 8, NOPE], 2),
                                      ALU.mult).then_inc(qk_n, 1)
            for s in range(NA + 2):
                if s < NA:
                    W = (s % NT + 1) * P
                    dve.wait_ge(s_done, s + 1)
                    dve.tensor_reduce(nm[:, s % 4:s % 4 + 1], bank[s % 2][:, 0:W], AX.X, ALU.max,
                                      negate=True).then_inc(nm_ready, 1)
                if s >= 2:
                    n = s - 2
                    h, i = divmod(n, NT)
                    dve.wait_ge(pv_done, n + 1)
                    link(dve.reciprocal(rinv[:, n % 4:n % 4 + 1], rs[:, n % 4:n % 4 + 1]))
                    if n >= 2:
                        dve.wait_ge(ya_add, n - 1)
                    dve.scalar_tensor_tensor(otmp[n % 2], bank[2 + n % 2][:, 0:VD], rinv[:, n % 4:n % 4 + 1],
                                             sigb[:, i, h * VD:(h + 1) * VD], ALU.mult, ALU.mult).then_inc(o_ready, 1)
            def by_block(z):
                return z.rearrange("q (p k) -> q p k", k=KD)

            def mT_low(t):
                for half in range(2):
                    T = T_M + 2 * t + half
                    dve.wait_ge(mT_hi, 2 * t + half + 1)
                    ks = slice(4 * half, 4 * half + 4)
                    dve.tensor_tensor(mT[1][t % 2][:, ks, :], half_T(T), mT[0][t % 2][:, ks, :].bitcast(F32),
                                      ALU.subtract).then_inc(tr_free[T % 2], 1)

            def h2T_evac(t):
                dve.wait_ge(tr_done, T_h2(t) + 2)
                dve.tensor_copy(hT[:, 4:8, t * P:(t + 1) * P], half_T(1)).then_inc(tr_free[1], 1)

            mT_low(0)
            mT_low(1)
            for t in range(NT):
                for c in range(2):
                    n = P_WO + 2 * t + c
                    dve.wait_ge(pj_done, n + 1)
                    dst = x[:, t, c * 512:(c + 1) * 512]
                    dve.tensor_tensor(dst, dst, bank[n % 4][:, :], ALU.add).then_inc(pj_free[n % 4], 1)
                if t + 2 < NT:
                    mT_low(t + 2)
                if t >= 1:
                    h2T_evac(t - 1)
                dve.wait_ge(rms_sq, NT + t + 1)
                mean(st[1][:, t:t + 1], st[0][:, t:t + 1], D, EPS).then_inc(rms_ms, 1)
                dve.wait_ge(rms_rt, NT + t + 1)
                link(dve.reciprocal(st[3][:, t:t + 1], st[2][:, t:t + 1]))
                if t == 0:
                    dve.wait_ge(ld_late, 32)
                dve.scalar_tensor_tensor(h2s[t].rearrange("q (k p) -> q p k", k=KD), by_block(x[:, t, :]),
                                         st[3][:, t:t + 1], by_block(gffn), ALU.mult, ALU.mult).then_inc(h2_n, 1)
            h2T_evac(NT - 1)
            def sh_hidden(m):
                dve.wait_ge(sh_silu, m + 1)
                if m >= 2:
                    dve.wait_ge(sh_at, m - 1)
                hidden(m, None).then_inc(sh_a, 1)

            def hidden(j, w):
                dst = a_[j % 2].rearrange("q k p -> q p k")
                up = bank[2 + j % 2][:, FF:2 * FF].rearrange("q (p k) -> q p k", k=KF)
                s_ = sg.rearrange("q (p k) -> q p k", k=KF)
                if w is None:
                    return dve.tensor_tensor(dst, s_, up, ALU.mult)
                return dve.scalar_tensor_tensor(dst, s_, w, up, ALU.mult, ALU.mult)

            link(dve.memset(low, 0.0))
            for g in range(1, NG):
                last = dve.memset(low[:, g, 0:g], 1.0)
            link(last)
            dve.wait_ge(const_pool, 3)
            dve.wait_ge(rt_score, 1)
            link(dve.tensor_tensor(rt_sel, rt_sc, rep(brt[:, :], [P, NT, E], 1), ALU.add))
            for t in range(NT):
                for g in range(NG):
                    last = dve.max(g8[:, t, g, :], rt_sel[:, t, g * EG:(g + 1) * EG])
            link(last)
            link(dve.tensor_tensor(gs, g8[:, :, :, 0], g8[:, :, :, 1], ALU.add))
            other, own = rep(gs, [P, NT, NG, NG], 2), rep(gs, [P, NT, NG, NG], 3)
            dve.tensor_tensor(rt_gt, other, own, ALU.is_gt)
            link(dve.tensor_tensor(rt_eq, other, own, ALU.is_equal))
            link(dve.tensor_tensor(rt_eq, rt_eq, low.unsqueeze(1).broadcast_to([P, NT, NG, NG]), ALU.mult))
            link(dve.tensor_tensor(rt_gt, rt_gt, rt_eq, ALU.add))
            link(dve.tensor_reduce(gr, rt_gt, AX.X, ALU.add))
            link(dve.tensor_scalar(gm, gr, float(TOPG), None, ALU.is_lt))
            link(dve.tensor_scalar(gm, gm, BIG, -BIG, ALU.mult, ALU.add))
            sel4 = rt_sel.rearrange("p t (g e) -> p t g e", g=NG)
            link(dve.tensor_tensor(sel4, sel4, rep(gm, [P, NT, NG, EG], 3), ALU.add))
            for t in range(NT):
                last = dve.max(t8[:, t, :], rt_sel[:, t, :])
            link(last)
            sh_hidden(0)
            for t in range(NT):
                last = dve.match_replace(out=rt_rep[:, t, :], in_to_replace=t8[:, t, :],
                                         in_values=rt_sel[:, t, :], imm_value=-3e38)
            link(last)
            dve.tensor_tensor(rt_M, rt_rep, rt_sel, ALU.not_equal).then_inc(m_ready, 1)
            dve.wait_ge(m_ready, 1)
            link(dve.tensor_tensor(rt_sc, rt_sc, rt_M, ALU.mult))
            link(dve.tensor_reduce(rden, rt_sc, AX.X, ALU.add))
            link(dve.reciprocal(rden, rden))
            link(dve.tensor_scalar(rden, rden, ROUTED, None, ALU.mult))
            link(dve.tensor_tensor(rt_sc, rt_sc, rep(rden, [P, NT, E], 2), ALU.mult))
            for i in range(3):
                part = Rv[:, :, :, 6 + i].rearrange("p e t -> p t e")
                link(dve.tensor_copy(part, rt_sc))
                if i < 2:
                    link(dve.tensor_tensor(rt_sc, rt_sc, part, ALU.subtract))
            sh_hidden(1)
            dve.wait_ge(pj_free[3], P_PLE // 4 + 2)
            link(dve.tensor_reduce(st[4], v2(sm, 76, NT, 2), AX.X, ALU.add))
            mean(st[5], st[4], D, EPS).then_inc(ple_ms, 1)
            dve.wait_ge(ple_rt, 1)
            link(dve.reciprocal(st[7], st[6]))
            for t in range(NT):
                dve.scalar_tensor_tensor(ya[:, t, :], ya[:, t, :], st[7][:, t:t + 1], gpo,
                                         ALU.mult, ALU.mult).then_inc(ple_n, 1)
            tile_ = addt.unsqueeze(1).broadcast_to([P, E, NT])
            within = pcol.unsqueeze(2).broadcast_to([P, E, NT])
            dve.tensor_copy(Rv[:, :, :, 0], within)
            dve.tensor_copy(Rv[:, :, :, 1], tile_)
            dve.memset(Rv[:, :, :, 2], 0.0)
            dve.tensor_scalar(Rv[:, :, :, 3], within, float(TOPK), None, ALU.mult)
            dve.tensor_scalar(Rv[:, :, :, 4], tile_, float(TOPK), None, ALU.mult)

            def sh_out(m):
                dve.wait_ge(sh_dn, m + 1)
                for half in range(2):
                    dst = x[:, m, half * 512:(half + 1) * 512]
                    last = dve.tensor_tensor(dst, dst, bank[6 + half][:, :], ALU.add)
                last.then_inc(sh_y, 1)

            for i in range(2):
                T = T_MT + i
                dve.wait_ge(tr_done, T + 1)
                dve.tensor_copy(MT[:, i * 256:(i + 1) * 256], bank[4 + T % 2][0:E, 0:256]).then_inc(tr_free[T % 2], 1)
            sh_hidden(2)
            dve.wait_ge(rk_done, 1)
            Mv = rt_M.rearrange("p t e -> p e t")
            pr = bank[0][:, 0:NT * E].rearrange("p (t e) -> p e t", t=NT)
            link(dve.scalar_tensor_tensor(rank, pr, 1.0, Mv, ALU.add, ALU.mult))
            dve.tensor_scalar(rank_[:, :], rank_[:, :], -1.0, None, ALU.add).then_inc(rank_ready, 1)
            link(dve.tensor_reduce(cmp_[:, 0:1], bank[0][:, NT * E:NT * E + E], AX.X, ALU.max))
            for i in range(1, NPASS_MAX):
                last = dve.tensor_scalar(cmp_[:, i:i + 1], cmp_[:, 0:1], float(NS * i), None, ALU.is_gt)
            link(last)
            link(dve.tensor_reduce(cmp_[:, 0:1], cmp_[:, 1:NPASS_MAX], AX.X, ALU.add))
            dve.tensor_scalar(nb_i, cmp_[0:1, 0:1], 1.0, None, ALU.add).then_inc(nb_ready, 1)
            sh_out(0)
            dve.wait_ge(ks_done, 1)
            dve.tensor_copy(Rv[:, :, :, 5], bank[1][:, 0:NT * E].rearrange("p (t e) -> p e t", t=NT)).then_inc(R_ready, 1)

            def one_hot(j, ranks, slot_numbers):
                dve.tensor_tensor(S_[j % 2], rep(ranks, [P, NT, P], 2),
                                  iota[:, slot_numbers].unsqueeze(1).broadcast_to([P, NT, P]),
                                  ALU.is_equal).then_inc(sel_ready, 1)

            def tokens_of(n, count):
                dve.tensor_reduce(slots[n % 4], bank[5][:, 0:9].rearrange("p (c i) -> p c i", c=3),
                                  AX.X, ALU.add).then_inc(tab_sum, 1)
                dve.wait_ge(tab_sum, count)
                dve.tensor_tensor(gidx[n % 4][:, :], slots[n % 4][:, 0:1], addc[:, 0:1], ALU.add).then_inc(idx_ready, 1)

            def first_selects(b):
                for j in range(2):
                    one_hot(j, rank[:, j, :], slice(0, P) if b is None else bass.ds(b * NS + NS, P))

            def first_tokens(b):
                for j in range(2):
                    dve.wait_ge(tab_done, ahead(b, j + 1))
                    tokens_of(j, ahead(b, j + 1))

            dve.wait_ge(rank_ready, 1)
            first_selects(None)
            sh_hidden(3)
            first_tokens(None)
            for m in range(1, NT):
                sh_out(m)
            dve.wait_ge(nb_ready, 1)
            n_pass = dve.value_load(nb_i, min_val=1, max_val=NPASS_MAX)

            def select(b, q, j):
                if q is not None or j >= 2:
                    dve.wait_ge(tab_done, at(b, q, 1, j - 1))
                e = j if q is None else q * RING + j
                r_ = rank[:, e, :] if q is None else rank[:, bass.ds(e, 1), :].rearrange("p o t -> p (o t)")
                one_hot(j, r_, bass.ds(b * NS, P))

            def step(b, q, j):
                free = q is None
                if not free or j + 3 < E:
                    select(b, q, j + 3)
                if not free or 1 <= j <= E:
                    n = j - 1
                    dve.wait_ge(at_hi, at(b, q, 1, n + 1))
                    dve.tensor_tensor(aT_lo[n % 2], bank[4][:, 0:FF].rearrange("p (k q) -> p k q", k=KF),
                                      aT_hi[n % 2].bitcast(F32), ALU.subtract).then_inc(at_ready, 1)
                if not free or 0 <= j < E:
                    dve.wait_ge(silu_done, at(b, q, 1, j + 1))
                    if not free or j >= 2:
                        dve.wait_ge(at_done, at(b, q, 1, j - 1))
                    dve.wait_ge(idx_ready, at(b, q, 1, j + 1))
                    hidden(j, wt[j % 4]).then_inc(a_ready, 1)
                if not free or 0 <= j + 1 < E:
                    dve.wait_ge(xt_done, at(b, q, 1, j + 2))
                    dve.tensor_copy(xgT[:, 4:8, :], bank[1][:, :].rearrange("p (k q) -> p k q", k=4)).then_inc(xtb, 1)
                if not free or 0 <= j < E:
                    for k in range(KF):
                        dve.wait_ge(dn_hi, at(b, q, KF, KF * j + k + 1))
                        dve.tensor_tensor(wdn_lo[j % RING][:, k, :], wdn[j % RING][:, k, :],
                                          wdn_hi[j % 2][:, k, :].bitcast(F32), ALU.subtract).then_inc(dn_lo, 1)
                if not free or 1 <= j <= E:
                    n = j - 1
                    dve.wait_ge(dn_done, at(b, q, 1, n + 1))
                    if not free or n >= 2:
                        dve.wait_ge(scat[n % 2], at(b, q, 8, 16 * (n // 2)))
                    dve.tensor_tensor(sidx[n % 2][:, :], slots[n % 4][:, 1:2], addc[:, 1:2], ALU.add)
                    dve.tensor_copy(yo[n % 2][:, 512:1024], bank[7][:, :]).then_inc(yB, 1)
                if not free or j + 3 < E:
                    n = j + 3
                    dve.wait_ge(tab_done, at(b, q, 1, n + 1))
                    if not free or n >= 4:
                        dve.wait_ge(yB, at(b, q, 1, n - 3))
                    tokens_of(n, at(b, q, 1, n + 1))

            with dve.Fori(0, n_pass) as b:
                for j in range(-1, 5):
                    step(b, None, j)
                with dve.Fori(0, Q_LOOP) as q:
                    for j in range(5, 5 + RING):
                        step(b, q, j)
                for j in range(E - 3, E + 1):
                    step(b, None, j)
                for i in range(2):
                    dve.wait_ge(scat[i], at(b, None, 8, 16 * E // 2))
                first_selects(b)
                first_tokens(b)

            def gated(t):
                dve.wait_ge(pn_ld[t], 16)
                for half in range(2):
                    dve.wait_ge(g_sig, 2 * t + half + 1)
                    sl = slice(half * 512, (half + 1) * 512)
                    link(dve.tensor_tensor(gt[:, sl], gt[:, sl], ya[:, t, sl], ALU.mult))
                    dve.tensor_tensor(x[:, t, sl], x[:, t, sl], gt[:, sl], ALU.add).then_inc(g_x, 1)

            def gate_low(c, ks):
                for k in ks:
                    dve.wait_ge(g_hi_r, KD * c + k + 1)
                    dve.scalar_tensor_tensor(v2(win_r, win_at(c), KD, 512)[:, k, :], v2(win, win_at(c), KD, 512)[:, k, :],
                                             gple[:, k:k + 1], g_hi[c][:, k, :].bitcast(F32), ALU.mult, ALU.subtract).then_inc(g_lo_r, 1)

            gate_low(0, range(KD))
            def add_row(t, n):
                return dve.tensor_tensor(x[:, t, :], x[:, t, :], yt[t][:, n * D:(n + 1) * D], ALU.add)

            def h3_low(t):
                for half in range(2):
                    T = T_H3 + 2 * t + half
                    dve.wait_ge(h3_hi, 2 * t + half + 1)
                    ks = slice(4 * half, 4 * half + 4)
                    dve.tensor_tensor(h3T[1][t % 2][:, ks, :], half_T(T), h3T[0][t % 2][:, ks, :].bitcast(F32),
                                      ALU.subtract).then_inc(tr_free[T % 2], 1)

            for t in range(NT):
                dve.wait_ge(yt_ld[2 * t], 16)
                link(add_row(t, 0))
                if t == 0:
                    gate_low(1, range(4))
                dve.wait_ge(yt_add, 2 * t + 1)
                link(add_row(t, 2))
                dve.wait_ge(yt_ld[2 * t + 1], 16)
                link(add_row(t, 4))
                link(add_row(t, 5))
                dve.wait_ge(yt_add, 2 * t + 2)
                add_row(t, 6).then_inc(yt_red, 1)
                dve.wait_ge(f_sq, t + 1)
                mean(st[1][:, t:t + 1], st[0][:, t:t + 1], D, EPS).then_inc(f_ms, 1)
                h3_low(t)
                if t == 0:
                    gate_low(1, range(4, KD))
                dve.wait_ge(f_rt, t + 1)
                dve.reciprocal(st[3][:, t:t + 1], st[2][:, t:t + 1]).then_inc(f_inv, 1)
                if t >= 1:
                    gated(t - 1)
            gated(NT - 1)

        @block.tensor
        def _(pe):
            def transposes(T, srcs, rows=P):
                if T >= 2:
                    pe.wait_ge(tr_free[T % 2], T // 2)
                for i, src in enumerate(srcs):
                    last = pe.transpose(bank[4 + T % 2][0:rows, i * P:(i + 1) * P], src, ident[:, :])
                last.then_inc(tr_done, 1)

            def project(n, pairs, width):
                if n >= 4:
                    pe.wait_ge(pj_free[n % 4], n // 4)
                for i, (l, r) in enumerate(pairs):
                    last = pe.matmul(bank[n % 4][:, 0:width], l, r, start=(i == 0), stop=(i == len(pairs) - 1))
                return last

            def blocks(z, half):
                return [z[:, k * P:(k + 1) * P] for k in range(4 * half, 4 * half + 4)]

            def tok(t):
                return slice(t * P, (t + 1) * P)

            pe.wait_ge(const_pool, 1)
            for t in range(NT):
                pe.wait_ge(rms_x, t + 1)
                for half in range(2):
                    transposes(T_H + 2 * t + half, blocks(hst[t], half))
                if t == 0:
                    pe.wait_ge(rows_ready, 1)
                    pe.transpose(bank[7][:, 0:NROW], rows[0:NROW, :], ident[0:NROW, 0:NROW]).then_inc(cols_done, 1)

            def z_chunk(slot, width, free, before):
                lo = v2(win_r, win_at(slot), KD, width)
                for t in range(NT):
                    if free is None:
                        for i in range(2):
                            pe.wait_ge(tr_free[i], t + 1)
                    else:
                        pe.wait_ge(pj_free[t], free)
                    for k in range(KD):
                        if t == 0:
                            pe.wait_ge(lo_ready, before + k + 1)
                        x_hi = hT_hi[:, k, tok(t)]
                        x_lo = [lo_[:, k - k0, tok(t)] for k0, k1, lo_ in hT_lo if k0 <= k < k1][0]
                        w_hi, w_lo = whi_r[:, k, 0:width], lo[:, k, :]
                        b_ = bank[t][:, 0:width]
                        pe.matmul(b_, x_hi, w_hi, start=(k == 0), stop=False)
                        last = pe.matmul(b_, x_lo, w_hi, start=False, stop=False)
                        if t == NT - 1:
                            last.then_inc(whi_used, 1)
                        last = pe.matmul(b_, x_hi, w_lo, start=False, stop=(k == KD - 1))
                    last.then_inc(pj_done, 1)

            z_chunk(0, QL, None, 0)
            z_chunk(1, KVL + ROPE, 1, KD)
            with pe.Fori(1, W_Q // 2) as i:
                for slot in range(2):
                    z_chunk(slot, 512, i * 2 + slot, i * (2 * KD) + slot * KD)
            pe.wait_ge(wsp_m, 1)
            for i in range(2):
                transposes(T_WSP + i, [wsp[:, g, :] for g in range(4 * i, 4 * i + 4)])
            pe.wait_ge(lat_n, 3)
            for k in range(KQ + KKV):
                transposes(T_LAT + k, [lat[:, t, k * P:(k + 1) * P] for t in range(NT)])
            pe.wait_ge(kp_rot, 1)
            transposes(T_KPE, [kprot[:, t].rearrange("p h d -> p (h d)") for t in range(NT)])
            pe.wait_ge(ln_v, NT)
            for i in range(2):
                pe.wait_ge(tr_free[i], T_LAT // 2)
            for g in range(G):
                n = P_SGU + g
                project(n, [(wspT[:, g, :], vbuf[:, :, g * P:(g + 1) * P])], 512).then_inc(pj_done, 1)
            for i in range(2):
                pe.wait_ge(tr_free[i], T_Q // 2)
            for s in range(9):
                if s < 8:
                    pe.wait_ge(qkv_lo, s + 1)
                    nk, k0, width = (KQ, 0, 2 * QK) if s < 4 else (KKV, KQ, 512)
                    w_lo, w_hi = (qkv_chunk(win_r, s, part).rearrange("p (k n) -> p k n", k=nk) for part in range(2))
                    for t in range(NT):
                        pairs = []
                        for k in range(nk):
                            hi, lo = latT_hi[:, k0 + k, tok(t)], latT_lo[k0 + k][:, tok(t)]
                            pairs += [(hi, w_hi[:, k, :]), (lo, w_hi[:, k, :]), (hi, w_lo[:, k, :])]
                        project(P_Q + 4 * s + t, pairs, width).then_inc(pj_done, 1)
                        if t == 1 and 2 <= s <= 5:
                            pe.wait_ge(q_rot, s - 1)
                            transposes(T_Q + 3 * (s - 2) + 2,
                                       [qrot[s % 2][:, t_].rearrange("p h d -> p (h d)") for t_ in range(NT)])
                if s >= 1:
                    c = s - 1
                    z = qc[c % 2]
                    pe.wait_ge(qk_n, c + 1)
                    for h in range(2):
                        transposes((T_Q + 3 * c if c < 4 else T_K + 2 * (c - 4)) + h,
                                   [z[:, t, h, 0:NOPE] for t in range(NT)])
            for i in range(4):
                pe.wait_ge(pj_free[i], P_WO // 4)
            for i in range(2):
                pe.wait_ge(tr_free[i], T_M // 2)
            for s in range(NA + 2):
                if s < NA:
                    h, i = divmod(s, NT)
                    W, r0 = (i + 1) * P, ROPE * (h % 2)
                    if s >= 2:
                        pe.wait_ge(exp_done, s - 1)
                    b_ = bank[s % 2]
                    pe.matmul(b_[:, 0:W], qT[:, h, tok(i)], kT[:, h, 0:W], start=True, stop=False)
                    pe.matmul(b_[:, i * P:W], identb[:, :], negmask[:, :], start=False, stop=False)
                    pe.matmul(b_[:, 0:W], qrT[r0:r0 + ROPE, h // 2, tok(i)], kpeT[r0:r0 + ROPE, 0:W],
                              start=False, stop=True).then_inc(s_done, 1)
                if 1 <= s <= NA:
                    n = s - 1
                    pe.wait_ge(exp_done, n + 1)
                    if n >= 2:
                        pe.wait_ge(pt_ready, n - 1)
                    for k in range(n % NT + 1):
                        last = pe.transpose(bank[4 + n % 2][:, tok(k)], probs[n % 2][:, tok(k)], ident[:, :])
                    last.then_inc(pt_done, 1)
                if s >= 2:
                    n = s - 2
                    h, i = divmod(n, NT)
                    pe.wait_ge(pt_ready, n + 1)
                    if n >= 2:
                        pe.wait_ge(o_ready, n - 1)
                    for k in range(i + 1):
                        last = pe.matmul(bank[2 + n % 2][:, 0:VD], probsT[n % 2][:, tok(k)], V[:, k, h, :],
                                         start=(k == 0), stop=(k == i))
                    last.then_inc(pv_done, 1)
            pe.wait_ge(pt_ready, NA)
            def merged_T(t):
                pe.wait_ge(ya_add, NA - NT + t + 1)
                for half in range(2):
                    transposes(T_M + 2 * t + half, blocks(ya[:, t, :], half))

            def h2_T(t):
                pe.wait_ge(h2_n, t + 1)
                for half in range(2):
                    transposes(T_h2(t) + half, blocks(h2s[t], half))

            def logits(t):
                for i in range(2):
                    pe.wait_ge(tr_free[i], T_h2(t) // 2 + 1)
                for k in range(KD):
                    last = pe.matmul(bank[7][:, t * E:(t + 1) * E], hT[:, k, tok(t)], wr[:, k * E:(k + 1) * E],
                                     start=(k == 0), stop=(k == KD - 1))
                return last

            merged_T(0)
            merged_T(1)
            wo_lo = [v2(win_r, win_at(c), KD, 512) for c in range(2)]
            pe.wait_ge(o_ready, NA)
            for t in range(NT):
                for i in range(2):
                    pe.wait_ge(tr_free[i], T_M // 2 + t + 1)
                for c in range(2):
                    if t == 0:
                        pe.wait_ge(wo_lo_r, KD * (c + 1))
                    pairs = []
                    for k in range(KD):
                        hi, lo = mT[0][t % 2][:, k, :], mT[1][t % 2][:, k, :]
                        pairs += [(hi, wo_hi[c][k]), (lo, wo_hi[c][k]), (hi, wo_lo[c][:, k, :])]
                    project(P_WO + 2 * t + c, pairs, 512).then_inc(pj_done, 1)
                if t + 2 < NT:
                    merged_T(t + 2)
                if t >= 1:
                    h2_T(t - 1)
            logits(0)
            logits(1)
            pe.wait_ge(ld_p, 16)
            for k in range(PLE // P):
                transposes(T_P + k, [pbuf[:, t, k * P:(k + 1) * P] for t in range(NT)])
            logits(2)
            for i in range(2):
                pe.wait_ge(tr_free[i], T_P // 2 + 1)
            pe.wait_ge(ld_pj, 16)
            for n in range(2 * NT):
                if n == 4:
                    h2_T(NT - 1)
                if n == 6:
                    logits(NT - 1).then_inc(rt_logit, 1)
                t, half = divmod(n, 2)
                project(P_PLE + n, [(pT[:, k, tok(t)], wpj[:, k, half * 512:(half + 1) * 512])
                                    for k in range(PLE // P)], 512).then_inc(pj_done, 1)
            for i in range(4):
                pe.wait_ge(pj_free[i], P_PLE // 4 + 2)
            pe.wait_ge(win_ready[1], win_count(W_SHGU))
            shgu = win[:, win_at(1):win_at(1) + WGU].rearrange("p (g k f) -> p k g f", g=2, k=KD)
            shdn = v2(win, win_at(0), KF, D)

            def gate_up(bk, xT, w):
                for k in range(KD):
                    last = pe.matmul(bk[:, :], xT[:, k, :], w[:, k], start=(k == 0), stop=(k == KD - 1))
                return last

            def hidden_T(a_buf):
                for k in range(KF):
                    last = pe.transpose(bank[4][:, k * P:(k + 1) * P], a_buf[:, k, :], ident[:, :])
                return last

            def down(aT_buf, w):
                for half in range(2):
                    for k in range(KF):
                        last = pe.matmul(bank[6 + half][:, :], aT_buf[:, k, :], w[:, k, half * 512:(half + 1) * 512],
                                         start=(k == 0), stop=(k == KF - 1))
                return last

            def tab(b, j):
                if b is None and j == 0:
                    pe.wait_ge(R_ready, 1)
                else:
                    pe.wait_ge(idx_ready, ahead(b, j))
                pe.wait_ge(sel_ready, ahead(b, j + 1))
                for t in range(NT):
                    last = pe.matmul(bank[5][:, 0:9], S_[j % 2][:, t, :], Rv[:, j, t, :], start=(t == 0), stop=(t == NT - 1))
                last.then_inc(tab_done, 1)

            for m in range(NT + 2):
                if m == 3:
                    for i in range(2):
                        pe.wait_ge(tr_free[i], T_H3 // 2)
                    for t in range(NT):
                        last = pe.matmul(bank[1][:, t * E:(t + 1) * E], MT[:, tok(t)], tri[0:E, 0:E],
                                         start=True, stop=True)
                    last.then_inc(ks_done, 1)
                if m < NT:
                    if m >= 2:
                        pe.wait_ge(sh_a, m - 1)
                    gate_up(bank[2 + m % 2], hT[:, :, tok(m)], shgu).then_inc(sh_gu, 1)
                if m == 2:
                    pe.wait_ge(m_ready, 1)
                    pe.wait_ge(sh_aT, 1)
                    for i in range(2):
                        T = T_MT + i
                        for t in range(2):
                            last = pe.transpose(bank[4 + i][0:E, tok(t)], rt_M[:, 2 * i + t, :], ident[:, :])
                        last.then_inc(tr_done, 1)
                    for t in range(NT):
                        for u in range(t + 1):
                            pe.matmul(bank[0][:, t * E:(t + 1) * E], (ones if u < t else tri)[:, :], rt_M[:, u, :],
                                      start=(u == 0), stop=(u == t))
                    for t in range(NT):
                        last = pe.matmul(bank[0][:, NT * E:NT * E + E], ones[:, :], rt_M[:, t, :],
                                         start=(t == 0), stop=(t == NT - 1))
                    last.then_inc(rk_done, 1)
                if m == 3:
                    tab(None, 0)
                if 1 <= m <= NT:
                    n = m - 1
                    pe.wait_ge(sh_a, n + 1)
                    if n >= 1:
                        pe.wait_ge(sh_aT, n)
                        for i in range(2):
                            pe.wait_ge(tr_free[i], T_H3 // 2)
                    hidden_T(a_[n % 2]).then_inc(sh_at, 1)
                if m >= 2:
                    n = m - 2
                    pe.wait_ge(sh_aT, n + 1)
                    if n == 0:
                        pe.wait_ge(win_ready[0], win_count(W_SHDN))
                        pe.wait_ge(rt_score, 1)
                    else:
                        pe.wait_ge(sh_y, n)
                    down(aT[n % 2], shdn).then_inc(sh_dn, 1)
                    if n == 1:
                        tab(None, 1)
            pe.wait_ge(sh_y, NT)
            n_pass = pe.value_load(nb_i, min_val=1, max_val=NPASS_MAX)

            def step(b, q, j):
                free = q is None
                if not free or 1 <= j <= E:
                    n = j - 1
                    pe.wait_ge(a_ready, at(b, q, 1, n + 1))
                    if not free or n >= 1:
                        pe.wait_ge(at_ready, at(b, q, 1, n))
                    hidden_T(a_[n % 2]).then_inc(at_done, 1)
                if not free or 0 <= j < E:
                    pe.wait_ge(w_gu[j % RING], at(b, q, 8, 32 * (j // RING + 1)))
                    pe.wait_ge(xta, at(b, q, 1, j + 1))
                    pe.wait_ge(xtb, at(b, q, 1, j + 1))
                    if not free or j >= 2:
                        pe.wait_ge(a_ready, at(b, q, 1, j - 1))
                    gate_up(bank[2 + j % 2], xgT, wgu[j % RING]).then_inc(gu_done, 1)
                if not free or j + 3 < E:
                    n = j + 3
                    pe.wait_ge(sel_ready, at(b, q, 1, n + 1))
                    if not free or n >= 1:
                        pe.wait_ge(idx_ready, at(b, q, 1, n))
                    for t in range(NT):
                        r_ = Rv[:, n, t, :] if free else Rv[:, bass.ds(q * RING + n, 1), t, :].rearrange("p o c -> p (o c)")
                        last = pe.matmul(bank[5][:, 0:9], S_[n % 2][:, t, :], r_, start=(t == 0), stop=(t == NT - 1))
                    last.then_inc(tab_done, 1)
                if not free or 0 <= j + 1 < E:
                    n = j + 1
                    pe.wait_ge(gath[n % 2], at(b, q, 8, 16 * (n // 2 + 1)))
                    if not free or n >= 1:
                        pe.wait_ge(xta, at(b, q, 1, n))
                        pe.wait_ge(xtb, at(b, q, 1, n))
                    for k in range(KD):
                        last = pe.transpose(bank[k // 4][:, (k % 4) * P:(k % 4 + 1) * P], xg[n % 2][:, k * P:(k + 1) * P],
                                            ident[:, :])
                    last.then_inc(xt_done, 1)
                if not free or 1 <= j <= E:
                    n = j - 1
                    pe.wait_ge(at_ready, at(b, q, 1, n + 1))
                    pe.wait_ge(dn_lo, at(b, q, KF, KF * (n + 1)))
                    if not free or n >= 1:
                        pe.wait_ge(yA, at(b, q, 1, n))
                        pe.wait_ge(yB, at(b, q, 1, n))
                    for half in range(2):
                        cols = slice(half * 512, (half + 1) * 512)
                        for k in range(KF):
                            hi, lo = aT_hi[n % 2][:, k, :], aT_lo[n % 2][:, k, :]
                            w_hi = wdn_hi[n % 2][:, k, cols]
                            b_ = bank[6 + half][:, :]
                            pe.matmul(b_, hi, w_hi, start=(k == 0), stop=False)
                            pe.matmul(b_, lo, w_hi, start=False, stop=False)
                            last = pe.matmul(b_, hi, wdn_lo[n % RING][:, k, cols], start=False, stop=(k == KF - 1))
                    last.then_inc(dn_done, 1)

            with pe.Fori(0, n_pass) as b:
                for j in range(-1, 5):
                    step(b, None, j)
                with pe.Fori(0, Q_LOOP) as q:
                    for j in range(5, 5 + RING):
                        step(b, q, j)
                for j in range(E - 3, E + 1):
                    step(b, None, j)
                for i in range(2):
                    pe.wait_ge(scat[i], at(b, None, 8, 16 * E // 2))
                for j in range(2):
                    tab(b, j)

            def h3_T(t):
                pe.wait_ge(yt_red, t + 1)
                for half in range(2):
                    transposes(T_H3 + 2 * t + half, blocks(x[:, t, :], half))

            h3_T(0)
            for t in range(NT):
                for i in range(2):
                    pe.wait_ge(tr_free[i], T_H3 // 2 + t + 1)
                for half in range(2):
                    w = W_GATE + half
                    if t >= 2:
                        pe.wait_ge(g_sig, 2 * (t - 2) + half + 1)
                    w_lo = v2(win_r, win_at(w), KD, 512)
                    for k in range(KD):
                        if t == 0:
                            pe.wait_ge(g_lo_r, KD * half + k + 1)
                        hi, lo = h3T[0][t % 2][:, k, :], h3T[1][t % 2][:, k, :]
                        b_ = bank[2 * (t % 2) + half][:, :]
                        pe.matmul(b_, hi, g_hi[half][:, k, :], start=(k == 0), stop=False)
                        pe.matmul(b_, lo, g_hi[half][:, k, :], start=False, stop=False)
                        last = pe.matmul(b_, hi, w_lo[:, k, :], start=False, stop=(k == KD - 1))
                    last.then_inc(g_done, 1)
                    if t + 1 < NT and half == (t + 1 == NT - 1):
                        h3_T(t + 1)


_INS = ["x", "p", "positions", "g_mix", "w_in", "sgu_ln_g", "sgu_ln_b", "sgu_w", "sgu_b", "mla_g_qa", "mla_w_qb",
        "mla_g_kva", "mla_w_kvb", "qk_g_q_nope", "qk_g_k_nope", "qk_g_q_rope", "qk_g_k_rope", "w_o", "g_ffn",
        "w_router", "b_router", "w_exp_gate", "w_exp_up", "w_exp_down", "w_sh_gate", "w_sh_up", "w_sh_down",
        "g_ple_in", "w_ple_gate", "w_ple_proj", "g_ple_out"]


def kernel(**inputs):
    import concourse.bacc as bacc
    from concourse.bass_utils import run_bass_kernel_spmd

    nc = bacc.Bacc("TRN2", target_bir_lowering=False, num_devices=1)
    arrays, aps = {}, {}
    for name in _INS:
        v = np.ascontiguousarray(inputs[name])
        arrays["in_" + name] = v
        aps[name] = nc.dram_tensor("in_" + name, v.shape, mybir.dt.from_np(v.dtype), kind="ExternalInput").ap()
    out = nc.dram_tensor("out_0", arrays["in_x"].shape, mybir.dt.float32, kind="ExternalOutput").ap()
    hybrid_block_kernel(nc, aps, out)
    r = run_bass_kernel_spmd(nc, [arrays], core_ids=[0])
    return r.results[0]["out_0"]
```
